# Optimizing a Trainium2 kernel written in Bass

```python
import jax, jax.numpy as jnp
from jax import lax
import numpy as np

D_MODEL = 1024
BATCH = 1
SEQ = 256
DEPTH = 2

N_A = DEPTH // 2
N_B = DEPTH - N_A
N_DENSE = (DEPTH + 1) // 2
N_MOE = DEPTH // 2

GLA_HEADS = 4
GLA_DK = D_MODEL // 2 // GLA_HEADS
GLA_DV = D_MODEL // GLA_HEADS
GLA_QK = GLA_HEADS * GLA_DK
GLA_V = GLA_HEADS * GLA_DV
GLA_GATE_RANK = 16
GLA_GATE_NORM = 16.0
GLA_CHUNK = 64
GLA_IN = 2 * GLA_QK + GLA_V + GLA_GATE_RANK + GLA_V

SB_HEADS = 8
SB_HEAD_DIM = D_MODEL // SB_HEADS
SB_BLOCK = 128

FFN_DIM = 2816
N_EXPERTS = 8
TOP_K = 2
EXPERT_DIM = 3584

RMS_EPS = 1e-6


def rms_norm(x, g):
    xf = x.astype(jnp.float32)
    y = xf * lax.rsqrt(jnp.mean(xf * xf, axis=-1, keepdims=True) + RMS_EPS)
    return (y * g.astype(jnp.float32)).astype(x.dtype)

def swiglu(h, w_gate, w_up, w_down):
    return (jax.nn.silu(h @ w_gate) * (h @ w_up)) @ w_down

def gla_mixer(h, w_in, w_gate_up, b_gate, g_head, w_out):
    B, S, _ = h.shape
    H, dk, dv, C = GLA_HEADS, GLA_DK, GLA_DV, GLA_CHUNK
    nc = S // C
    proj = h @ w_in
    q, k, v, g_lr, r = jnp.split(
        proj, [GLA_QK, 2 * GLA_QK, 2 * GLA_QK + GLA_V, 2 * GLA_QK + GLA_V + GLA_GATE_RANK], axis=-1)
    log_a = jax.nn.log_sigmoid((g_lr @ w_gate_up + b_gate).astype(jnp.float32)) / GLA_GATE_NORM

    def to_chunks(t, d):
        return t.reshape(B, nc, C, H, d).transpose(1, 0, 3, 2, 4).astype(jnp.float32)

    qc = to_chunks(q, dk) * (dk ** -0.5)
    kc = to_chunks(k, dk)
    vc = to_chunks(v, dv)
    gc = to_chunks(log_a, dk)
    b = jnp.cumsum(gc, axis=3)
    b_end = b[:, :, :, -1:, :]
    q_dec = qc * jnp.exp(b)
    k_inv = kc * jnp.exp(-b)
    k_end = kc * jnp.exp(b_end - b)
    decay_end = jnp.exp(b_end[:, :, :, 0, :])

    tri = jnp.tril(jnp.ones((C, C), dtype=bool))
    attn = jnp.where(tri, jnp.einsum('nbhid,nbhjd->nbhij', q_dec, k_inv), 0.0)
    o_intra = jnp.einsum('nbhij,nbhjv->nbhiv', attn, vc)

    def step(state, inp):
        q_n, k_n, v_n, dec_n = inp
        o_n = jnp.einsum('bhid,bhdv->bhiv', q_n, state)
        state = dec_n[..., None] * state + jnp.einsum('bhid,bhiv->bhdv', k_n, v_n)
        return state, o_n

    state0 = jnp.zeros((B, H, dk, dv), dtype=jnp.float32)
    _, o_inter = lax.scan(step, state0, (q_dec, k_end, vc, decay_end))
    o = (o_inter + o_intra).transpose(1, 0, 3, 2, 4).reshape(B, S, H, dv)
    o = rms_norm(o, g_head).reshape(B, S, GLA_V)
    o = (o * jax.nn.silu(r.astype(jnp.float32))).astype(h.dtype)
    return o @ w_out

def stick_breaking_mixer(h, k, v, w_q, w_out):
    B, S, _ = h.shape
    H, hd = SB_HEADS, SB_HEAD_DIM
    q = (h @ w_q).reshape(B, S, H, hd).transpose(0, 2, 1, 3)
    scale = hd ** -0.5
    outs = []
    for blk in range(S // SB_BLOCK):
        t0 = blk * SB_BLOCK
        t1 = t0 + SB_BLOCK
        qb = q[:, :, t0:t1]
        kb = k[:, :, :t1]
        vb = v[:, :, :t1]
        z = jnp.einsum('bhtd,bhsd->bhts', qb, kb).astype(jnp.float32) * scale
        t_idx = t0 + jnp.arange(SB_BLOCK)[:, None]
        s_idx = jnp.arange(t1)[None, :]
        causal = s_idx < t_idx
        log_beta = jax.nn.log_sigmoid(z)
        log_keep = jnp.where(causal, jax.nn.log_sigmoid(-z), 0.0)
        log_stay = lax.cumsum(log_keep, axis=3, reverse=True) - log_keep
        w = jnp.where(causal, jnp.exp(log_beta + log_stay), 0.0)
        outs.append(jnp.einsum('bhts,bhsd->bhtd', w.astype(vb.dtype), vb))
    o = jnp.concatenate(outs, axis=2).transpose(0, 2, 1, 3).reshape(B, S, H * hd)
    return o @ w_out

def moe_swiglu(h, w_router, w_gate, w_up, w_down):
    logits = (h @ w_router).astype(jnp.float32)
    top_val, top_idx = lax.top_k(logits, TOP_K)
    top_w = jax.nn.softmax(top_val, axis=-1)
    gates = jnp.sum(jax.nn.one_hot(top_idx, N_EXPERTS, dtype=jnp.float32) * top_w[..., None], axis=-2)
    out = jnp.zeros_like(h)
    for e in range(N_EXPERTS):
        y = swiglu(h, w_gate[e], w_up[e], w_down[e])
        out = out + gates[..., e:e + 1].astype(h.dtype) * y
    return out

def first_inputs(seed: int = 0) -> dict:
    key = jax.random.key(seed)
    ks = jax.random.split(key, 20)
    D = D_MODEL

    def w(k, shape, fan_in):
        return jax.random.normal(k, shape, dtype=jnp.float32) * (fan_in ** -0.5)

    def gain(k, shape):
        return 1.0 + 0.02 * jax.random.normal(k, shape, dtype=jnp.float32)

    return {
        "x": jax.random.normal(ks[0], (BATCH, SEQ, D), dtype=jnp.float32),
        "attn_norm": gain(ks[1], (DEPTH, D)),
        "ffn_norm": gain(ks[2], (DEPTH, D)),
        "kv_norm": gain(ks[3], (D,)),
        "final_norm": gain(ks[4], (D,)),
        "gla_w_in": w(ks[5], (N_A, D, GLA_IN), D),
        "gla_w_gate_up": w(ks[6], (N_A, GLA_GATE_RANK, GLA_QK), GLA_GATE_RANK),
        "gla_b_gate": 0.1 * jax.random.normal(ks[7], (N_A, GLA_QK), dtype=jnp.float32),
        "gla_head_norm": gain(ks[8], (N_A, GLA_DV)),
        "gla_w_out": w(ks[9], (N_A, GLA_V, D), GLA_V),
        "sb_w_kv": w(ks[10], (D, 2 * SB_HEADS * SB_HEAD_DIM), D),
        "sb_w_q": w(ks[11], (N_B, D, SB_HEADS * SB_HEAD_DIM), D),
        "sb_w_out": w(ks[12], (N_B, SB_HEADS * SB_HEAD_DIM, D), SB_HEADS * SB_HEAD_DIM),
        "ffn_w_gate": w(ks[13], (N_DENSE, D, FFN_DIM), D),
        "ffn_w_up": w(ks[14], (N_DENSE, D, FFN_DIM), D),
        "ffn_w_down": w(ks[15], (N_DENSE, FFN_DIM, D), FFN_DIM),
        "moe_w_router": w(ks[16], (N_MOE, D, N_EXPERTS), D),
        "moe_w_gate": w(ks[17], (N_MOE, N_EXPERTS, D, EXPERT_DIM), D),
        "moe_w_up": w(ks[18], (N_MOE, N_EXPERTS, D, EXPERT_DIM), D),
        "moe_w_down": w(ks[19], (N_MOE, N_EXPERTS, EXPERT_DIM, D), EXPERT_DIM),
    }

def first_block(x, attn_norm, ffn_norm, kv_norm, final_norm, gla_w_in, gla_w_gate_up, gla_b_gate,
              gla_head_norm, gla_w_out, sb_w_kv, sb_w_q, sb_w_out, ffn_w_gate, ffn_w_up, ffn_w_down,
              moe_w_router, moe_w_gate, moe_w_up, moe_w_down):
    B, S, D = x.shape
    h = x
    k_shared = None
    v_shared = None
    for layer in range(DEPTH):
        if layer < N_A:
            h = h + gla_mixer(rms_norm(h, attn_norm[layer]), gla_w_in[layer], gla_w_gate_up[layer],
                              gla_b_gate[layer], gla_head_norm[layer], gla_w_out[layer])
        else:
            if layer == N_A:
                kv = rms_norm(h, kv_norm) @ sb_w_kv
                k_s, v_s = jnp.split(kv, 2, axis=-1)
                k_shared = k_s.reshape(B, S, SB_HEADS, SB_HEAD_DIM).transpose(0, 2, 1, 3)
                v_shared = v_s.reshape(B, S, SB_HEADS, SB_HEAD_DIM).transpose(0, 2, 1, 3)
            ib = layer - N_A
            h = h + stick_breaking_mixer(rms_norm(h, attn_norm[layer]), k_shared, v_shared,
                                         sb_w_q[ib], sb_w_out[ib])
        hn = rms_norm(h, ffn_norm[layer])
        if layer % 2 == 0:
            i = layer // 2
            h = h + swiglu(hn, ffn_w_gate[i], ffn_w_up[i], ffn_w_down[i])
        else:
            i = layer // 2
            h = h + moe_swiglu(hn, moe_w_router[i], moe_w_gate[i], moe_w_up[i], moe_w_down[i])
    return rms_norm(h, final_norm)


DEPTH_2 = 1

HEAD_DIM = 64
A_HEADS = D_MODEL // 128
B_HEADS = D_MODEL // 256
C_HEADS = D_MODEL // 256
A_DIM = A_HEADS * HEAD_DIM
B_DIM = B_HEADS * HEAD_DIM
C_DIM = C_HEADS * HEAD_DIM
D_MIX = A_DIM + B_DIM + C_DIM
IN_SPLITS = (A_DIM, A_DIM, A_DIM, A_HEADS, 2 * B_DIM, B_DIM, B_HEADS, B_HEADS, B_DIM, C_DIM, C_DIM, C_DIM, C_DIM)
IN_WIDTH = 3 * A_DIM + A_HEADS + 4 * B_DIM + 2 * B_HEADS + 4 * C_DIM
Q_BLOCK = 128
MLSTM_CHUNK = 64
HGRN_CHUNK = 16
MLSTM_CONV = 4
FFN_CONV = 3
D_FF = ((8 * D_MODEL // 3 + 255) // 256) * 256
EPS = 1e-6


def _rms(x, g):
    xf = x.astype(jnp.float32)
    y = xf * lax.rsqrt(jnp.mean(xf * xf, axis=-1, keepdims=True) + EPS)
    return (y * g.astype(jnp.float32)).astype(x.dtype)

def _heads(z, h):
    b, t, _ = z.shape
    return z.reshape(b, t, h, -1).transpose(0, 2, 1, 3).astype(jnp.float32)

def _merge(o):
    return o.transpose(0, 2, 1, 3)

def _split_cols(z):
    idx = np.cumsum(IN_SPLITS)[:-1].tolist()
    return jnp.split(z, idx, axis=-1)

def _causal_dwconv(x, w):
    k, c = w.shape
    return lax.conv_general_dilated(x, w[:, None, :], window_strides=(1,), padding=[(k - 1, 0)],
                                    dimension_numbers=('NWC', 'WIO', 'NWC'), feature_group_count=c)

def _fox_attention(q, k, v, c):
    bsz, h, t, d = q.shape
    nb = t // Q_BLOCK
    qb = q.reshape(bsz, h, nb, Q_BLOCK, d).transpose(2, 0, 1, 3, 4)
    cb = c.reshape(bsz, h, nb, Q_BLOCK).transpose(2, 0, 1, 3)
    kpos = jnp.arange(t)
    scale = d ** -0.5

    def one_block(args):
        qi, ci, bi = args
        s = jnp.einsum('bhqd,bhkd->bhqk', qi, k) * scale
        s = s + ci[..., None] - c[:, :, None, :]
        qpos = bi * Q_BLOCK + jnp.arange(Q_BLOCK)
        s = jnp.where(kpos[None, :] <= qpos[:, None], s, -jnp.inf)
        p = jax.nn.softmax(s, axis=-1)
        return jnp.einsum('bhqk,bhkd->bhqd', p, v)

    ob = lax.map(one_block, (qb, cb, jnp.arange(nb)))
    return ob.transpose(1, 2, 0, 3, 4).reshape(bsz, h, t, d)

def _mlstm_chunkwise(q, k, v, i_pre, f_pre):
    bsz, h, t, d = q.shape
    L = MLSTM_CHUNK
    nc = t // L
    k = k * d ** -0.5
    qc = q.reshape(bsz, h, nc, L, d)
    kc = k.reshape(bsz, h, nc, L, d)
    vc = v.reshape(bsz, h, nc, L, d)
    ic = i_pre.reshape(bsz, h, nc, L)
    bc = jnp.cumsum(jax.nn.log_sigmoid(f_pre).reshape(bsz, h, nc, L), axis=-1)
    gc = bc[..., -1]
    ac = gc[..., None] - bc + ic

    def step(carry, inp):
        cs, ns, m = carry
        kj, vj, aj, gj = inp
        m_new = jnp.maximum(gj + m, jnp.max(aj, axis=-1))
        decay = jnp.exp(gj + m - m_new)
        w = jnp.exp(aj - m_new[..., None])
        cs_new = decay[..., None, None] * cs + jnp.einsum('bhl,bhld,bhle->bhde', w, kj, vj)
        ns_new = decay[..., None] * ns + jnp.einsum('bhl,bhld->bhd', w, kj)
        return (cs_new, ns_new, m_new), (cs, ns, m)

    mv = lambda a: jnp.moveaxis(a, 2, 0)
    init = (jnp.zeros((bsz, h, d, d), jnp.float32), jnp.zeros((bsz, h, d), jnp.float32),
            jnp.full((bsz, h), -jnp.inf, jnp.float32))
    _, (c_prev, n_prev, m_prev) = lax.scan(step, init, (mv(kc), mv(vc), mv(ac), gc.transpose(2, 0, 1)))
    c_prev = jnp.moveaxis(c_prev, 0, 2)
    n_prev = jnp.moveaxis(n_prev, 0, 2)
    m_prev = jnp.moveaxis(m_prev, 0, 2)

    tri = jnp.tril(jnp.ones((L, L), bool))
    log_d = jnp.where(tri, bc[..., :, None] - bc[..., None, :] + ic[..., None, :], -jnp.inf)
    m_inter = bc + m_prev[..., None]
    m_out = jnp.maximum(m_inter, jnp.max(log_d, axis=-1))
    sqk = jnp.einsum('bhcld,bhcsd->bhcls', qc, kc) * jnp.exp(log_d - m_out[..., None])
    inter_w = jnp.exp(m_inter - m_out)
    num = jnp.einsum('bhcls,bhcse->bhcle', sqk, vc) + inter_w[..., None] * jnp.einsum('bhcld,bhcde->bhcle', qc, c_prev)
    den = jnp.sum(sqk, axis=-1) + inter_w * jnp.einsum('bhcld,bhcd->bhcl', qc, n_prev)
    out = num / jnp.maximum(jnp.abs(den), jnp.exp(-m_out))[..., None]
    return out.reshape(bsz, h, t, d)

def _hgrn2_chunkwise(q, logf, i):
    bsz, h, t, dk = q.shape
    dv = i.shape[-1]
    L = HGRN_CHUNK
    nc = t // L
    k = -jnp.expm1(logf)
    qc = q.reshape(bsz, h, nc, L, dk)
    kc = k.reshape(bsz, h, nc, L, dk)
    vc = i.reshape(bsz, h, nc, L, dv)
    bc = jnp.cumsum(logf.reshape(bsz, h, nc, L, dk), axis=3)
    blast = bc[:, :, :, -1]
    tri = jnp.tril(jnp.ones((L, L), bool))
    rel = jnp.where(tri[:, :, None], bc[:, :, :, :, None, :] - bc[:, :, :, None, :, :], -jnp.inf)
    att = jnp.einsum('bhctd,bhcsd,bhctsd->bhcts', qc, kc, jnp.exp(rel))
    intra = jnp.einsum('bhcts,bhcse->bhcte', att, vc)

    def step(s, inp):
        kj, vj, bj, blj = inp
        kd = kj * jnp.exp(blj[:, :, None, :] - bj)
        return jnp.exp(blj)[..., None] * s + jnp.einsum('bhld,bhle->bhde', kd, vj), s

    mv = lambda a: jnp.moveaxis(a, 2, 0)
    _, s_prev = lax.scan(step, jnp.zeros((bsz, h, dk, dv), jnp.float32), (mv(kc), mv(vc), mv(bc), mv(blast)))
    s_prev = jnp.moveaxis(s_prev, 0, 2)
    inter = jnp.einsum('bhctd,bhcde->bhcte', qc * jnp.exp(bc), s_prev)
    return (intra + inter).reshape(bsz, h, t, dv)

def _mixer(h, lb, w_in, b_in, a_q_g, a_k_g, b_conv_w, out_g, w_out):
    bsz, t, _ = h.shape
    f32 = jnp.float32
    z = h @ w_in + b_in
    (a_q, a_k, a_v, a_f, b_qk, b_v, b_i, b_f, b_o, c_q, c_f, c_i, c_g) = _split_cols(z)
    qa = _rms(_heads(a_q, A_HEADS), a_q_g)
    ka = _rms(_heads(a_k, A_HEADS), a_k_g)
    ca = jnp.cumsum(jax.nn.log_sigmoid(a_f.astype(f32)), axis=1).transpose(0, 2, 1)
    oa = _fox_attention(qa, ka, _heads(a_v, A_HEADS), ca)
    qk = jax.nn.silu(_causal_dwconv(b_qk, b_conv_w))
    qb, kb = jnp.split(qk, 2, axis=-1)
    ob = _mlstm_chunkwise(_heads(qb, B_HEADS), _heads(kb, B_HEADS), _heads(b_v, B_HEADS),
                          b_i.astype(f32).transpose(0, 2, 1), b_f.astype(f32).transpose(0, 2, 1))
    lbh = lb.reshape(C_HEADS, 1, HEAD_DIM)
    logf = jnp.logaddexp(jnp.log(lbh), jnp.log1p(-lbh) + jax.nn.log_sigmoid(_heads(c_f, C_HEADS)))
    oc = _hgrn2_chunkwise(jax.nn.silu(_heads(c_q, C_HEADS)), logf, _heads(c_i, C_HEADS))
    g_a, g_b, g_c = jnp.split(out_g.astype(f32), [A_DIM, A_DIM + B_DIM])
    ya = _rms(_merge(oa), g_a.reshape(A_HEADS, HEAD_DIM)).reshape(bsz, t, A_DIM)
    yb = jax.nn.sigmoid(b_o.astype(f32)) * _rms(_merge(ob), g_b.reshape(B_HEADS, HEAD_DIM)).reshape(bsz, t, B_DIM)
    yc = jax.nn.silu(c_g.astype(f32)) * _rms(_merge(oc), g_c.reshape(C_HEADS, HEAD_DIM)).reshape(bsz, t, C_DIM)
    y = jnp.concatenate([ya, yb, yc], axis=-1).astype(h.dtype)
    return y @ w_out

def _conv_glu(h, w_up, conv_w, conv_b, w_down):
    u = _causal_dwconv(h @ w_up, conv_w) + conv_b
    gate, up = jnp.split(u, 2, axis=-1)
    return (jax.nn.silu(gate) * up) @ w_down

def second_inputs(seed: int = 0) -> dict:
    key = jax.random.key(seed)
    ks = jax.random.split(key, 16)
    f32 = jnp.float32
    nrm = lambda k, shape, s: jax.random.normal(k, shape, f32) * s
    gate_offsets = jnp.concatenate([
        jnp.zeros((3 * A_DIM,), f32), jnp.linspace(1.0, 4.0, A_HEADS, dtype=f32),
        jnp.zeros((3 * B_DIM + B_HEADS,), f32), jnp.linspace(3.0, 6.0, B_HEADS, dtype=f32),
        jnp.zeros((B_DIM + 4 * C_DIM,), f32)])
    return {
        "x": nrm(ks[0], (BATCH, SEQ, D_MODEL), 1.0),
        "lb_logits": nrm(ks[1], (DEPTH_2, C_DIM), 0.5),
        "norm_mix_g": 1.0 + nrm(ks[2], (DEPTH_2, D_MODEL), 0.02),
        "w_in": nrm(ks[3], (DEPTH_2, D_MODEL, IN_WIDTH), D_MODEL ** -0.5),
        "b_in": nrm(ks[4], (DEPTH_2, IN_WIDTH), 0.02) + gate_offsets,
        "a_q_g": 1.0 + nrm(ks[5], (DEPTH_2, HEAD_DIM), 0.02),
        "a_k_g": 1.0 + nrm(ks[6], (DEPTH_2, HEAD_DIM), 0.02),
        "b_conv_w": nrm(ks[7], (DEPTH_2, MLSTM_CONV, 2 * B_DIM), MLSTM_CONV ** -0.5),
        "out_g": 1.0 + nrm(ks[8], (DEPTH_2, D_MIX), 0.02),
        "w_out": nrm(ks[9], (DEPTH_2, D_MIX, D_MODEL), D_MIX ** -0.5),
        "norm_ffn_g": 1.0 + nrm(ks[10], (DEPTH_2, D_MODEL), 0.02),
        "w_up": nrm(ks[11], (DEPTH_2, D_MODEL, 2 * D_FF), D_MODEL ** -0.5),
        "ffn_conv_w": nrm(ks[12], (DEPTH_2, FFN_CONV, 2 * D_FF), FFN_CONV ** -0.5),
        "ffn_conv_b": nrm(ks[13], (DEPTH_2, 2 * D_FF), 0.02),
        "w_down": nrm(ks[14], (DEPTH_2, D_FF, D_MODEL), D_FF ** -0.5),
    }

def second_block(x, lb_logits, norm_mix_g, w_in, b_in, a_q_g, a_k_g, b_conv_w, out_g, w_out,
              norm_ffn_g, w_up, ffn_conv_w, ffn_conv_b, w_down):
    p = jax.nn.softmax(lb_logits.astype(jnp.float32), axis=0)
    lb_all = jnp.maximum(jnp.cumsum(p, axis=0) - p[0], 0.0)
    for l in range(DEPTH_2):
        h = _rms(x, norm_mix_g[l])
        x = x + _mixer(h, lb_all[l], w_in[l], b_in[l], a_q_g[l], a_k_g[l], b_conv_w[l], out_g[l], w_out[l])
        h = _rms(x, norm_ffn_g[l])
        x = x + _conv_glu(h, w_up[l], ffn_conv_w[l], ffn_conv_b[l], w_down[l])
    return x


def setup_inputs(seed=0):
    out = dict(first_inputs(seed))
    for name, value in second_inputs(seed + 1).items():
        if name != "x":
            out[name + "_2"] = value
    return out


def reference(
    x, attn_norm, ffn_norm, kv_norm, final_norm, gla_w_in, gla_w_gate_up, gla_b_gate,
    gla_head_norm, gla_w_out, sb_w_kv, sb_w_q, sb_w_out, ffn_w_gate, ffn_w_up, ffn_w_down,
    moe_w_router, moe_w_gate, moe_w_up, moe_w_down, lb_logits_2, norm_mix_g_2, w_in_2, b_in_2,
    a_q_g_2, a_k_g_2, b_conv_w_2, out_g_2, w_out_2, norm_ffn_g_2, w_up_2, ffn_conv_w_2,
    ffn_conv_b_2, w_down_2,
):
    x = first_block(
        x, attn_norm, ffn_norm, kv_norm, final_norm, gla_w_in, gla_w_gate_up, gla_b_gate,
        gla_head_norm, gla_w_out, sb_w_kv, sb_w_q, sb_w_out, ffn_w_gate, ffn_w_up, ffn_w_down,
        moe_w_router, moe_w_gate, moe_w_up, moe_w_down,
    )
    return second_block(
        x, lb_logits_2, norm_mix_g_2, w_in_2, b_in_2, a_q_g_2, a_k_g_2, b_conv_w_2, out_g_2,
        w_out_2, norm_ffn_g_2, w_up_2, ffn_conv_w_2, ffn_conv_b_2, w_down_2,
    )


_drawn_inputs = setup_inputs


def setup_inputs(seed=0):
    import zlib

    import numpy as np

    out = dict(_drawn_inputs(seed))
    spreads = {}
    factors = {'norm_mix_g_2': 2.69,
     'a_q_g_2': 4.95,
     'a_k_g_2': 6.463,
     'out_g_2': 3.938,
     'norm_ffn_g_2': 4.613,
     'ffn_conv_b_2': 4.601}
    for name, (base, spread) in spreads.items():
        noise = np.random.default_rng([zlib.crc32(name.encode()), seed]).standard_normal(out[name].shape)
        drawn = base * np.exp(spread * noise) if base else spread * noise
        out[name] = __import__('jax').numpy.asarray(drawn.astype(out[name].dtype))
    for name, factor in factors.items():
        out[name] = (out[name] * factor).astype(out[name].dtype)
    return out
```

```python
def build(nc, IN, out):
    import concourse.bass as bass
    from concourse import mybir
    from contextlib import ExitStack

    F32, I32 = mybir.dt.float32, mybir.dt.int32
    ACT, ALU, AX = mybir.ActivationFunctionType, mybir.AluOpType, mybir.AxisListType
    P = 128
    _, S, D = IN["x"].shape
    TT = S // P
    KD = D // P
    EPS = 1e-6
    NEG = -1e30
    F1 = IN["ffn_w_gate"].shape[2]
    F2 = IN["w_down_2"].shape[1]
    _, NE, _, FE = IN["moe_w_gate"].shape
    GH, GDK, GDV = 4, 128, 256
    GR = IN["gla_w_gate_up"].shape[1]
    GQK, GV = GH * GDK, GH * GDV
    GATE_NORM = 16.0
    SH = 8
    AH, BH, CH, HD = 8, 4, 4, 64
    AD, BD = AH * HD, BH * HD
    FJ = 256
    NJ1, NJ2 = F1 // FJ, F2 // FJ
    assert NJ1 == NJ2 and NJ1 % 2 == 1
    EJ = 512
    NEJ = FE // EJ
    SLOT = 512 * KD
    NS = 6
    LEVELS = [0, 1, 2, 4, 8, 16, 32, 64]
    C_AQ, C_AK, C_AV, C_AF = 0, AD, 2 * AD, 3 * AD
    C_BQK = 3 * AD + AH
    C_BV = C_BQK + 2 * BD
    C_BI = C_BV + BD
    C_BF = C_BI + BH
    C_BO = C_BF + BH
    C_CQ = C_BO + BD
    C_CI = C_CQ + 2 * BD
    C_CG = C_CI + BD

    ctx = ExitStack()
    with ctx:
        def sb(name, shape, dt=F32):
            return ctx.enter_context(nc.sbuf_tensor(name, shape, dt))

        sems = {}

        def sg(name):
            if name not in sems:
                sems[name] = ctx.enter_context(nc.semaphore(name))
            return sems[name]

        ring = sb("ring", [P, NS, SLOT])
        h = sb("h", [P, TT, D])
        xT = sb("xT", [P, KD, S])
        xT2 = sb("xT2", [P, KD, S])
        xn = sb("xn", [P, TT, D])
        arena = sb("arena", [P, 13312])
        ident = sb("ident", [P, P])
        lmask = sb("lmask", [P, len(LEVELS) - 1, P])
        after = sb("after", [P, P])
        before3 = sb("before3", [P, 3, P])
        rowneg3 = sb("rowneg3", [P, 3, P])
        colneg3 = sb("colneg3", [P, 3, P])
        pair64 = sb("pair64", [P, P])
        sel = sb("sel", [P, AH, P])
        iota = sb("iota", [P, P])
        tri8 = sb("tri8", [P, NE, NE])
        cst = sb("cst", [P, 34])
        c_eps, c_one, c_half = cst[:, 0:1], cst[:, 1:2], cst[:, 2:34]
        ws = sb("ws", [P, 3, KD, 72])
        wglr = sb("wglr", [P, KD, GR])
        wgu = sb("wgu", [GR, GQK])
        wrt = sb("wrt", [P, KD, NE])
        vT = sb("vT", [P, 3, P])
        ssq = sb("ssq", [P, 32])
        ms = sb("ms", [P, 32])
        rstd = sb("rstd", [P, 32])
        scr = sb("scr", [P, 1])
        bank = [ctx.enter_context(nc.psum_tensor(f"bank{b}", [P, 512], F32)) for b in range(8)]

        ar_at = [0]

        def ar_reset(at=0):
            ar_at[0] = at

        def ar(n):
            a = arena[:, ar_at[0]:ar_at[0] + n]
            ar_at[0] += n
            assert ar_at[0] <= 13312, ar_at[0]
            return a

        vec_rows = {}
        vec_dma = []
        at = [0, 0, 0]

        def rows(name, tile, ap, n):
            vec_rows[name] = (tile, at[tile])
            vec_dma.append((tile, at[tile], n, ap))
            at[tile] += n

        for nm, n in (("attn_norm", 2 * KD), ("ffn_norm", 2 * KD), ("kv_norm", KD), ("norm_mix_g_2", KD),
                      ("norm_ffn_g_2", KD), ("out_g_2", KD), ("gla_b_gate", GQK // P), ("gla_head_norm", GDV // P),
                      ("gla_head_norm again", GDV // P), ("lb_logits_2", 2)):
            a = IN[nm.split()[0]]
            a = a.rearrange("(r p) -> r p", p=P) if len(a.shape) == 1 else a.rearrange("a (r p) -> (a r) p", p=P)
            rows(nm, 0, a, n)
        for nm, c0, n in (("aq_b", C_AQ, 4), ("ak_b", C_AK, 4), ("bqk_b", C_BQK, 4), ("cqf_b", C_CQ, 4)):
            rows(nm, 0, IN["b_in_2"][0, c0:c0 + n * P].rearrange("(r p) -> r p", p=P), n)
        rows("b_conv", 0, IN["b_conv_w_2"].rearrange("a k (r p) -> (a k r) p", p=P), 16)
        R_G = at[0]
        at[0] += 5
        NF2 = 2 * F2 // P
        rows("tap01", 1, IN["ffn_conv_w_2"][0, 0:2, :].rearrange("k (r p) -> (k r) p", p=P), 2 * NF2)
        rows("tap2", 2, IN["ffn_conv_w_2"][0, 2:3, :].rearrange("k (r p) -> (k r) p", p=P), NF2)
        rows("conv_b", 2, IN["ffn_conv_b_2"].rearrange("k (r p) -> (k r) p", p=P), NF2)
        V_ROWS = [at[0], at[1], at[2]]
        N_VEC = len(vec_dma) + 10

        def col(name, i=0):
            tile, r = vec_rows[name]
            return vT[:, tile, r + i:r + i + 1]

        def cols(name, i, n):
            tile, r = vec_rows[name]
            return vT[:, tile, r + i:r + i + n]

        turns, uses, rr = {}, [0] * 8, [0]

        def turn(label, b=None):
            if b is None:
                b = rr[0] % 8
                rr[0] += 1
            turns[label] = (b, uses[b])
            uses[b] += 1

        full = [sg(f"full{b}") for b in range(8)]
        freed = [sg(f"freed{b}") for b in range(8)]

        def plan_norm(n):
            for t in range(TT):
                for half in range(2):
                    turn((n, t, half))

        def plan_ffn(f):
            def gu(j):
                turn((f, j, "g"), 2 * (j % 2))
                turn((f, j, "u"), 2 * (j % 2) + 1)
            gu(0)
            for t in range(TT):
                for half in range(2):
                    turn((f, "acc", t, half), 4 + 2 * t + half)
            for j in range(1, NJ1):
                gu(j)
            rr[0] = 0

        for i in range(3):
            turn(("vec", i))
        plan_norm("n0")
        for lab in ("glr", ("gate", 0), ("gate", 1), ("q", 0), ("q", 1), ("k", 0), ("k", 1)):
            turn(lab)
        for nm in "vr":
            for c in range(2):
                for t in range(TT):
                    turn((nm, c, t))

        def plan_levels(pre, cross):
            for m in LEVELS:
                for g in range(2):
                    turn((pre, m, g))
            for g in range(cross):
                turn((pre, P, g))

        plan_levels("gl", 1)
        for t in range(TT):
            for hp in range(2):
                turn(("o", t, hp))
        plan_norm("y")
        for c in range(2):
            for t in range(TT):
                turn(("wo", c, t))
        plan_norm("n1")
        plan_ffn("f1")
        plan_norm("n2")
        for b in range(4):
            turn(("sk", b))
        for c in range(2):
            for t in range(TT):
                turn(("sv", c, t))
        for b in range(4):
            turn(("sq", b))
        for hd in range(SH):
            turn(("z", hd))
        for hd in range(SH):
            turn(("stay", hd))
        for hp in range(SH // 2):
            turn(("so", hp))
        for c in range(2):
            for t in range(TT):
                turn(("swo", c, t))
        plan_norm("n3")
        turn("lg")
        turn("pos")
        turn("cnt")
        uses_before_moe = list(uses)
        plan_norm("n4")
        for b in range(2):
            turn(("cqf", b))
        for t in range(TT):
            turn(("cig", t))
        plan_levels("hl", 2)
        for t in range(TT):
            turn(("co", t))
        for nm in ("aq", "ak"):
            for b in range(2):
                turn((nm, b))
        for t in range(TT):
            turn(("av", t))
        for b in range(2):
            turn(("bqk", b))
        for t in range(TT):
            turn(("bvo", t))
        for nm in ("cf", "bi", "bf"):
            turn(nm)
        for i in range(4):
            turn(("qkss", i))
        rr[0] = 0
        for t in range(TT):
            turn(("ao", t), 6 + t)
        for hd in range(AH):
            turn(("s", hd), hd % 3)
            turn(("pT", hd), 3 + hd % 3)
        turn("mT", 0)
        for t in range(TT):
            turn(("bo", t), 6 + t)
        for hd in range(BH):
            turn(("P2", hd), 1 + hd % 2)
            turn(("P1", hd), 3 + hd % 2)
        rr[0] = 0
        plan_norm("yy")
        for c in range(2):
            for t in range(TT):
                turn(("w2", c, t))
        plan_norm("n5")
        plan_ffn("f2")

        def see(eng, label):
            b, n = turns[label]
            eng.wait_ge(full[b], n + 1)
            return bank[b]

        def gone(eng, label):
            b, n = turns[label]
            eng.wait_ge(freed[b], n + 1)

        class Order:

            def __init__(self, eng, name):
                self.eng, self.own, self.count = eng, sg(name), {}

            def __call__(self, ins, name=None, frees=None):
                if frees is not None:
                    b, n = turns[frees]
                    ins.then_inc(freed[b], 1)
                    self.eng.wait_ge(freed[b], n + 1)
                    return
                s = self.own if name is None else sg(name)
                n = self.count[name] = self.count.get(name, 0) + 1
                ins.then_inc(s, 1)
                self.eng.wait_ge(s, n)

        def kpn(ap):
            return ap.rearrange("(k p) n -> p k n", p=P)

        w1 = IN["gla_w_in"][0]
        chunks = []

        def chunk(parts, last, phase):
            chunks.append((parts, last, phase))

        def slot(i):
            return ring[:, i % NS, :]

        def wide(i, c0=0, n=512):
            return slot(i).rearrange("p (k n) -> p k n", k=KD)[:, :, c0:c0 + n]

        def deep(i, k=4):
            return slot(i).rearrange("p (k n) -> p k n", k=4)[:, 0:k, :]

        def cols_chunk(src, c0, last, phase, n=512):
            chunk([(0, n, kpn(src[:, c0:c0 + n]))], last, phase)

        pos = {}

        def name_chunk(nm):
            pos[nm] = len(chunks)

        for nm, c0, last in (("q", 0, ("q", 1)), ("k", GQK, ("k", 1)), ("v0", 2 * GQK, ("v", 0, 1)),
                             ("v1", 2 * GQK + 512, ("v", 1, 1)),
                             ("r0", 2 * GQK + GV + GR, ("r", 0, 1)), ("r1", 2 * GQK + GV + GR + 512, ("r", 1, 1))):
            name_chunk(nm)
            cols_chunk(w1, c0, last, 0)
        for c in range(2):
            name_chunk(("wo", c))
            cols_chunk(IN["gla_w_out"][0], 512 * c, ("wo", c, 1), 0)

        def ffn_chunks(f, gate, up, down, phase):
            for j in range(NJ1):
                name_chunk((f, "gu", j))
                chunk([(0, FJ, kpn(gate[:, j * FJ:(j + 1) * FJ])), (FJ, 2 * FJ, kpn(up[:, j * FJ:(j + 1) * FJ]))],
                      (f, j, "u"), phase)
                if j % 2 == 1 or j == NJ1 - 1:
                    j0 = j - j % 2
                    name_chunk((f, "d", j0))
                    chunk([("deep", kpn(down[j0 * FJ:(j + 1) * FJ, :]))],
                          ("down", f, j + 1) if j < NJ1 - 1 else (f, "acc", 1, 1), phase)

        ffn_chunks("f1", IN["ffn_w_gate"][0], IN["ffn_w_up"][0], IN["ffn_w_down"][0], 0)
        for nm, src, c0, last in (("sk0", "sb_w_kv", 0, ("sk", 1)), ("sk1", "sb_w_kv", 512, ("sk", 3)),
                                  ("sv0", "sb_w_kv", 1024, ("sv", 0, 1)), ("sv1", "sb_w_kv", 1536, ("sv", 1, 1)),
                                  ("sq0", "sb_w_q", 0, ("sq", 1)), ("sq1", "sb_w_q", 512, ("sq", 3)),
                                  ("so0", "sb_w_out", 0, ("swo", 0, 1)), ("so1", "sb_w_out", 512, ("swo", 1, 1))):
            name_chunk(nm)
            a = IN[src]
            cols_chunk(a if len(a.shape) == 2 else a[0], c0, last, 0)
        N_PRE = len(chunks)
        M0 = N_PRE
        w2 = IN["w_in_2"][0]
        for nm, c0, last in (("cqf", C_CQ, ("cqf", 1)), ("cig", C_CI, ("cig", 1)), ("aq", C_AQ, ("aq", 1)),
                             ("ak", C_AK, ("ak", 1)), ("av", C_AV, ("av", 1)), ("bqk", C_BQK, ("bqk", 1))):
            name_chunk(nm)
            cols_chunk(w2, c0, last, 1)
        name_chunk("bvo")
        chunk([(0, BD, kpn(w2[:, C_BV:C_BV + BD])), (BD, 2 * BD, kpn(w2[:, C_BO:C_BO + BD]))], ("bvo", 1), 1)
        for c in range(2):
            name_chunk(("w2", c))
            cols_chunk(IN["w_out_2"][0], 512 * c, ("w2", c, 1), 1)
        ffn_chunks("f2", IN["w_up_2"][0][:, 0:F2], IN["w_up_2"][0][:, F2:2 * F2], IN["w_down_2"][0], 1)

        ring_in = [sg(f"ring_in{s}") for s in range(NS)]
        ring_in2 = [sg(f"ring_in2_{s}") for s in range(NS)]
        arrive, filled = [], {0: [0] * NS, 1: [0] * NS}
        for i, (parts, last, ph) in enumerate(chunks):
            filled[ph][i % NS] += 16 * len(parts)
            arrive.append(filled[ph][i % NS])

        def arrived(pe, nm):
            i = pos[nm]
            pe.wait_ge((ring_in if chunks[i][2] == 0 else ring_in2)[i % NS], arrive[i])
            return i

        uorder = []
        for j in range(NEJ):
            uorder += [("g", j), ("u", j)] + ([("d", j - 1)] if j else [])
        uorder += [("d", NEJ - 1)]
        UC = len(uorder)
        PC = 2 * UC
        assert PC % NS == 0
        upos = {c: i for i, c in enumerate(uorder)}
        NPAIR = NE // 2

        vrow = xT2.rearrange("p k s -> p (k s)")[:, 0:3 * P].rearrange("p (a b) -> p a b", a=3)
        ar_reset()
        g = {}
        for nm in ("Q", "K", "A", "E", "W", "qt", "kt"):
            g[nm] = ar(GH * S)
        g["att"] = ar(2 * 512).rearrange("p (g n) -> p g n", g=2)
        g["crs"] = ar(512)
        g["mt"] = ar(512)
        gv = ar(TT * GV).rearrange("p (t n) -> p t n", t=TT)
        gr = ar(TT * GV).rearrange("p (t n) -> p t n", t=TT)
        glrT = xT2.rearrange("p k s -> p (k s)")[0:GR, 512:512 + S]
        ar_reset()
        f_sg = ar(2 * 512).rearrange("p (a n) -> p a n", a=2)
        f_act = ar(2 * 512).rearrange("p (a n) -> p a n", a=2)
        f_cu = ar(2 * 1024).rearrange("p (a n) -> p a n", a=2)
        ar_reset()
        skT = ar(SH * S).rearrange("p (h s) -> p h s", h=SH)
        sqT = ar(SH * S).rearrange("p (h s) -> p h s", h=SH)
        sE, sT, sU = (ar(SH * 384).rearrange("p (h s) -> p h s", h=SH) for _ in range(3))
        sv = xn
        ar_reset()
        lg = ar(TT * NE).rearrange("p (t e) -> p t e", t=TT)
        cmp1 = ar(TT * NE * NE).rearrange("p (t e j) -> p t e j", t=TT, e=NE)
        cmp2 = ar(TT * NE * NE).rearrange("p (t e j) -> p t e j", t=TT, e=NE)
        rank = ar(TT * NE).rearrange("p (t e) -> p t e", t=TT)
        selx = ar(TT * NE).rearrange("p (t e) -> p t e", t=TT)
        mx = ar(TT)
        ex = ar(TT * NE).rearrange("p (t e) -> p t e", t=TT)
        exs = ar(TT)
        NU = 2 * NE + 2
        pm = ar(NU * TT).rearrange("p (u t) -> p u t", u=NU)
        gt = ar(NU * TT).rearrange("p (u t) -> p u t", u=NU)
        cmax = ar(2)
        more_i = ar(1).bitcast(I32)
        oh = ar(TT * P).rearrange("p (t s) -> p t s", t=TT)
        ohg = ar(TT * P).rearrange("p (t s) -> p t s", t=TT)
        ohT = ar(S)
        xg = ar(KD * P).rearrange("p (k s) -> p k s", k=KD)
        esg = ar(2 * EJ).rearrange("p (a n) -> p a n", a=2)
        eact = ar(2 * EJ).rearrange("p (a n) -> p a n", a=2)
        eactT = ar(2 * EJ).rearrange("p (a n) -> p a n", a=2)
        ey = ar(D)
        fgain = xT2.rearrange("p k s -> p (k s)")[:, 0:D]
        ar_reset()
        aq, ak = (ar(4 * S).rearrange("p (b s) -> p b s", b=4) for _ in range(2))
        av = ar(TT * AD).rearrange("p (t n) -> p t n", t=TT)
        bz, bc = (ar(4 * S).rearrange("p (b s) -> p b s", b=4) for _ in range(2))
        bv = ar(TT * BH * 65).rearrange("p (t h n) -> p t h n", t=TT, h=BH)
        bog = ar(TT * BD).rearrange("p (t n) -> p t n", t=TT)
        ci = ar(TT * BD).rearrange("p (t n) -> p t n", t=TT)
        cg = ar(TT * BD).rearrange("p (t n) -> p t n", t=TT)
        mix_tmp = ar_at[0]
        m = {}
        for nm in ("Q", "K", "A", "E", "W", "qt", "kt"):
            m[nm] = ar(2 * S)
        m["att"] = ar(2 * 512).rearrange("p (g n) -> p g n", g=2)
        m["crs"] = ar(512)
        m["mt"] = ar(512)
        lbp, lb1 = ar(2), ar(2)
        ar_reset(mix_tmp)
        rs = ar(8 * S)
        ar_reset(mix_tmp)
        sS = ar(2 * 384).rearrange("p (a n) -> p a n", a=2)
        pTs = ar(2 * 384).rearrange("p (a n) -> p a n", a=2)
        Dm = ar(2 * 384).rearrange("p (a n) -> p a n", a=2)
        ar_at[0] = max(ar_at[0], mix_tmp + 8 * S)
        cS, ncS, iF, nM, mS, row1 = (ar(S) for _ in range(6))
        nmx, asum, arec = ar(AH * TT), ar(AH * TT), ar(AH * TT)
        em, den = ar(TT * BH), ar(TT * BH)
        gq = ar(2)
        tmb = xT2.rearrange("p k s -> p (k s)")[:, 0:1536]
        tmb2 = xT2.rearrange("p k s -> p (k s)")[:, 1536:2048]
        o_all = xn

        block = ctx.enter_context(nc.Block())
        xv = IN["x"][0].rearrange("(t p) d -> p t d", p=P)
        ov = out[0].rearrange("(t p) d -> p t d", p=P)

        @block.sync
        def _(sp):
            sp.dma_start(h[:, :, :], xv).then_inc(sg("x_in"), 16)

            def load(i):
                parts, _, ph = chunks[i]
                s = (ring_in if ph == 0 else ring_in2)[i % NS]
                for part in parts:
                    if part[0] == "deep":
                        src = part[1]
                        sp.dma_start(deep(i, src.shape[1]), src).then_inc(s, 16)
                    else:
                        sp.dma_start(wide(i, part[0], part[1] - part[0]), part[2]).then_inc(s, 16)

            def released(i):
                last = chunks[i][1]
                if last[0] == "down":
                    sp.wait_ge(sg("down_done_" + last[1]), last[2])
                else:
                    see(sp, last)

            for i in range(N_PRE):
                if i >= NS:
                    released(i - NS)
                load(i)

            def load_expert(c, e):
                kind, j = uorder[c % UC]
                ee = e + c // UC
                i = M0 + c
                if kind == "d":
                    src = IN["moe_w_down"][0, bass.ds(ee, 1), j * EJ:(j + 1) * EJ, :]
                    sp.dma_start(deep(i), src.rearrange("a (k p) n -> p (a k) n", p=P)).then_inc(ring_in[i % NS], 16)
                else:
                    src = IN["moe_w_gate" if kind == "g" else "moe_w_up"][0, bass.ds(ee, 1), :, j * EJ:(j + 1) * EJ]
                    sp.dma_start(wide(i), src.rearrange("a (k p) n -> p (a k) n", p=P)).then_inc(ring_in[i % NS], 16)

            for c in range(NS):
                released(N_PRE - NS + c)
                load_expert(c, 0)
            sp.wait_ge(sg("more_ready"), 1)
            more = sp.value_load(more_i[0:1, 0:1], min_val=0, max_val=NPAIR)
            with sp.Fori(0, more + (NPAIR - 1)) as p:
                e = (p % NPAIR) * 2
                for c in range(NS, PC):
                    sp.wait_ge(sg("moe_used"), p * PC + (c - NS + 1))
                    load_expert(c, e)
                e2 = ((p + 1) % NPAIR) * 2
                for c in range(NS):
                    sp.wait_ge(sg("moe_used"), p * PC + (PC + c - NS + 1))
                    load_expert(c, e2)
            for c in range(NS, PC):
                sp.wait_ge(sg("moe_used"), more * PC + ((NPAIR - 1) * PC + c - NS + 1))
                load_expert(c, NE - 2)
            for i in range(N_PRE, len(chunks)):
                if i < N_PRE + NS:
                    sp.wait_ge(sg("moe_used"), more * PC + (NPAIR * PC + i - N_PRE - NS + 1))
                else:
                    released(i - NS)
                load(i)
            for t in range(TT):
                for half in range(2):
                    gone(sp, ("f2", "acc", t, half))
                sp.dma_start(ov[:, t, :], h[:, t, :]).then_inc(sg("out_done"), 16)
            sp.wait_ge(sg("out_done"), 16 * TT)

        @block.gpsimd
        def _(pool):
            G = Order(pool, "pool_order")
            V = nc.gpsimd
            G(V.memset(vrow, 0.0), "vrow_zero")
            G(V.memset(ws[:, :, :, :], 0.0), "ws_zero")
            G(V.memset(ident[:, :], 0.0))
            G(V.affine_select(out=ident[:, :], in_=ident[:, :], compare_op=ALU.not_equal, fill=1.0, base=0,
                              pattern=[[-1, P]], channel_multiplier=1), "const")
            G(V.memset(cst[:, 0:1], EPS))
            G(V.memset(cst[:, 1:2], 1.0))
            G(V.memset(c_half, -0.5), "const")
            for mm in (g["E"],):
                G(V.memset(mm, 0.0))
            G(V.memset(lmask[:, :, :], 0.0))
            for i, mh in enumerate(LEVELS[1:]):
                n = P // (2 * mh)
                v = lmask[:, i, :].rearrange("p (n two m) -> p n two m", two=2, m=mh)[:, :, 1, :]
                G(V.memset(v, 1.0))
                G(V.affine_select(out=v, in_=v, compare_op=ALU.is_ge, fill=0.0, base=0,
                                  pattern=[[-2 * mh, n], [0, mh]], channel_multiplier=1))
                G(V.affine_select(out=v, in_=v, compare_op=ALU.is_ge, fill=0.0, base=mh - 1,
                                  pattern=[[2 * mh, n], [0, mh]], channel_multiplier=-1))
            G(V.memset(g["qt"], 0.0))
            G(V.memset(g["kt"], 0.0), "masks")

            turn_of = [0]

            def rsqrt(n):
                turn_of[0] += 1
                pool.wait_ge(sg("ms_ready"), turn_of[0])
                G(V.tensor_tensor(rstd[:, 0:n], ms[:, 0:n], c_half[:, 0:n], ALU.pow), "rstd_ready")

            def halves(a, mh):
                v = a.rearrange("p (n two m) -> p n two m", two=2, m=mh)
                return v[:, :, 0, :], v[:, :, 1, :]

            def grow(pre, T):
                for i, mh in enumerate(LEVELS[1:]):
                    Al, Ar = halves(T["A"], mh)
                    El, Er = halves(T["E"], mh)
                    pool.wait_ge(sg(pre + "_exp"), 2 * (i + 1))
                    G(V.tensor_tensor(El, El, Ar[:, :, mh - 1:mh].to_broadcast(list(El.shape)), ALU.add))
                    G(V.tensor_tensor(Ar, Ar, Al[:, :, mh - 1:mh].to_broadcast(list(Ar.shape)), ALU.add), pre + "_sums")

            rsqrt(TT)
            G(V.memset(after[:, :], 1.0))
            G(V.affine_select(out=after[:, :], in_=after[:, :], compare_op=ALU.is_ge, fill=0.0, base=-1,
                              pattern=[[-1, P]], channel_multiplier=1))
            G(V.memset(before3[:, :, :], 1.0))
            for i in (0, 2):
                G(V.affine_select(out=before3[:, i, :], in_=before3[:, i, :], compare_op=ALU.is_ge, fill=0.0,
                                  base=-1, pattern=[[1, P]], channel_multiplier=-1))
            G(V.memset(rowneg3[:, :, :], 0.0))
            G(V.memset(colneg3[:, :, :], 0.0))
            for i in (0, 2):
                G(V.affine_select(out=rowneg3[:, i, :], in_=rowneg3[:, i, :], compare_op=ALU.is_ge, fill=NEG,
                                  base=0, pattern=[[-1, P]], channel_multiplier=1))
                G(V.affine_select(out=colneg3[:, i, :], in_=colneg3[:, i, :], compare_op=ALU.is_ge, fill=NEG,
                                  base=0, pattern=[[1, P]], channel_multiplier=-1))
            G(V.memset(pair64[:, :], 0.0))
            G(V.memset(pair64[0:64, 0:64], 1.0))
            G(V.memset(pair64[64:P, 64:P], 1.0))
            G(V.memset(sel[:, :, :], 0.0))
            for b0 in (0, 64):
                G(V.affine_select(out=sel[:, :, :], in_=sel[:, :, :], compare_op=ALU.not_equal, fill=1.0, base=-b0,
                                  pattern=[[-1, AH], [0, P]], channel_multiplier=1))
            G(V.iota(iota[:, :], pattern=[[1, P]], base=0, channel_multiplier=0, allow_small_or_imprecise_dtypes=True))
            G(V.memset(tri8[:, :, :], 1.0))
            G(V.affine_select(out=tri8[:, :, :], in_=tri8[:, :, :], compare_op=ALU.is_ge, fill=0.0, base=-1,
                              pattern=[[1, NE], [-1, NE]], channel_multiplier=0), "masks2")
            pool.wait_ge(sg("gl_A"), 1)
            grow("gl", g)
            rsqrt(GH * TT)
            rsqrt(TT)
            rsqrt(TT)
            rsqrt(TT)
            rsqrt(TT)
            rsqrt(TT)
            pool.wait_ge(sg("xn_ready"), 5 * TT)
            G(V.memset(m["kt"], 0.0))
            G(V.memset(bv[:, :, :, 64:65], 1.0), "mix_zero")
            pool.wait_ge(sg("hl_A"), 1)
            grow("hl", m)
            rsqrt(TT * 16)
            rsqrt(TT)

        @block.scalar
        def _(act):
            A = Order(act, "act_order")
            V = nc.scalar
            act.wait_ge(sg("vrow_zero"), 1)
            nv = 0
            for tile, r0, n, ap in vec_dma:
                act.dma_start(vrow[r0:r0 + n, tile, :], ap).then_inc(sg("vec_in"), 16)
                nv += 1
            for i, nm in enumerate(("a_q_g_2", "a_k_g_2")):
                for half in range(2):
                    act.dma_start(vrow[R_G + i:R_G + i + 1, 0, 64 * half:64 * half + 64], IN[nm]).then_inc(sg("vec_in"), 16)
                    nv += 1
            for i, (c0, n) in enumerate(((C_AF, AH), (C_BI, BH), (C_BF, BH))):
                for half in range(2):
                    act.dma_start(vrow[R_G + 2 + i:R_G + 3 + i, 0, 64 * half:64 * half + n],
                                  IN["b_in_2"][0:1, c0:c0 + n]).then_inc(sg("vec_in"), 16)
                    nv += 1
            assert nv == N_VEC, nv
            act.dma_start(wglr[:, :, :], kpn(w1[:, 2 * GQK + GV:2 * GQK + GV + GR])).then_inc(sg("glr_in"), 16)
            act.dma_start(wgu[:, :], IN["gla_w_gate_up"][0]).then_inc(sg("glr_in"), 16)
            act.dma_start(wrt[:, :, :], kpn(IN["moe_w_router"][0])).then_inc(sg("rt_in"), 16)
            act.wait_ge(sg("ws_zero"), 1)
            for i, (c0, n) in enumerate(((C_AF, AH), (C_BI, BH), (C_BF, BH))):
                for half in range(2):
                    act.dma_start(ws[:, i, :, 64 * half:64 * half + n], kpn(w2[:, c0:c0 + n]),
                                  allow_slow_non_contiguous=True).then_inc(sg("ws_in"), 16)

            def norm(before):
                for t in range(TT):
                    for lab in before(t):
                        gone(act, lab)
                    A(V.activation(xn[:, t, :], h[:, t, :], ACT.Square, accum_out=ssq[:, t:t + 1]), "ssq_ready")

            def exps(pre, T):
                for i, mh in enumerate(LEVELS[1:] + [P]):
                    def half(a, j):
                        return a.rearrange("p (n two m) -> p n two m", two=2, m=mh)[:, :, j, :]
                    if i:
                        act.wait_ge(sg(pre + "_sums"), i)
                        act.wait_ge(sg(pre + "_qk"), 2 * i)
                    A(V.activation(half(T["W"], 1), half(T["A"], 1), ACT.Exp), pre + "_exp")
                    A(V.activation(half(T["W"], 0), half(T["E"], 0), ACT.Exp), pre + "_exp")

            act.wait_ge(sg("x_in"), 16)
            norm(lambda t: [])
            for b in range(2):
                A(V.activation(g["Q"][:, b * 512:(b + 1) * 512], see(act, ("q", b))[:, :], ACT.Copy, scale=GDK ** -0.5),
                  frees=("q", b))
            for b in range(2):
                A(V.activation(g["K"][:, b * 512:(b + 1) * 512], see(act, ("k", b))[:, :], ACT.Copy), frees=("k", b))
            act.wait_ge(sg("gl_abs"), 1)
            A(V.activation(g["W"], g["W"], ACT.Exp, scale=-1.0))
            A(V.activation(g["W"], g["W"], ACT.Ln, bias=c_one), "gl_ln")
            for nm, dst in (("v", gv), ("r", gr)):
                for c in range(2):
                    for t in range(TT):
                        A(V.activation(dst[:, t, c * 512:(c + 1) * 512], see(act, (nm, c, t))[:, :], ACT.Copy),
                          frees=(nm, c, t))
            act.wait_ge(sg("gl_A"), 1)
            act.wait_ge(sg("masks"), 1)
            exps("gl", g)
            A(V.activation(gr[:, :, :], gr[:, :, :], ACT.Silu), "gr_ready")
            for t in range(TT):
                for hp in range(2):
                    o = see(act, ("o", t, hp))
                    for i in range(2):
                        k = t * GH + 2 * hp + i
                        A(V.activation(xn[:, t, (2 * hp + i) * GDV:(2 * hp + i + 1) * GDV], o[:, i * GDV:(i + 1) * GDV],
                                       ACT.Square, accum_out=ssq[:, k:k + 1]), "gssq_ready")
            norm(lambda t: [("wo", 0, t), ("wo", 1, t)])

            def ffn(f, conv):
                for j in range(NJ1):
                    gp = see(act, (f, j, "g"))
                    if conv:
                        up = see(act, (f, j, "u"))
                        if j >= 2:
                            act.wait_ge(sg("act_" + f), j - 1)
                        for i, ps in enumerate((gp, up)):
                            for b in range(2):
                                r = i * (F2 // P) + 2 * j + b
                                A(V.activation(f_cu[:, j % 2, (2 * i + b) * S:(2 * i + b + 1) * S], ps[:, b * S:(b + 1) * S],
                                               ACT.Identity, scale=col("tap2", r), bias=col("conv_b", r)), "conv0")
                        act.wait_ge(sg("conv_done"), j + 1)
                        A(V.activation(f_sg[:, j % 2, :], f_cu[:, j % 2, 0:512], ACT.Silu), "silu_" + f)
                    else:
                        if j >= 2:
                            act.wait_ge(sg("act_" + f), j - 1)
                        A(V.activation(f_sg[:, j % 2, :], gp[:, :], ACT.Silu), frees=(f, j, "g"))

            ffn("f1", False)
            norm(lambda t: [("f1", "acc", t, 0), ("f1", "acc", t, 1)])
            for b in range(4):
                A(V.activation(skT[:, 2 * b:2 * b + 2, :].rearrange("p h s -> p (h s)"), see(act, ("sk", b))[:, :], ACT.Copy),
                  frees=("sk", b))
            for c in range(2):
                for t in range(TT):
                    A(V.activation(sv[:, t, c * 512:(c + 1) * 512], see(act, ("sv", c, t))[:, :], ACT.Copy),
                      frees=("sv", c, t))
            for b in range(4):
                A(V.activation(sqT[:, 2 * b:2 * b + 2, :].rearrange("p h s -> p (h s)"), see(act, ("sq", b))[:, :],
                               ACT.Copy, scale=float(P) ** -0.5), frees=("sq", b))
            for hd in range(SH):
                A(V.activation(sE[:, hd, :], see(act, ("z", hd))[:, 0:384], ACT.Abs), "sb_abs")
            A(V.activation(sE[:, :, :], sE[:, :, :], ACT.Exp, scale=-1.0))
            A(V.activation(sE[:, :, :], sE[:, :, :], ACT.Ln, bias=c_one), "sb_ln")
            for hd in range(SH):
                gone(act, ("stay", hd))
                A(V.activation(sU[:, hd, :], sU[:, hd, :], ACT.Exp), "sb_w")
            norm(lambda t: [("swo", 0, t), ("swo", 1, t)])
            act.wait_ge(sg("rt_max"), 1)
            A(V.activation(ex[:, :, :], ex[:, :, :], ACT.Exp), "rt_exp")
            act.dma_start(fgain, IN["final_norm"].rearrange("(a d) -> a d", a=1).to_broadcast([P, D])).then_inc(sg("fg_in"), 16)
            act.wait_ge(sg("more_ready"), 1)
            more = act.value_load(more_i[0:1, 0:1], min_val=0, max_val=NPAIR)
            with act.Fori(0, more + NPAIR) as p:
                for i in range(2):
                    for j in range(NEJ + 1):
                        if j < NEJ:
                            n = NEJ * i + j
                            act.wait_ge(sg("moe_used"), p * PC + (UC * i + upos["g", j] + 1))
                            act.wait_ge(sg("moe_act"), p * (2 * NEJ) + (n + 1))
                            V.activation(esg[:, n % 2, :], bank[n % 2][:, :], ACT.Silu).then_inc(sg("moe_silu"), 1)
                        if j >= 1:
                            n = NEJ * i + j - 1
                            act.wait_ge(sg("moe_Tfull"), p * (2 * NEJ) + (n + 1))
                            V.activation(eactT[:, n % 2, :], bank[4][:, :], ACT.Copy).then_inc(sg("moe_actT"), 1)
                        if j == 4:
                            act.wait_ge(sg("moe_ohfull"), p * 2 + (i + 1))
                            V.activation(ohT, bank[7][:, 0:S], ACT.Copy).then_inc(sg("moe_ohT"), 1)
                    act.wait_ge(sg("moe_used"), p * PC + UC * (i + 1))
                    V.activation(ey[:, 0:512], bank[5][:, :], ACT.Copy).then_inc(sg("moe_y0"), 1)
            act.wait_ge(sg("moe_h"), more * 8 + (8 * NPAIR + 1))
            norm(lambda t: [])
            act.wait_ge(sg("h_final"), TT)
            norm(lambda t: [])
            nb = 0
            for c0, n, d0 in ((C_AV, AD, 0), (C_BV, BD, 512), (C_BO, BD, 768), (C_CI, 2 * BD, 1024)):
                act.dma_start(tmb[:, d0:d0 + n], IN["b_in_2"][0:1, c0:c0 + n].to_broadcast([P, n])).then_inc(sg("tmb_in"), 16)
                nb += 1
            act.wait_ge(sg("c_pre"), 1)
            A(V.activation(m["Q"], m["Q"], ACT.Silu))
            A(V.activation(m["K"], m["E"], ACT.Sigmoid, scale=-1.0), "c_sig")
            A(V.activation(m["qt"], m["W"], ACT.Exp, scale=-1.0))
            A(V.activation(lbp, lbp, ACT.Exp), "c_lb")
            A(V.activation(m["qt"], m["qt"], ACT.Ln, bias=c_one), "c_ln")
            act.wait_ge(sg("c_ls"), 1)
            A(V.activation(m["W"], m["W"], ACT.Exp), "c_exp")
            act.wait_ge(sg("c_mixd"), 1)
            A(V.activation(m["W"], m["W"], ACT.Ln), "c_ln2")
            act.wait_ge(sg("hl_A"), 1)
            exps("hl", m)
            act.wait_ge(sg("aqk"), 1)
            A(V.activation(rs[:, 0:4 * S], aq.rearrange("p b s -> p (b s)"), ACT.Square))
            A(V.activation(rs[:, 4 * S:8 * S], ak.rearrange("p b s -> p (b s)"), ACT.Square), "qk_sq")
            act.wait_ge(sg("row_abs"), 1)
            A(V.activation(cS[0:72, :], cS[0:72, :], ACT.Exp, scale=-1.0))
            A(V.activation(mS[0:72, :], mS[0:72, :], ACT.Exp, scale=-1.0))
            A(V.activation(cS[0:72, :], cS[0:72, :], ACT.Ln, bias=c_one[0:72, :]))
            A(V.activation(mS[0:72, :], mS[0:72, :], ACT.Ln, bias=c_one[0:72, :]), "row_ln")
            for i in range(4):
                A(V.activation(rs[:, i * 512:(i + 1) * 512], see(act, ("qkss", i))[:, :], ACT.Ln, scale=1.0 / HD, bias=c_eps),
                  frees=("qkss", i))
            A(V.activation(rs, rs, ACT.Exp, scale=-0.5), "qk_rstd")
            act.wait_ge(sg("b_pre"), 1)
            A(V.activation(bc[:, :, :], bc[:, :, :], ACT.Silu), "b_act")
            for hd in range(AH):
                act.wait_ge(sg("s_max"), hd + 1)
                for t in range(TT):
                    sl = sS[:, hd % 2, 0:P] if t == 0 else sS[:, hd % 2, P:3 * P]
                    k = hd * TT + t
                    A(V.activation(sl, sl, ACT.Exp, bias=nmx[:, k:k + 1], accum_out=asum[:, k:k + 1]), "s_exp")
                A(V.activation(pTs[:, hd % 2, :], see(act, ("pT", hd))[:, 0:384], ACT.Copy), frees=("pT", hd))
            mt = see(act, "mT")
            A(V.activation(em.rearrange("p (t h) -> p t h", t=TT),
                           mt[:, 0:TT * P].rearrange("p (t r) -> p t r", t=TT)[:, :, 0:BH], ACT.Exp, scale=-1.0), frees="mT")
            for hd in range(BH):
                act.wait_ge(sg("d_arg"), hd + 1)
                A(V.activation(Dm[:, hd % 2, :], Dm[:, hd % 2, :], ACT.Exp), "d_exp")
            act.wait_ge(sg("o_all"), 1)
            A(V.activation(rs, xn.rearrange("p t d -> p (t d)"), ACT.Square), "o_sq")
            A(V.activation(bog[:, :, :], bog[:, :, :], ACT.Sigmoid))
            A(V.activation(cg[:, :, :], cg[:, :, :], ACT.Silu), "gates")
            norm(lambda t: [("w2", 0, t), ("w2", 1, t)])
            ffn("f2", True)

        @block.vector
        def _(dve):
            C = Order(dve, "dve_order")
            V = nc.vector
            n_norm = [0]

            def norm(n, dsts):
                n_norm[0] += 1
                k = n_norm[0]
                dve.wait_ge(sg("ssq_ready"), TT * k)
                C(V.tensor_scalar(ms[:, 0:TT], ssq[:, 0:TT], 1.0 / D, EPS, ALU.mult, ALU.add), "ms_ready")
                rst[0] += 1
                dve.wait_ge(sg("rstd_ready"), rst[0])
                for t in range(TT):
                    C(V.tensor_scalar(xn[:, t, :], h[:, t, :], rstd[:, t:t + 1], None, ALU.mult), "xn_ready")
                evac(n, dsts)

            rst = [0]

            def tick(name=None, frees=None):
                C(V.tensor_copy(scr[:, :], c_one), name, frees)

            def evac(n, dsts, gain=None):
                for t in range(TT):
                    for half in range(2):
                        ps = see(dve, (n, t, half))[:, :].rearrange("p (k s) -> p k s", k=4)
                        for i, (dst, nm, r0) in enumerate(dsts):
                            gains = cols(nm, r0 + 4 * half, 4) if gain is None else gain(half)
                            ins = V.tensor_tensor(dst[:, 4 * half:4 * half + 4, t * P:(t + 1) * P], ps,
                                                  gains.unsqueeze(2).to_broadcast([P, 4, P]), ALU.mult)
                            if i == len(dsts) - 1:
                                C(ins, frees=(n, t, half))
                            else:
                                C(ins)

            def add_h(nm):
                for c in range(2):
                    for t in range(TT):
                        hs = h[:, t, c * 512:(c + 1) * 512]
                        C(V.tensor_tensor(hs, hs, see(dve, (nm, c, t))[:, :], ALU.add), frees=(nm, c, t))

            def levels(pre, T, cross):
                def half(a, mh, j):
                    return a.rearrange("p (n two m) -> p n two m", two=2, m=mh)[:, :, j, :]

                def qk(i):
                    mh = (LEVELS[1:] + [P])[i]
                    dve.wait_ge(sg(pre + "_exp"), 2 * (i + 1))
                    C(V.tensor_tensor(half(T["qt"], mh, 1), half(T["Q"], mh, 1), half(T["W"], mh, 1), ALU.mult), pre + "_qk")
                    C(V.tensor_tensor(half(T["kt"], mh, 0), half(T["K"], mh, 0), half(T["W"], mh, 0), ALU.mult), pre + "_qk")

                qk(0)
                for i, mh in enumerate(LEVELS):
                    ps = [see(dve, (pre, mh, gg))[:, :].rearrange("p (e s) -> p e s", e=4) for gg in range(2)]
                    if i:
                        qk(i)
                    for gg in range(2):
                        mask = (ident[:, :] if i == 0 else lmask[:, i - 1, :]).unsqueeze(1).to_broadcast([P, 4, P])
                        a4 = T["att"][:, gg, :].rearrange("p (e s) -> p e s", e=4)
                        m4 = T["mt"].rearrange("p (e s) -> p e s", e=4)
                        if i == 0:
                            C(V.tensor_tensor(a4, ps[gg], mask, ALU.mult), frees=(pre, mh, gg))
                        else:
                            C(V.tensor_tensor(m4, ps[gg], mask, ALU.mult), frees=(pre, mh, gg))
                            C(V.tensor_tensor(a4, a4, m4, ALU.add), pre + "_att")
                w = 512 // cross
                for gg in range(cross):
                    C(V.tensor_copy(T["crs"][:, gg * w:(gg + 1) * w], see(dve, (pre, P, gg))[:, 0:w]), frees=(pre, P, gg))

            def bcast(a, shape):
                return a.unsqueeze(len(shape) - 1).to_broadcast(shape)

            dve.wait_ge(sg("const"), 2)
            for i in range(3):
                C(V.tensor_copy(vT[:, i, 0:V_ROWS[i]], see(dve, ("vec", i))[:, 0:V_ROWS[i]]), frees=("vec", i))
            norm("n0", [(xT, "attn_norm", 0)])
            C(V.tensor_copy(glrT, see(dve, "glr")[0:GR, 0:S]), frees="glr")
            dve.wait_ge(sg("masks"), 1)
            for b in range(2):
                C(V.tensor_tensor(g["A"][:, b * 512:(b + 1) * 512].rearrange("p (e s) -> p e s", e=2),
                                  see(dve, ("gate", b))[:, :].rearrange("p (e s) -> p e s", e=2),
                                  bcast(cols("gla_b_gate", 2 * b, 2), [P, 2, S]), ALU.add), frees=("gate", b))
            C(V.scalar_tensor_tensor(g["W"], g["A"], -1.0, g["A"], ALU.mult, ALU.max), "gl_abs")
            dve.wait_ge(sg("gl_ln"), 1)
            C(V.scalar_tensor_tensor(g["A"], g["A"], 0.0, g["W"], ALU.min, ALU.subtract))
            C(V.tensor_scalar(g["A"], g["A"], 1.0 / GATE_NORM, None, ALU.mult), "gl_A")
            for lab in (("q", 0), ("q", 1), ("k", 0), ("k", 1)):
                gone(dve, lab)
            levels("gl", g, 1)
            dve.wait_ge(sg("gssq_ready"), GH * TT)
            C(V.tensor_scalar(ms[:, 0:GH * TT], ssq[:, 0:GH * TT], 1.0 / GDV, EPS, ALU.mult, ALU.add), "ms_ready")
            rst[0] += 1
            dve.wait_ge(sg("rstd_ready"), rst[0])
            for t in range(TT):
                for hp in range(2):
                    o = see(dve, ("o", t, hp))
                    for i in range(2):
                        hd = 2 * hp + i
                        cs = slice(hd * GDV, (hd + 1) * GDV)
                        ins = V.scalar_tensor_tensor(xn[:, t, cs], o[:, i * GDV:(i + 1) * GDV], rstd[:, t * GH + hd:t * GH + hd + 1],
                                                     gr[:, t, cs], ALU.mult, ALU.mult)
                        if i == 1:
                            C(ins, frees=("o", t, hp))
                        else:
                            C(ins)
            evac("y", [(xT, "gla_head_norm", 0)],
                 lambda half: cols("gla_head_norm", 0, 4))
            add_h("wo")
            norm("n1", [(xT, "ffn_norm", 0)])

            def ffn(f, conv):
                for j in range(NJ1):
                    if conv:
                        gp, up = see(dve, (f, j, "g")), see(dve, (f, j, "u"))
                        dve.wait_ge(sg("conv0"), 4 * (j + 1))
                        for i, ps in enumerate((gp, up)):
                            for b in range(2):
                                r = i * (F2 // P) + 2 * j + b
                                cu = f_cu[:, j % 2, (2 * i + b) * S:(2 * i + b + 1) * S]
                                x = ps[:, b * S:(b + 1) * S]
                                C(V.scalar_tensor_tensor(cu[:, 1:S], x[:, 0:S - 1], col("tap01", NF2 + r), cu[:, 1:S],
                                                         ALU.mult, ALU.add))
                                ins = V.scalar_tensor_tensor(cu[:, 2:S], x[:, 0:S - 2], col("tap01", r), cu[:, 2:S],
                                                             ALU.mult, ALU.add)
                                if b == 1:
                                    C(ins, frees=(f, j, "gu"[i]))
                                else:
                                    C(ins)
                        tick("conv_done")
                        dve.wait_ge(sg("silu_" + f), j + 1)
                        lhs, rhs = f_sg[:, j % 2, :], f_cu[:, j % 2, 512:1024]
                    else:
                        gone(dve, (f, j, "g"))
                        lhs, rhs = f_sg[:, j % 2, :], see(dve, (f, j, "u"))[:, :]
                    if j >= 2:
                        dve.wait_ge(sg("down_done_" + f), j - 1)
                    ins = V.tensor_tensor(f_act[:, j % 2, :], lhs, rhs, ALU.mult)
                    C(ins, "act_" + f)
                    if not conv:
                        tick(frees=(f, j, "u"))
                for t in range(TT):
                    for half in range(2):
                        hs = h[:, t, half * 512:(half + 1) * 512]
                        C(V.tensor_tensor(hs, hs, see(dve, (f, "acc", t, half))[:, :], ALU.add), frees=(f, "acc", t, half))

            ffn("f1", False)
            norm("n2", [(xT2, "kv_norm", 0), (xT, "attn_norm", KD)])
            dve.wait_ge(sg("masks2"), 1)
            for hd in range(SH):
                z = see(dve, ("z", hd))[:, 0:384]
                dve.wait_ge(sg("sb_abs"), hd + 1)
                C(V.tensor_scalar(sT[:, hd, :], z, 0.0, None, ALU.max))
                C(V.tensor_scalar(sU[:, hd, :], z, 0.0, None, ALU.min), frees=("z", hd))
            dve.wait_ge(sg("sb_ln"), 1)
            C(V.tensor_tensor(sT[:, :, :], sT[:, :, :], sE[:, :, :], ALU.add))
            C(V.tensor_tensor(sT[:, :, :], sT[:, :, :],
                              before3.rearrange("p a s -> p (a s)").unsqueeze(1).to_broadcast([P, SH, 384]), ALU.mult), "sb_keep")
            C(V.tensor_tensor(sU[:, :, :], sU[:, :, :], sE[:, :, :], ALU.subtract))
            for hd in range(SH):
                C(V.tensor_tensor(sU[:, hd, :], sU[:, hd, :], see(dve, ("stay", hd))[:, 0:384], ALU.subtract),
                  frees=("stay", hd))
            for hd in range(SH):
                dve.wait_ge(sg("sb_w"), hd + 1)
                C(V.tensor_tensor(sU[:, hd, :], sU[:, hd, :], before3.rearrange("p a s -> p (a s)"), ALU.mult), "sb_wm")
            for hp in range(SH // 2):
                C(V.tensor_copy(xT[:, 2 * hp:2 * hp + 2, :].rearrange("p k s -> p (k s)"), see(dve, ("so", hp))[:, :]),
                  frees=("so", hp))
            add_h("swo")
            norm("n3", [(xT, "ffn_norm", KD)])
            C(V.tensor_copy(lg, see(dve, "lg")[:, 0:TT * NE].rearrange("p (t e) -> p t e", t=TT)), frees="lg")
            for t in range(TT):
                le = lg[:, t, :].unsqueeze(2).to_broadcast([P, NE, NE])
                lj = lg[:, t, :].unsqueeze(1).to_broadcast([P, NE, NE])
                C(V.tensor_tensor(cmp1[:, t], lj, le, ALU.is_gt))
                C(V.tensor_tensor(cmp2[:, t], lj, le, ALU.is_equal))
                C(V.tensor_tensor(cmp2[:, t], cmp2[:, t], tri8[:, :, :], ALU.mult))
                C(V.tensor_tensor(cmp1[:, t], cmp1[:, t], cmp2[:, t], ALU.add))
                C(V.tensor_reduce(rank[:, t, :], cmp1[:, t], AX.X, ALU.add))
            C(V.tensor_scalar(selx, rank, 1.5, None, ALU.is_lt), "rt_sel")
            C(V.tensor_reduce(mx, lg, AX.X, ALU.max))
            C(V.tensor_tensor(ex, lg, bcast(mx, [P, TT, NE]), ALU.subtract), "rt_max")
            dve.wait_ge(sg("rt_exp"), 1)
            C(V.tensor_tensor(ex, ex, selx, ALU.mult))
            C(V.tensor_reduce(exs, ex, AX.X, ALU.add))
            C(V.reciprocal(exs, exs))
            C(V.memset(pm, -1.0))
            C(V.memset(gt, 0.0))
            for t in range(TT):
                for r in range(2):
                    C(V.tensor_scalar(gt[:, r * NE:(r + 1) * NE, t], ex[:, t, :], exs[:, t:t + 1], None, ALU.mult))
            pp = see(dve, "pos")[:, 0:TT * NE].rearrange("p (t e) -> p t e", t=TT)
            C(V.scalar_tensor_tensor(lg, pp, 1.0, selx, ALU.add, ALU.mult), frees="pos")
            for t in range(TT):
                for r in range(2):
                    C(V.tensor_scalar(pm[:, r * NE:(r + 1) * NE, t], lg[:, t, :], -1.0 - P * r, None, ALU.add))
            C(V.tensor_reduce(cmax[0:1, 0:1], see(dve, "cnt")[0:1, 0:NE], AX.X, ALU.max), frees="cnt")
            C(V.tensor_scalar(cmax[0:1, 1:2], cmax[0:1, 0:1], P + 0.5, float(NPAIR), ALU.is_gt, ALU.mult))
            C(V.tensor_copy(more_i[0:1, 0:1], cmax[0:1, 1:2]), "more_ready")

            more = dve.value_load(more_i[0:1, 0:1], min_val=0, max_val=NPAIR)
            iota2 = iota[:, :].unsqueeze(1).to_broadcast([P, TT, P])

            def onehot(u, order):
                pmu = pm[:, bass.ds(u, 1), :].rearrange("p a t -> p (a t)")
                gtu = gt[:, bass.ds(u, 1), :].rearrange("p a t -> p (a t)")
                order(V.tensor_tensor(oh, iota2, pmu.unsqueeze(2).to_broadcast([P, TT, P]), ALU.is_equal), 0)
                order(V.tensor_tensor(ohg, oh, gtu.unsqueeze(2).to_broadcast([P, TT, P]), ALU.mult), 1)

            def first(ins, k):
                ins.then_inc(sg("moe_oh"), 1)
                dve.wait_ge(sg("moe_oh"), k + 1)

            onehot(0, first)

            def gather_out(value):
                for half in range(2):
                    dve.wait_ge(sg("moe_xgfull"), value + half)
                    b = bank[7] if half == 0 else bank[gb[0]]
                    V.tensor_tensor(xg[:, 4 * half:4 * half + 4, :], b[:, :].rearrange("p (k s) -> p k s", k=4),
                                    cols("ffn_norm", KD + 4 * half, 4).unsqueeze(2).to_broadcast([P, 4, P]),
                                    ALU.mult).then_inc(sg("moe_xg"), 1)

            gb = [0]
            gather_out(1)
            tick("moe_act")
            tick("moe_act")
            tick("moe_h")
            with dve.Fori(0, more + NPAIR) as p:
                for i in range(2):
                    for j in range(NEJ):
                        n = NEJ * i + j
                        dve.wait_ge(sg("moe_used"), p * PC + (UC * i + upos["u", j] + 1))
                        dve.wait_ge(sg("moe_silu"), p * (2 * NEJ) + (n + 1))
                        V.tensor_tensor(eact[:, n % 2, :], esg[:, n % 2, :], bank[2 + n % 2][:, :],
                                        ALU.mult).then_inc(sg("moe_act"), 1)
                        if j == 4:
                            dve.wait_ge(sg("moe_ohfull"), p * 2 + (i + 1))

                            def nxt(ins, k):
                                ins.then_inc(sg("moe_oh"), 1)
                                dve.wait_ge(sg("moe_oh"), p * 4 + (2 * i + k + 3))

                            onehot(p * 2 + (i + 1), nxt)
                    gb[0] = (NEJ * (i + 1)) % 2
                    gather_out(p * 4 + (2 * i + 3))
                    dve.wait_ge(sg("moe_used"), p * PC + UC * (i + 1))
                    V.tensor_copy(ey[:, 512:1024], bank[6][:, :]).then_inc(sg("moe_y1"), 1)
                    for q in range(4):
                        t, half = q // 2, q % 2
                        dve.wait_ge(sg("moe_scfull"), p * 8 + (4 * i + q + 1))
                        hs = h[:, t, half * 512:(half + 1) * 512]
                        V.tensor_tensor(hs, hs, bank[7 if q % 2 == 0 else 4][:, :], ALU.add).then_inc(sg("moe_h"), 1)
            dve.wait_ge(sg("moe_h"), more * 8 + (8 * NPAIR + 1))
            n_norm[0] += 1
            dve.wait_ge(sg("ssq_ready"), TT * n_norm[0])
            C(V.tensor_scalar(ms[:, 0:TT], ssq[:, 0:TT], 1.0 / D, EPS, ALU.mult, ALU.add), "ms_ready")
            rst[0] += 1
            dve.wait_ge(sg("rstd_ready"), rst[0])
            dve.wait_ge(sg("fg_in"), 16)
            for t in range(TT):
                C(V.scalar_tensor_tensor(h[:, t, :], h[:, t, :], rstd[:, t:t + 1], fgain, ALU.mult, ALU.mult), "h_final")
            norm("n4", [(xT, "norm_mix_g_2", 0)])
            dve.wait_ge(sg("mix_zero"), 1)

            def fm_bias(dst, lab, nm, r0):
                C(V.tensor_tensor(dst, see(dve, lab)[:, :].rearrange("p (e s) -> p e s", e=2),
                                  bcast(cols(nm, r0, 2), [P, 2, S]), ALU.add), frees=lab)

            q3 = m["Q"].rearrange("p (e s) -> p e s", e=2)
            f3 = m["E"].rearrange("p (e s) -> p e s", e=2)
            fm_bias(q3, ("cqf", 0), "cqf_b", 0)
            fm_bias(f3, ("cqf", 1), "cqf_b", 2)
            lbl = cols("lb_logits_2", 0, 2)
            C(V.tensor_tensor(lbp, lbl, lbl, ALU.subtract))
            C(V.scalar_tensor_tensor(m["W"], m["E"], -1.0, m["E"], ALU.mult, ALU.max), "c_pre")
            dve.wait_ge(sg("c_lb"), 1)
            C(V.reciprocal(lb1, lbp))
            C(V.tensor_tensor(lbp, lbp, lb1, ALU.mult))
            C(V.tensor_tensor(lbp, lbp, lbp, ALU.subtract))
            C(V.tensor_scalar(lbp, lbp, 0.0, None, ALU.max))
            C(V.tensor_scalar(lb1, lbp, -1.0, 1.0, ALU.mult, ALU.add))
            dve.wait_ge(sg("c_ln"), 1)
            C(V.scalar_tensor_tensor(m["A"], m["E"], 0.0, m["qt"], ALU.min, ALU.subtract))
            C(V.tensor_scalar(m["W"], m["A"], -1.0, 80.0, ALU.mult, ALU.min), "c_ls")
            dve.wait_ge(sg("c_exp"), 1)
            for b in range(2):
                bs = slice(b * S, (b + 1) * S)
                C(V.tensor_scalar(m["W"][:, bs], m["W"][:, bs], lbp[:, b:b + 1], lb1[:, b:b + 1], ALU.mult, ALU.add))
                C(V.tensor_scalar(m["K"][:, bs], m["K"][:, bs], lb1[:, b:b + 1], None, ALU.mult))
            tick("c_mixd")
            dve.wait_ge(sg("c_ln2"), 1)
            C(V.tensor_tensor(m["A"], m["A"], m["W"], ALU.add))
            C(V.memset(m["E"], 0.0))
            C(V.memset(m["qt"], 0.0), "hl_A")
            dve.wait_ge(sg("tmb_in"), 64)
            for t in range(TT):
                ps = see(dve, ("cig", t))
                C(V.tensor_tensor(ci[:, t, :], ps[:, 0:BD], tmb[:, 1024:1024 + BD], ALU.add), "ci")
                C(V.tensor_tensor(cg[:, t, :], ps[:, BD:2 * BD], tmb[:, 1280:1280 + BD], ALU.add), frees=("cig", t))
            levels("hl", m, 2)
            for t in range(TT):
                C(V.tensor_copy(o_all[:, t, AD + BD:AD + 2 * BD], see(dve, ("co", t))[:, 0:BD]), frees=("co", t))
            for dst, nm in ((aq, "aq"), (ak, "ak")):
                for b in range(2):
                    fm_bias(dst[:, 2 * b:2 * b + 2, :], (nm, b), nm + "_b", 2 * b)
            C(V.tensor_copy(gq[:, 1:2], vT[:, 0, R_G + 1:R_G + 2]))
            C(V.tensor_scalar(gq[:, 0:1], vT[:, 0, R_G:R_G + 1], HD ** -0.5, None, ALU.mult), "aqk")
            for t in range(TT):
                C(V.tensor_tensor(av[:, t, :], see(dve, ("av", t))[:, :], tmb[:, 0:AD], ALU.add), frees=("av", t))
            for b in range(2):
                fm_bias(bz[:, 2 * b:2 * b + 2, :], ("bqk", b), "bqk_b", 2 * b)
            for t in range(TT):
                ps = see(dve, ("bvo", t))
                C(V.tensor_tensor(bv[:, t, :, 0:HD], ps[:, 0:BD].rearrange("p (h n) -> p h n", h=BH),
                                  tmb[:, 512:512 + BD].rearrange("p (h n) -> p h n", h=BH), ALU.add), "bv")
                C(V.tensor_tensor(bog[:, t, :], ps[:, BD:2 * BD], tmb[:, 768:768 + BD], ALU.add), frees=("bvo", t))
            rw = slice(0, 72)
            for a in (cS, ncS, iF, nM, mS):
                C(V.memset(a, 0.0))
            for nm, dst, i in (("cf", ncS, 0), ("bi", iF, 1), ("bf", nM, 2)):
                C(V.tensor_scalar(dst[rw, :], see(dve, nm)[rw, 0:S], vT[rw, 0, R_G + 2 + i:R_G + 3 + i], None, ALU.add), frees=nm)
            C(V.scalar_tensor_tensor(cS[rw, :], ncS[rw, :], -1.0, ncS[rw, :], ALU.mult, ALU.max))
            C(V.scalar_tensor_tensor(mS[rw, :], nM[rw, :], -1.0, nM[rw, :], ALU.mult, ALU.max), "row_abs")
            for b in range(4):
                C(V.tensor_scalar(bc[:, b, :], bz[:, b, :], col("b_conv", 12 + b), None, ALU.mult))
                for k in range(1, 4):
                    C(V.scalar_tensor_tensor(bc[:, b, k:S], bz[:, b, 0:S - k], col("b_conv", 4 * (3 - k) + b), bc[:, b, k:S],
                                             ALU.mult, ALU.add))
            tick("b_pre")
            dve.wait_ge(sg("row_ln"), 1)
            C(V.scalar_tensor_tensor(cS[rw, :], ncS[rw, :], 0.0, cS[rw, :], ALU.min, ALU.subtract))
            C(V.scalar_tensor_tensor(mS[rw, :], nM[rw, :], 0.0, mS[rw, :], ALU.min, ALU.subtract))
            C(V.memset(row1, 1.0))
            C(V.tensor_tensor_scan(ncS[rw, :], row1[rw, :], cS[rw, :], 0.0, ALU.mult, ALU.add))
            C(V.tensor_tensor_scan(nM[rw, :], row1[rw, :], mS[rw, :], 0.0, ALU.mult, ALU.add))
            C(V.tensor_copy(cS[rw, :], ncS[rw, :]))
            C(V.tensor_scalar(ncS[rw, :], ncS[rw, :], -1.0, None, ALU.mult), "c_rows")
            C(V.tensor_tensor(iF[rw, :], iF[rw, :], nM[rw, :], ALU.subtract))
            C(V.tensor_tensor_scan(row1[rw, :], iF[rw, :], iF[rw, :], -3.0e38, ALU.max, ALU.max))
            C(V.tensor_tensor(mS[rw, :], nM[rw, :], row1[rw, :], ALU.add))
            C(V.tensor_scalar(nM[rw, :], row1[rw, :], -1.0, None, ALU.mult), "m_rows")
            dve.wait_ge(sg("qk_rstd"), 1)
            for dst, i in ((aq, 0), (ak, 1)):
                d2 = dst.rearrange("p b s -> p (b s)")
                C(V.scalar_tensor_tensor(d2, d2, gq[:, i:i + 1], rs[:, i * 4 * S:(i + 1) * 4 * S], ALU.mult, ALU.mult), "qk_n")
            r3 = rowneg3.rearrange("p a s -> p (a s)")

            for hd in range(AH):
                if hd >= 2:
                    see(dve, ("pT", hd - 2))
                C(V.tensor_tensor(sS[:, hd % 2, :], see(dve, ("s", hd))[:, 0:384], r3, ALU.add), frees=("s", hd))
                C(V.tensor_reduce(nmx[:, hd * TT:hd * TT + 1], sS[:, hd % 2, 0:P], AX.X, ALU.max, negate=True))
                C(V.tensor_reduce(nmx[:, hd * TT + 1:hd * TT + 2], sS[:, hd % 2, P:3 * P], AX.X, ALU.max, negate=True), "s_max")
            dve.wait_ge(sg("s_exp"), AH * TT)
            C(V.reciprocal(arec, asum))
            for t in range(TT):
                C(V.tensor_tensor(o_all[:, t, 0:AD].rearrange("p (h n) -> p h n", h=AH),
                                  see(dve, ("ao", t))[:, :].rearrange("p (h n) -> p h n", h=AH),
                                  bcast(arec.rearrange("p (h t) -> p h t", t=TT)[:, :, t], [P, AH, HD]), ALU.mult), frees=("ao", t))
            c3 = colneg3.rearrange("p a s -> p (a s)")
            for hd in range(BH):
                C(V.tensor_tensor(Dm[:, hd % 2, :], see(dve, ("P2", hd))[:, 0:384], c3, ALU.add), "d_arg")
                p1 = see(dve, ("P1", hd))[:, 0:384]
                dve.wait_ge(sg("d_exp"), hd + 1)
                if hd >= 2:
                    dve.wait_ge(sg("b_pv"), hd - 1)
                C(V.scalar_tensor_tensor(sS[:, hd % 2, :], p1, HD ** -0.5, Dm[:, hd % 2, :], ALU.mult, ALU.mult), "d_w")
                tick(frees=("P2", hd))
                tick(frees=("P1", hd))
            gone(dve, "mT")
            for t in range(TT):
                ps = see(dve, ("bo", t))[:, 0:BH * 65].rearrange("p (h n) -> p h n", h=BH)
                dn = den[:, t * BH:(t + 1) * BH]
                C(V.tensor_copy(dn, ps[:, :, HD]))
                C(V.scalar_tensor_tensor(dn, dn, -1.0, dn, ALU.mult, ALU.max))
                C(V.tensor_tensor(dn, dn, em[:, t * BH:(t + 1) * BH], ALU.max))
                C(V.reciprocal(dn, dn))
                C(V.tensor_tensor(o_all[:, t, AD:AD + BD].rearrange("p (h n) -> p h n", h=BH), ps[:, :, 0:HD],
                                  bcast(dn, [P, BH, HD]), ALU.mult), frees=("bo", t))
            tick("o_all")
            dve.wait_ge(sg("o_sq"), 1)
            C(V.tensor_reduce(ssq[:, 0:32], rs.rearrange("p (g n) -> p g n", n=HD), AX.X, ALU.add))
            C(V.tensor_scalar(ms[:, 0:32], ssq[:, 0:32], 1.0 / HD, EPS, ALU.mult, ALU.add), "ms_ready")
            rst[0] += 1
            dve.wait_ge(sg("rstd_ready"), rst[0])
            o3 = o_all.rearrange("p t (g n) -> p (t g) n", n=HD)
            C(V.tensor_tensor(o3, o3, bcast(rstd[:, 0:32], [P, 32, HD]), ALU.mult))
            dve.wait_ge(sg("gates"), 1)
            C(V.tensor_tensor(o_all[:, :, AD:AD + BD], o_all[:, :, AD:AD + BD], bog, ALU.mult))
            C(V.tensor_tensor(o_all[:, :, AD + BD:AD + 2 * BD], o_all[:, :, AD + BD:AD + 2 * BD], cg, ALU.mult), "o_done")
            evac("yy", [(xT, "out_g_2", 0)])
            add_h("w2")
            norm("n5", [(xT, "norm_ffn_g_2", 0)])
            ffn("f2", True)

        @block.tensor
        def _(pe):
            T = nc.tensor

            def take(label):
                b, n = turns[label]
                if n:
                    pe.wait_ge(freed[b], n)
                return bank[b]

            def done(ins, label):
                ins.then_inc(full[turns[label][0]], 1)

            n_xn, n_xT = [0], [0]

            def transposes(n):
                for t in range(TT):
                    for half in range(2):
                        ps = take((n, t, half))
                        for k in range(4):
                            kk = 4 * half + k
                            ins = T.transpose(ps[:, k * P:(k + 1) * P], xn[:, t, kk * P:(kk + 1) * P], ident[:, :])
                        done(ins, (n, t, half))
                for t in range(TT):
                    for half in range(2):
                        gone(pe, (n, t, half))

            def norm(n):
                n_xn[0] += TT
                pe.wait_ge(sg("xn_ready"), n_xn[0])
                transposes(n)

            def fm(label, i, c0, x=None):
                x = xT if x is None else x
                ps = take(label)
                w = wide(i)
                for j in range(2):
                    for k in range(KD):
                        ins = T.matmul(ps[:, j * S:(j + 1) * S], w[:, k, c0 + j * P:c0 + (j + 1) * P], x[:, k, :],
                                       start=(k == 0), stop=(k == KD - 1))
                done(ins, label)

            def tm(label, i, t, x=None):
                x = xT if x is None else x
                ps = take(label)
                w = wide(i)
                for k in range(KD):
                    ins = T.matmul(ps[:, :], x[:, k, t * P:(t + 1) * P], w[:, k, :], start=(k == 0), stop=(k == KD - 1))
                done(ins, label)

            def out_proj(nm, keys):
                for c in range(2):
                    i = arrived(pe, keys[c])
                    for t in range(TT):
                        tm((nm, c, t), i, t)

            def levels(pre, T_, heads):
                ent = [[(h_, st) for h_ in range(4)] for st in range(2)] if heads else \
                      [[(2 * b + hf, st) for st in range(2) for b in range(2)] for hf in range(2)]

                def operands(hd, lo, hi, level):
                    rws = slice(0, P) if heads else slice(64 * (hd % 2), 64 * (hd % 2) + 64)
                    o = (hd if heads else hd // 2) * S
                    kk, qq = (T_["K"], T_["Q"]) if level == 0 else (T_["kt"], T_["qt"])
                    return kk[rws, o + lo * P:o + (lo + 1) * P], qq[rws, o + hi * P:o + (hi + 1) * P]

                for i, mh in enumerate(LEVELS):
                    if i:
                        pe.wait_ge(sg(pre + "_qk"), 2 * i)
                    for gg in range(2):
                        ps = take((pre, mh, gg))
                        for e, (hd, st) in enumerate(ent[gg]):
                            kk, qq = operands(hd, st, st, i)
                            ins = T.matmul(ps[:, e * P:(e + 1) * P], kk, qq, start=True, stop=True)
                        done(ins, (pre, mh, gg))
                pe.wait_ge(sg(pre + "_qk"), 2 * len(LEVELS))
                for gg in range(1 if heads else 2):
                    ps = take((pre, P, gg))
                    hds = range(4) if heads else [2 * b + gg for b in range(2)]
                    for e, hd in enumerate(hds):
                        kk, qq = operands(hd, 0, 1, 1)
                        ins = T.matmul(ps[:, e * P:(e + 1) * P], kk, qq, start=True, stop=True)
                    done(ins, (pre, P, gg))
                pe.wait_ge(sg(pre + "_att"), 2 * (len(LEVELS) - 1))
                for gg in range(1 if heads else 2):
                    gone(pe, (pre, P, gg))

            pe.wait_ge(sg("const"), 1)
            pe.wait_ge(sg("vec_in"), 16 * N_VEC)
            for i in range(3):
                n = V_ROWS[i]
                done(T.transpose(take(("vec", i))[:, 0:n], vrow[0:n, i, :], ident[0:n, 0:n]), ("vec", i))
            norm("n0")
            pe.wait_ge(sg("glr_in"), 32)
            ps = take("glr")
            for k in range(KD):
                ins = T.matmul(ps[0:GR, 0:S], wglr[:, k, :], xT[:, k, :], start=(k == 0), stop=(k == KD - 1))
            done(ins, "glr")
            gone(pe, "glr")
            for b in range(2):
                ps = take(("gate", b))
                for j in range(2):
                    hd = 2 * b + j
                    ins = T.matmul(ps[:, j * S:(j + 1) * S], wgu[:, hd * P:(hd + 1) * P], glrT, start=True, stop=True)
                done(ins, ("gate", b))
            for nm in ("q", "k"):
                i = arrived(pe, nm)
                for b in range(2):
                    fm((nm, b), i, b * 2 * P)
            for nm in "vr":
                for c in range(2):
                    i = arrived(pe, f"{nm}{c}")
                    for t in range(TT):
                        tm((nm, c, t), i, t)
            for lab in (("q", 0), ("q", 1), ("k", 0), ("k", 1)):
                gone(pe, lab)
            levels("gl", g, True)
            for c in range(2):
                for t in range(TT):
                    gone(pe, ("v", c, t))
            for t in range(TT):
                for hp in range(2):
                    ps = take(("o", t, hp))
                    for i in range(2):
                        hd = 2 * hp + i
                        cs = slice(hd * GDV, (hd + 1) * GDV)
                        o = ps[:, i * GDV:(i + 1) * GDV]
                        if t:
                            T.matmul(o, g["crs"][:, hd * P:(hd + 1) * P], gv[:, 0, cs], start=True, stop=False)
                        ins = T.matmul(o, g["att"][:, t, hd * P:(hd + 1) * P], gv[:, t, cs], start=(t == 0), stop=True)
                    done(ins, ("o", t, hp))
            for t in range(TT):
                for hp in range(2):
                    gone(pe, ("o", t, hp))
            transposes("y")
            out_proj("wo", [("wo", 0), ("wo", 1)])
            norm("n1")

            def ffn(f):
                def down(j):
                    pe.wait_ge(sg("act_" + f), j + 1)
                    i = arrived(pe, (f, "d", j - j % 2))
                    w = deep(i)
                    for t in range(TT):
                        for half in range(2):
                            lab = (f, "acc", t, half)
                            ps = take(lab) if j == 0 else bank[turns[lab][0]]
                            for b in range(2):
                                last = j == NJ1 - 1 and b == 1
                                ins = T.matmul(ps[:, :], f_act[:, j % 2, b * S + t * P:b * S + (t + 1) * P],
                                               w[:, 2 * (j % 2) + b, half * 512:(half + 1) * 512],
                                               start=(j == 0 and b == 0), stop=last)
                            if j == NJ1 - 1:
                                done(ins, lab)
                    if j < NJ1 - 1:
                        ins.then_inc(sg("down_done_" + f), 1)

                for j in range(NJ1):
                    i = arrived(pe, (f, "gu", j))
                    fm((f, j, "g"), i, 0)
                    fm((f, j, "u"), i, FJ)
                    if j:
                        down(j - 1)
                down(NJ1 - 1)

            ffn("f1")
            norm("n2")
            for b in range(4):
                fm(("sk", b), arrived(pe, f"sk{b // 2}"), (b % 2) * 2 * P, xT2)
            for c in range(2):
                for t in range(TT):
                    tm(("sv", c, t), arrived(pe, f"sv{c}"), t, xT2)
            for b in range(4):
                fm(("sq", b), arrived(pe, f"sq{b // 2}"), (b % 2) * 2 * P)
            for b in range(4):
                gone(pe, ("sk", b))
                gone(pe, ("sq", b))
            for hd in range(SH):
                ps = take(("z", hd))
                T.matmul(ps[:, 0:S], skT[:, hd, 0:P], sqT[:, hd, :], start=True, stop=True)
                done(T.matmul(ps[:, S:384], skT[:, hd, P:S], sqT[:, hd, P:S], start=True, stop=True), ("z", hd))
            pe.wait_ge(sg("sb_keep"), 1)
            pe.wait_ge(sg("masks2"), 1)
            for hd in range(SH):
                ps = take(("stay", hd))
                T.matmul(ps[:, 0:P], after[:, :], sT[:, hd, 0:P], start=True, stop=True)
                T.matmul(ps[:, P:S], after[:, :], sT[:, hd, P:S], start=True, stop=False)
                T.matmul(ps[:, P:S], before3[:, 1, :], sT[:, hd, S:384], start=False, stop=True)
                done(T.matmul(ps[:, S:384], after[:, :], sT[:, hd, S:384], start=True, stop=True), ("stay", hd))
            for c in range(2):
                for t in range(TT):
                    gone(pe, ("sv", c, t))
            for hp in range(SH // 2):
                ps = take(("so", hp))
                for i in range(2):
                    hd = 2 * hp + i
                    pe.wait_ge(sg("sb_wm"), hd + 1)
                    vs = slice(hd * P, (hd + 1) * P)
                    T.matmul(ps[:, i * S:i * S + P], sv[:, 0, vs], sU[:, hd, 0:P], start=True, stop=True)
                    T.matmul(ps[:, i * S + P:(i + 1) * S], sv[:, 0, vs], sU[:, hd, P:S], start=True, stop=False)
                    ins = T.matmul(ps[:, i * S + P:(i + 1) * S], sv[:, 1, vs], sU[:, hd, S:384], start=False, stop=True)
                done(ins, ("so", hp))
            for hp in range(SH // 2):
                gone(pe, ("so", hp))
            out_proj("swo", ["so0", "so1"])
            norm("n3")
            pe.wait_ge(sg("rt_in"), 16)
            ps = take("lg")
            for t in range(TT):
                for k in range(KD):
                    ins = T.matmul(ps[:, t * NE:(t + 1) * NE], xT[:, k, t * P:(t + 1) * P], wrt[:, k, :],
                                   start=(k == 0), stop=(k == KD - 1))
            done(ins, "lg")
            pe.wait_ge(sg("rt_sel"), 1)
            ps = take("pos")
            T.matmul(ps[:, 0:NE], before3[:, 0, :], selx[:, 0, :], start=True, stop=True)
            T.matmul(ps[:, NE:2 * NE], before3[:, 1, :], selx[:, 0, :], start=True, stop=False)
            done(T.matmul(ps[:, NE:2 * NE], before3[:, 0, :], selx[:, 1, :], start=False, stop=True), "pos")
            ps = take("cnt")
            T.matmul(ps[:, 0:NE], before3[:, 1, :], selx[:, 0, :], start=True, stop=False)
            done(T.matmul(ps[:, 0:NE], before3[:, 1, :], selx[:, 1, :], start=False, stop=True), "cnt")

            for b in range(8):
                pe.wait_ge(freed[b], uses_before_moe[b])
            pe.wait_ge(sg("more_ready"), 1)
            more = pe.value_load(more_i[0:1, 0:1], min_val=0, max_val=NPAIR)

            def gather(half, b):
                for k in range(4):
                    kk = 4 * half + k
                    for t in range(TT):
                        ins = T.matmul(b[:, k * P:(k + 1) * P], xn[:, t, kk * P:(kk + 1) * P], oh[:, t, :],
                                       start=(t == 0), stop=(t == TT - 1))
                ins.then_inc(sg("moe_xgfull"), 1)

            pe.wait_ge(sg("moe_oh"), 1)
            gather(0, bank[7])
            gather(1, bank[0])
            moe_base = filled[0]
            with pe.Fori(0, more + NPAIR) as p:
                def used(ins):
                    ins.then_inc(sg("moe_used"), 1)

                def here(i, c):
                    cc = UC * i + c
                    s = (M0 + cc) % NS
                    pe.wait_ge(ring_in[s], p * (16 * (PC // NS)) + (moe_base[s] + 16 * (cc // NS + 1)))
                    return M0 + cc

                for i in range(2):
                    pe.wait_ge(sg("moe_xg"), p * 4 + (2 * i + 2))
                    for j in range(NEJ + 1):
                        if j < NEJ:
                            n = NEJ * i + j
                            w = wide(here(i, upos["g", j]))
                            pe.wait_ge(sg("moe_act"), p * (2 * NEJ) + (n + 1))
                            for k in range(KD):
                                ins = T.matmul(bank[n % 2][:, :], xg[:, k, :], w[:, k, :], start=(k == 0), stop=(k == KD - 1))
                            used(ins)
                            w = wide(here(i, upos["u", j]))
                            for k in range(KD):
                                ins = T.matmul(bank[2 + n % 2][:, :], xg[:, k, :], w[:, k, :], start=(k == 0), stop=(k == KD - 1))
                            used(ins)
                        if j == NEJ:
                            pe.wait_ge(sg("moe_oh"), p * 4 + (2 * i + 3))
                            pe.wait_ge(sg("moe_ohT"), p * 2 + (i + 1))
                            gather(0, bank[7])
                            pe.wait_ge(sg("moe_act"), p * (2 * NEJ) + (NEJ * i + NEJ - 2 + 3))
                            gather(1, bank[(NEJ * (i + 1)) % 2])
                        if j == 0:
                            continue
                        n = NEJ * i + j - 1
                        pe.wait_ge(sg("moe_act"), p * (2 * NEJ) + (n + 3))
                        if j == 1:
                            pe.wait_ge(sg("moe_h"), p * 8 + (4 * i + 1))
                        for k in range(4):
                            ins = T.transpose(bank[4][:, k * P:(k + 1) * P], eact[:, n % 2, k * P:(k + 1) * P], ident[:, :])
                        ins.then_inc(sg("moe_Tfull"), 1)
                        w = deep(here(i, upos["d", j - 1]))
                        pe.wait_ge(sg("moe_actT"), p * (2 * NEJ) + (n + 1))
                        for k in range(4):
                            for half in range(2):
                                ins = T.matmul(bank[5 + half][:, :], eactT[:, n % 2, k * P:(k + 1) * P],
                                               w[:, k, half * 512:(half + 1) * 512],
                                               start=(j == 1 and k == 0), stop=(j == NEJ and k == 3))
                        used(ins)
                        if j == 3:
                            pe.wait_ge(sg("moe_oh"), p * 4 + (2 * i + 2))
                            for t in range(TT):
                                ins = T.transpose(bank[7][:, t * P:(t + 1) * P], ohg[:, t, :], ident[:, :])
                            ins.then_inc(sg("moe_ohfull"), 1)
                    pe.wait_ge(sg("moe_y0"), p * 2 + (i + 1))
                    pe.wait_ge(sg("moe_y1"), p * 2 + (i + 1))
                    pe.wait_ge(sg("moe_xg"), p * 4 + (2 * i + 4))
                    for q in range(4):
                        t, half = q // 2, q % 2
                        if q >= 2:
                            pe.wait_ge(sg("moe_h"), p * 8 + (4 * i + q))
                        T.matmul(bank[7 if q % 2 == 0 else 4][:, :], ohT[:, t * P:(t + 1) * P],
                                 ey[:, half * 512:(half + 1) * 512], start=True, stop=True).then_inc(sg("moe_scfull"), 1)
            pe.wait_ge(sg("moe_h"), more * 8 + (8 * NPAIR + 1))
            norm("n4")
            for b in range(2):
                fm(("cqf", b), arrived(pe, "cqf"), b * 2 * P)
            for t in range(TT):
                tm(("cig", t), arrived(pe, "cig"), t)
            pe.wait_ge(sg("hl_A"), 1)
            levels("hl", m, False)
            pe.wait_ge(sg("ci"), TT)
            for t in range(TT):
                ps = take(("co", t))
                for hd in range(CH):
                    b, hf = hd // 2, hd % 2
                    o = ps[:, hd * HD:(hd + 1) * HD]
                    cs = slice(hd * HD, (hd + 1) * HD)
                    if t:
                        T.matmul(o, m["crs"][:, hf * 256 + b * P:hf * 256 + (b + 1) * P], ci[:, 0, cs], start=True, stop=False)
                    ins = T.matmul(o, m["att"][:, hf, (2 * t + b) * P:(2 * t + b + 1) * P], ci[:, t, cs], start=(t == 0), stop=True)
                done(ins, ("co", t))
            for nm in ("aq", "ak"):
                for b in range(2):
                    fm((nm, b), arrived(pe, nm), b * 2 * P)
            for t in range(TT):
                tm(("av", t), arrived(pe, "av"), t)
            for b in range(2):
                fm(("bqk", b), arrived(pe, "bqk"), b * 2 * P)
            for t in range(TT):
                tm(("bvo", t), arrived(pe, "bvo"), t)
            pe.wait_ge(sg("ws_in"), 96)
            for i, nm in enumerate(("cf", "bi", "bf")):
                ps = take(nm)
                for k in range(KD):
                    ins = T.matmul(ps[0:72, 0:S], ws[:, i, k, :], xT[:, k, :], start=(k == 0), stop=(k == KD - 1))
                done(ins, nm)
            pe.wait_ge(sg("qk_sq"), 1)
            for i in range(4):
                done(T.matmul(take(("qkss", i))[:, :], pair64[:, :], rs[:, i * 512:(i + 1) * 512], start=True, stop=True),
                     ("qkss", i))
            pe.wait_ge(sg("qk_n"), 2)
            pe.wait_ge(sg("c_rows"), 1)
            ao = [take(("ao", t)) for t in range(TT)]

            def fox_scores(hd):
                b, r = hd // 2, slice(64 * (hd % 2), 64 * (hd % 2) + 64)
                ps = take(("s", hd))
                for i, (qt_, kt_) in enumerate(((0, 0), (1, 0), (1, 1))):
                    o = ps[:, i * P:(i + 1) * P]
                    qs, ks = slice(qt_ * P, (qt_ + 1) * P), slice(kt_ * P, (kt_ + 1) * P)
                    T.matmul(o, aq[r, b, qs], ak[r, b, ks], start=True, stop=False)
                    T.matmul(o, cS[r, qs], sel[r, hd, :], start=False, stop=False)
                    ins = T.matmul(o, sel[r, hd, :], ncS[r, ks], start=False, stop=True)
                done(ins, ("s", hd))

            def fox_values(hd):
                ps = take(("pT", hd))
                pe.wait_ge(sg("s_exp"), TT * (hd + 1))
                for i in range(3):
                    ins = T.transpose(ps[:, i * P:(i + 1) * P], sS[:, hd % 2, i * P:(i + 1) * P], ident[:, :])
                done(ins, ("pT", hd))
                gone(pe, ("pT", hd))
                cs = slice(hd * HD, (hd + 1) * HD)
                i0 = T.matmul(ao[0][:, cs], pTs[:, hd % 2, 0:P], av[:, 0, cs], start=True, stop=True)
                T.matmul(ao[1][:, cs], pTs[:, hd % 2, P:S], av[:, 0, cs], start=True, stop=False)
                i1 = T.matmul(ao[1][:, cs], pTs[:, hd % 2, S:384], av[:, 1, cs], start=False, stop=True)
                if hd == AH - 1:
                    done(i0, ("ao", 0))
                    done(i1, ("ao", 1))

            fox_scores(0)
            for hd in range(AH):
                if hd + 1 < AH:
                    fox_scores(hd + 1)
                fox_values(hd)
            pe.wait_ge(sg("m_rows"), 1)
            pe.wait_ge(sg("b_act"), 1)
            ps = take("mT")
            for t in range(TT):
                ins = T.transpose(ps[:, t * P:(t + 1) * P], mS[:, t * P:(t + 1) * P], ident[:, :])
            done(ins, "mT")
            bo = [take(("bo", t)) for t in range(TT)]

            def lstm_scores(hd):
                b, r = hd // 2, slice(64 * (hd % 2), 64 * (hd % 2) + 64)
                ps = take(("P2", hd))
                for i, (st, tt) in enumerate(((0, 0), (0, 1), (1, 1))):
                    o = ps[:, i * P:(i + 1) * P]
                    T.matmul(o, sel[r, hd, :], nM[r, tt * P:(tt + 1) * P], start=True, stop=False)
                    ins = T.matmul(o, iF[r, st * P:(st + 1) * P], sel[r, hd, :], start=False, stop=True)
                done(ins, ("P2", hd))
                ps = take(("P1", hd))
                for i, (st, tt) in enumerate(((0, 0), (0, 1), (1, 1))):
                    ins = T.matmul(ps[:, i * P:(i + 1) * P], bc[r, 2 + b, st * P:(st + 1) * P], bc[r, b, tt * P:(tt + 1) * P],
                                   start=True, stop=True)
                done(ins, ("P1", hd))

            def lstm_values(hd):
                pe.wait_ge(sg("d_w"), hd + 1)
                cs = slice(hd * 65, (hd + 1) * 65)
                w = sS[:, hd % 2, :]
                i0 = T.matmul(bo[0][:, cs], w[:, 0:P], bv[:, 0, hd, :], start=True, stop=True)
                T.matmul(bo[1][:, cs], w[:, P:S], bv[:, 0, hd, :], start=True, stop=False)
                i1 = T.matmul(bo[1][:, cs], w[:, S:384], bv[:, 1, hd, :], start=False, stop=True)
                if hd == BH - 1:
                    done(i0, ("bo", 0))
                    done(i1, ("bo", 1))
                else:
                    i1.then_inc(sg("b_pv"), 1)

            lstm_scores(0)
            for hd in range(BH):
                if hd + 1 < BH:
                    lstm_scores(hd + 1)
                lstm_values(hd)
            pe.wait_ge(sg("o_done"), 1)
            transposes("yy")
            out_proj("w2", [("w2", 0), ("w2", 1)])
            norm("n5")
            ffn("f2")


def kernel(**inputs):
    import numpy as np
    import concourse.bacc as bacc
    from concourse import mybir
    from concourse.bass_utils import run_bass_kernel_spmd

    nc = bacc.Bacc("TRN2", target_bir_lowering=False, num_devices=1)
    arrays, aps = {}, {}
    for name, a in inputs.items():
        a = np.ascontiguousarray(a)
        arrays[f"in_{name}"] = a
        aps[name] = nc.dram_tensor(f"in_{name}", a.shape, mybir.dt.from_np(a.dtype), kind="ExternalInput").ap()
    shape = inputs["x"].shape
    out = nc.dram_tensor("out_0", shape, mybir.dt.float32, kind="ExternalOutput").ap()
    build(nc, aps, out)
    r = run_bass_kernel_spmd(nc, [arrays], core_ids=[0])
    return r.results[0]["out_0"]
```

```python
def build(nc, IN, out):
    import concourse.bass as bass
    from concourse import mybir
    from contextlib import ExitStack

    F32, F32R, I32 = mybir.dt.float32, mybir.dt.float32r, mybir.dt.int32
    ACT, ALU, AX = mybir.ActivationFunctionType, mybir.AluOpType, mybir.AxisListType
    P = 128
    _, S, D = IN["x"].shape
    TT = S // P
    KD = D // P
    EPS = 1e-6
    NEG = -1e30
    F1 = IN["ffn_w_gate"].shape[2]
    F2 = IN["w_down_2"].shape[1]
    _, NE, _, FE = IN["moe_w_gate"].shape
    GH, GDK, GDV = 4, 128, 256
    GR = IN["gla_w_gate_up"].shape[1]
    GQK, GV = GH * GDK, GH * GDV
    GATE_NORM = 16.0
    SH = 8
    AH, BH, CH, HD = 8, 4, 4, 64
    AD, BD = AH * HD, BH * HD
    FJ = 256
    NJ1, NJ2 = F1 // FJ, F2 // FJ
    assert NJ1 == NJ2 and NJ1 % 2 == 1
    EJ = 512
    NEJ = FE // EJ
    PIECE = 2048
    NR, NRX, NW = 4, 6, 4
    LO_V = 1536
    AR = 11392
    LEVELS = [0, 1, 2, 4, 8, 16, 32, 64]
    C_AQ, C_AK, C_AV, C_AF = 0, AD, 2 * AD, 3 * AD
    C_BQK = 3 * AD + AH
    C_BV = C_BQK + 2 * BD
    C_BI = C_BV + BD
    C_BF = C_BI + BH
    C_BO = C_BF + BH
    C_CQ = C_BO + BD
    C_CI = C_CQ + 2 * BD
    C_CG = C_CI + BD

    ctx = ExitStack()
    with ctx:
        def sb(name, shape, dt=F32):
            return ctx.enter_context(nc.sbuf_tensor(name, shape, dt))

        sems = {}

        def sg(name):
            if name not in sems:
                sems[name] = ctx.enter_context(nc.semaphore(name))
            return sems[name]

        raw = sb("raw", [P, NR, PIECE])
        wh = sb("wh", [P, NW, PIECE], F32R)
        wl = sb("wl", [P, NW, PIECE], F32R)
        h = sb("h", [P, TT, D])
        xT = sb("xT", [P, KD, S])
        xTh = sb("xTh", [P, KD, S], F32R)
        xTl = sb("xTl", [P, KD, S], F32R)
        acth = sb("acth", [P, 2, 512], F32R)
        actl = sb("actl", [P, 2, 512], F32R)
        xn = sb("xn", [P, TT, D])
        arena = sb("arena", [P, AR])
        ident = sb("ident", [P, P])
        lmask = sb("lmask", [P, len(LEVELS) - 2, P])
        after = sb("after", [P, P])
        before3 = sb("before3", [P, 3, P])
        rowneg3 = sb("rowneg3", [P, 3, P])
        colneg3 = sb("colneg3", [P, 3, P])
        pair64 = sb("pair64", [P, P])
        sel = sb("sel", [P, AH, P])
        iota = sb("iota", [P, P])
        tri8 = sb("tri8", [P, NE, NE])
        cst = sb("cst", [P, 34])
        c_eps, c_one, c_half = cst[:, 0:1], cst[:, 1:2], cst[:, 2:34]
        WS0 = (0, AH, AH + BH)
        ws = sb("ws", [P, KD, WS0[2] + 72])
        wglr = sb("wglr", [P, KD, GR])
        wrt = sb("wrt", [P, KD, NE])
        vT = sb("vT", [P, 3, P])
        ssq = sb("ssq", [P, 32])
        ms = sb("ms", [P, 32])
        rstd = sb("rstd", [P, 32])
        scr = sb("scr", [P, 1])
        bank = [ctx.enter_context(nc.psum_tensor(f"bank{b}", [P, 512], F32)) for b in range(8)]

        ar_at = [0]

        def ar_reset(at=0):
            ar_at[0] = at

        def ar(n):
            a = arena[:, ar_at[0]:ar_at[0] + n]
            ar_at[0] += n
            assert ar_at[0] <= AR, ar_at[0]
            return a

        vec_rows = {}
        vec_dma = []
        at = [0, 0, 0]

        def rows(name, tile, ap, n):
            vec_rows[name] = (tile, at[tile])
            vec_dma.append((tile, at[tile], n, ap))
            at[tile] += n

        names = (("attn_norm", 2 * KD), ("gla_b_gate", GQK // P), ("gla_head_norm", GDV // P),
                 ("gla_head_norm again", GDV // P),
                 ("ffn_norm", 2 * KD), ("kv_norm", KD), ("norm_mix_g_2", KD), ("norm_ffn_g_2", KD), ("out_g_2", KD),
                 ("lb_logits_2", 2))
        N_EARLY = 4
        for nm, n in names:
            a = IN[nm.split()[0]]
            a = a.rearrange("(r p) -> r p", p=P) if len(a.shape) == 1 else a.rearrange("a (r p) -> (a r) p", p=P)
            rows(nm, 0, a, n)
            if len(vec_dma) == N_EARLY:
                V_EARLY = at[0]
                at[0] = 32
        for nm, c0, n in (("aq_b", C_AQ, 4), ("ak_b", C_AK, 4), ("bqk_b", C_BQK, 4), ("cqf_b", C_CQ, 4)):
            rows(nm, 0, IN["b_in_2"][0, c0:c0 + n * P].rearrange("(r p) -> r p", p=P), n)
        rows("b_conv", 0, IN["b_conv_w_2"].rearrange("a k (r p) -> (a k r) p", p=P), 16)
        R_G = at[0]
        at[0] += 5
        NF2 = 2 * F2 // P
        rows("tap01", 1, IN["ffn_conv_w_2"][0, 0:2, :].rearrange("k (r p) -> (k r) p", p=P), 2 * NF2)
        rows("tap2", 2, IN["ffn_conv_w_2"][0, 2:3, :].rearrange("k (r p) -> (k r) p", p=P), NF2)
        rows("conv_b", 2, IN["ffn_conv_b_2"].rearrange("k (r p) -> (k r) p", p=P), NF2)
        V_ROWS = [at[0], at[1], at[2]]
        N_VEC = len(vec_dma) - N_EARLY + 10

        def col(name, i=0):
            tile, r = vec_rows[name]
            return vT[:, tile, r + i:r + i + 1]

        def cols(name, i, n):
            tile, r = vec_rows[name]
            return vT[:, tile, r + i:r + i + n]

        turns, uses, rr = {}, [0] * 8, [0]

        def turn(label, b=None):
            if b is None:
                b = rr[0] % 8
                rr[0] += 1
            turns[label] = (b, uses[b])
            uses[b] += 1

        full = [sg(f"full{b}") for b in range(8)]
        freed = [sg(f"freed{b}") for b in range(8)]

        def plan_norm(n):
            for t in range(TT):
                for half in range(2):
                    turn((n, t, half))

        def plan_ffn(f):
            def gu(j):
                turn((f, j, "g"), 2 * (j % 2))
                turn((f, j, "u"), 2 * (j % 2) + 1)
            gu(0)
            for t in range(TT):
                for half in range(2):
                    turn((f, "acc", t, half), 4 + 2 * t + half)
            for j in range(1, NJ1):
                gu(j)
            rr[0] = 0

        turn(("vec", "early"))
        plan_norm("n0")
        for lab in ("glr", ("gate", 0), ("gate", 1), ("q", 0), ("q", 1), ("k", 0), ("k", 1)):
            turn(lab)
        for nm in "vr":
            for c in range(2):
                for t in range(TT):
                    turn((nm, c, t))
            if nm == "v":
                for i in range(3):
                    turn(("vec", i))

        def plan_levels(pre, cross):
            for m in LEVELS:
                for g in range(2):
                    turn((pre, m, g))
            for g in range(cross):
                turn((pre, P, g))

        plan_levels("gl", 1)
        for t in range(TT):
            for hp in range(2):
                turn(("o", t, hp))
        plan_norm("y")
        for c in range(2):
            for t in range(TT):
                turn(("wo", c, t))
        plan_norm("n1")
        plan_ffn("f1")
        plan_norm("n2")
        for b in range(4):
            turn(("sk", b))
        for c in range(2):
            for t in range(TT):
                turn(("sv", c, t))
        for b in range(4):
            turn(("sq", b))
        for hd in range(SH):
            turn(("z", hd))
        for hd in range(SH):
            turn(("stay", hd))
        for hp in range(SH // 2):
            turn(("so", hp))
        for c in range(2):
            for t in range(TT):
                turn(("swo", c, t))
        plan_norm("n3")
        turn("lg")
        turn("pos")
        turn("cnt")
        uses_before_moe = list(uses)
        plan_norm("n4")
        for b in range(2):
            turn(("cqf", b))
        for t in range(TT):
            turn(("cig", t))
        plan_levels("hl", 2)
        for t in range(TT):
            turn(("co", t))
        for nm in ("aq", "ak"):
            for b in range(2):
                turn((nm, b))
        for t in range(TT):
            turn(("av", t))
        for b in range(2):
            turn(("bqk", b))
        for t in range(TT):
            turn(("bvo", t))
        for nm in ("cf", "bi", "bf"):
            turn(nm)
        for i in range(4):
            turn(("qkss", i))
        rr[0] = 0
        for t in range(TT):
            turn(("ao", t), 6 + t)
        for hd in range(AH):
            turn(("s", hd), hd % 3)
            turn(("pT", hd), 3 + hd % 3)
        turn("mT", 0)
        for t in range(TT):
            turn(("bo", t), 6 + t)
        for hd in range(BH):
            turn(("P2", hd), 1 + hd % 2)
            turn(("P1", hd), 3 + hd % 2)
        rr[0] = 0
        plan_norm("yy")
        for c in range(2):
            for t in range(TT):
                turn(("w2", c, t))
        plan_norm("n5")
        plan_ffn("f2")

        def see(eng, label):
            b, n = turns[label]
            eng.wait_ge(full[b], n + 1)
            return bank[b]

        def gone(eng, label):
            b, n = turns[label]
            eng.wait_ge(freed[b], n + 1)

        class Order:

            def __init__(self, eng, name):
                self.eng, self.own, self.count = eng, sg(name), {}

            def __call__(self, ins, name=None, frees=None):
                if frees is not None:
                    b, n = turns[frees]
                    ins.then_inc(freed[b], 1)
                    self.eng.wait_ge(freed[b], n + 1)
                    return
                s = self.own if name is None else sg(name)
                n = self.count[name] = self.count.get(name, 0) + 1
                ins.then_inc(s, 1)
                self.eng.wait_ge(s, n)

        def kpn(ap):
            return ap.rearrange("(k p) n -> p k n", p=P)

        pieces, pos = [], {}

        def piece(nm, parts, last, phase):
            pos[nm] = len(pieces)
            pieces.append((parts, last, phase))

        def fm_pieces(nm, src, phase, n):
            for b in range(n):
                piece((nm, b), [kpn(src[:, b * 256:(b + 1) * 256])], (nm, b), phase)

        def tm_pieces(nm, srcs, phase):
            for k in range(2):
                piece((nm, k), [kpn(a[k * 512:(k + 1) * 512, :]) for a in srcs], nm + (TT - 1,), phase)

        def ffn_pieces(f, gate, up, down, phase):
            for j in range(NJ1 + 1):
                if j < NJ1:
                    js = slice(j * FJ, (j + 1) * FJ)
                    piece((f, j, "g"), [kpn(gate[:, js])], (f, j, "g"), phase)
                    piece((f, j, "u"), [kpn(up[:, js])], (f, j, "u"), phase)
                if j:
                    piece((f, j - 1, "d"), [kpn(down[(j - 1) * FJ:j * FJ, :])],
                          ("down", f, j) if j < NJ1 else (f, "acc", TT - 1, 1), phase)

        w1 = IN["gla_w_in"][0]
        fm_pieces("q", w1[:, 0:GQK], 0, 2)
        fm_pieces("k", w1[:, GQK:2 * GQK], 0, 2)
        for nm, c0 in (("v", 2 * GQK), ("r", 2 * GQK + GV + GR)):
            for c in range(2):
                tm_pieces((nm, c), [w1[:, c0 + 512 * c:c0 + 512 * (c + 1)]], 0)
        for c in range(2):
            tm_pieces(("wo", c), [IN["gla_w_out"][0][:, 512 * c:512 * (c + 1)]], 0)
        ffn_pieces("f1", IN["ffn_w_gate"][0], IN["ffn_w_up"][0], IN["ffn_w_down"][0], 0)
        fm_pieces("sk", IN["sb_w_kv"][:, 0:D], 0, 4)
        for c in range(2):
            tm_pieces(("sv", c), [IN["sb_w_kv"][:, D + 512 * c:D + 512 * (c + 1)]], 0)
        fm_pieces("sq", IN["sb_w_q"][0], 0, 4)
        for c in range(2):
            tm_pieces(("swo", c), [IN["sb_w_out"][0][:, 512 * c:512 * (c + 1)]], 0)
        N_PRE = len(pieces)
        w2 = IN["w_in_2"][0]
        fm_pieces("cqf", w2[:, C_CQ:C_CQ + 2 * BD], 1, 2)
        tm_pieces(("cig",), [w2[:, C_CI:C_CI + 2 * BD]], 1)
        fm_pieces("aq", w2[:, C_AQ:C_AQ + AD], 1, 2)
        fm_pieces("ak", w2[:, C_AK:C_AK + AD], 1, 2)
        tm_pieces(("av",), [w2[:, C_AV:C_AV + AD]], 1)
        fm_pieces("bqk", w2[:, C_BQK:C_BQK + 2 * BD], 1, 2)
        tm_pieces(("bvo",), [w2[:, C_BV:C_BV + BD], w2[:, C_BO:C_BO + BD]], 1)
        for c in range(2):
            tm_pieces(("w2", c), [IN["w_out_2"][0][:, 512 * c:512 * (c + 1)]], 1)
        ffn_pieces("f2", IN["w_up_2"][0][:, 0:F2], IN["w_up_2"][0][:, F2:2 * F2], IN["w_down_2"][0], 1)
        by_pool = {pos[("wo", 1), k] for k in range(2)} | {pos[("w2", c), k] for c in range(2) for k in range(2)}

        raw_in = [[sg(f"raw_in{s}") for s in range(NR)], [sg(f"raw_in2_{s}") for s in range(NR)]]
        hi_ready = [sg("hi_ready"), sg("hi_ready2")]
        lo_ready = [sg("lo_ready"), sg("lo_ready2")]
        lo_pool = [sg("lo_pool"), sg("lo_pool2")]
        arrive, filled, lo_of, los = [], [[0] * NR, [0] * NR], [], {}
        for i, (parts, last, ph) in enumerate(pieces):
            filled[ph][i % NR] += 16 * len(parts)
            arrive.append(filled[ph][i % NR])
            s = (lo_pool if i in by_pool else lo_ready)[ph]
            los[s.name] = los.get(s.name, 0) + 1
            lo_of.append((s, los[s.name]))

        def of(slots, i, k):
            return slots[:, i % NW, :].rearrange("p (k n) -> p k n", k=k)

        def split_done(eng, i):
            eng.wait_ge(lo_of[i][0], lo_of[i][1])

        def released(eng, i):
            last = pieces[i][1]
            if last[0] == "down":
                eng.wait_ge(sg("down_done_" + last[1]), last[2])
            else:
                see(eng, last)

        class Split:

            def __init__(self, eng, mine):
                self.eng, self.mine, self.next = eng, mine, 0

            def upto(self, n):
                for i in range(self.next, n + 1):
                    if self.mine(i):
                        self.one(i)
                self.next = max(self.next, n + 1)

        class Hi(Split):
            def one(self, i):
                ph = pieces[i][2]
                self.eng.wait_ge(raw_in[ph][i % NR], arrive[i])
                if ph == 0 and i >= NW or i >= N_PRE + NW:
                    released(self.eng, i - NW)
                elif ph == 1:
                    self.eng.wait_ge(sg("moe_used"), self.more * PC + (NPAIR * PC - NW + 1 + i - N_PRE))
                nc.scalar.activation(wh[:, i % NW, :], raw[:, i % NR, :], ACT.Copy).then_inc(hi_ready[ph], 1)

        class Lo(Split):
            def one(self, i):
                ph = pieces[i][2]
                self.eng.wait_ge(hi_ready[ph], i + 1 if ph == 0 else i - N_PRE + 1)
                V = nc.gpsimd if i in by_pool else nc.vector
                V.tensor_tensor(wl[:, i % NW, :], raw[:, i % NR, :], wh[:, i % NW, :].bitcast(F32),
                                ALU.subtract).then_inc(lo_of[i][0], 1)

        uorder = []
        for j in range(NEJ):
            uorder += [("g", j, 0), ("g", j, 1), ("u", j, 0), ("u", j, 1)]
            if j:
                uorder += [("d", j - 1, 0), ("d", j - 1, 1)]
        uorder += [("d", NEJ - 1, 0), ("d", NEJ - 1, 1)]
        UC = len(uorder)
        PC = 2 * UC
        assert PC % NRX == 0 and PC % NW == 0
        upos = {c: i for i, c in enumerate(uorder)}
        NPAIR = NE // 2
        M0 = N_PRE
        lo_moe = [sg("lo_moe_v"), sg("lo_moe_p")]

        def moe_split(eng, at, c):
            n = at(PC, c + 1)
            for s in lo_moe:
                eng.wait_ge(s, n)

        def moe_raw(c):
            s = c % NRX
            return (raw[:, (M0 + s) % NR, :] if s < NR else extra[:, s - NR, :]), raw_moe[s]

        raw_moe = [sg(f"raw_moe{s}") for s in range(NRX)]

        def pairs(eng, body):
            more = eng.value_load(more_i[0:1, 0:1], min_val=0, max_val=NPAIR)
            with eng.Fori(0, more + (NPAIR - 1)) as p:
                body(lambda a, b: p * a + b, True)
            body(lambda a, b: more * a + ((NPAIR - 1) * a + b), False)
            return more

        ar_reset()
        g = {}
        for nm in ("Q", "K", "A", "E", "W", "qt", "kt"):
            g[nm] = ar(GH * S)
        g["att"] = ar(2 * 512).rearrange("p (g n) -> p g n", g=2)
        g["crs"] = ar(512)
        g["mt"] = ar(512)
        gr = ar(TT * GV).rearrange("p (t n) -> p t n", t=TT)
        gv = xT.rearrange("p k s -> p (k s)").rearrange("p (t n) -> p t n", t=TT)
        wgu = g["mt"][0:GR, :]
        glrT = g["att"].rearrange("p g n -> p (g n)")[0:GR, 0:S]
        vrow = gr.rearrange("p t n -> p (t n)")[:, 0:3 * P].rearrange("p (a b) -> p a b", a=3)
        ar_reset()
        f_sg = ar(2 * 512).rearrange("p (a n) -> p a n", a=2)
        f_act = ar(2 * 512).rearrange("p (a n) -> p a n", a=2)
        f_cu = ar(2 * 1024).rearrange("p (a n) -> p a n", a=2)
        ar_reset()
        skT = xT
        sqT = ar(SH * S).rearrange("p (h s) -> p h s", h=SH)
        xq = arena[:, ar_at[0]:ar_at[0] + KD * S].rearrange("p (k s) -> p k s", k=KD)
        sE, sT, sU = (ar(SH * 384).rearrange("p (h s) -> p h s", h=SH) for _ in range(3))
        sv = xn
        ar_reset()
        lg = ar(TT * NE).rearrange("p (t e) -> p t e", t=TT)
        cmp1 = ar(TT * NE * NE).rearrange("p (t e j) -> p t e j", t=TT, e=NE)
        cmp2 = ar(TT * NE * NE).rearrange("p (t e j) -> p t e j", t=TT, e=NE)
        rank = ar(TT * NE).rearrange("p (t e) -> p t e", t=TT)
        selx = ar(TT * NE).rearrange("p (t e) -> p t e", t=TT)
        mx = ar(TT)
        ex = ar(TT * NE).rearrange("p (t e) -> p t e", t=TT)
        exs = ar(TT)
        NU = 2 * NE + 2
        pm = ar(NU * TT).rearrange("p (u t) -> p u t", u=NU)
        gt = ar(NU * TT).rearrange("p (u t) -> p u t", u=NU)
        cmax = ar(2)
        more_i = ar(1).bitcast(I32)
        oh = ar(TT * P).rearrange("p (t s) -> p t s", t=TT)
        ohg = ar(TT * P).rearrange("p (t s) -> p t s", t=TT)
        ohT = ar(S)
        xg = ar(KD * P).rearrange("p (k s) -> p k s", k=KD)
        xgh, xgl = xTh[:, :, 0:P], xTl[:, :, 0:P]
        eactTh, eactTl = xTh[:, :, P:S], xTl[:, :, P:S]
        esg = ar(2 * EJ).rearrange("p (a n) -> p a n", a=2)
        eact = ar(2 * EJ).rearrange("p (a n) -> p a n", a=2)
        ey = ar(D)
        fgain = ar(D)
        assert ar_at[0] <= AR - (NRX - NR) * PIECE
        ar_reset(AR - (NRX - NR) * PIECE)
        extra = ar((NRX - NR) * PIECE).rearrange("p (a n) -> p a n", n=PIECE)
        ar_reset()
        m = {}
        for nm in ("Q", "K", "A", "E", "W", "qt", "kt"):
            m[nm] = ar(2 * S)
        m["att"] = ar(2 * 512).rearrange("p (g n) -> p g n", g=2)
        m["crs"] = ar(512)
        m["mt"] = ar(512)
        mix0 = ar_at[0]
        ar_reset()
        aq, ak = (ar(4 * S).rearrange("p (b s) -> p b s", b=4) for _ in range(2))
        av = ar(TT * AD).rearrange("p (t n) -> p t n", t=TT)
        bz, bc = (ar(4 * S).rearrange("p (b s) -> p b s", b=4) for _ in range(2))
        ar_reset(max(mix0, ar_at[0]))
        bv = ar(TT * BH * 65).rearrange("p (t h n) -> p t h n", t=TT, h=BH)
        bog = ar(TT * BD).rearrange("p (t n) -> p t n", t=TT)
        cg = ar(TT * BD).rearrange("p (t n) -> p t n", t=TT)
        tmb = ar(1536)
        lbp, lb1 = ar(2), ar(2)
        nmx, asum, arec = ar(AH * TT), ar(AH * TT), ar(AH * TT)
        em, den = ar(TT * BH), ar(TT * BH)
        gq = ar(2)
        mix1 = ar_at[0]
        ci = ar(TT * BD).rearrange("p (t n) -> p t n", t=TT)
        ar_reset(mix1)
        rs = ar(8 * S)
        ar_reset(mix1)
        sS, pTs, Dm = (ar(2 * 384).rearrange("p (a n) -> p a n", a=2) for _ in range(3))
        cS, ncS, iF, nM, mS, row1 = (xT[:, i, :] for i in range(6))
        o_all = xn

        def quarters(n):
            return [((n, t, half), (slice(None), slice(4 * half, 4 * half + 4), slice(t * P, (t + 1) * P)))
                    for t in range(TT) for half in range(2)]

        head_pairs = [(("so", hp), (slice(None), slice(2 * hp, 2 * hp + 2), slice(None))) for hp in range(SH // 2)]

        block = ctx.enter_context(nc.Block())
        xv = IN["x"][0].rearrange("(t p) d -> p t d", p=P)
        ov = out[0].rearrange("(t p) d -> p t d", p=P)

        @block.sync
        def _(sp):
            sp.dma_start(h[:, :, :], xv).then_inc(sg("x_in"), 16)

            def load(i):
                parts, _, ph = pieces[i]
                n0 = 0
                for part in parts:
                    k, n = part.shape[1], part.shape[2]
                    sp.dma_start(of(raw, i, k)[:, :, n0:n0 + n], part).then_inc(raw_in[ph][i % NR], 16)
                    n0 += n

            def load_expert(c, e):
                kind, j, k = uorder[c % UC]
                ee = e + c // UC
                to, arrived = moe_raw(c)
                if kind == "d":
                    r0 = j * EJ + k * (EJ // 2)
                    src = IN["moe_w_down"][0].rearrange("e f n -> (e f) n")[bass.ds(ee * FE + r0, EJ // 2), :]
                    src = kpn(src)
                else:
                    src = IN["moe_w_gate" if kind == "g" else "moe_w_up"][0, bass.ds(ee, 1), k * (D // 2):(k + 1) * (D // 2),
                                                                          j * EJ:(j + 1) * EJ]
                    src = src.rearrange("a (k p) n -> p (a k) n", p=P)
                sp.dma_start(to.rearrange("p (k n) -> p k n", k=src.shape[1]), src).then_inc(arrived, 16)

            for i in range(NR):
                load(i)
            sp.wait_ge(sg("vrow_zero"), 1)
            nv = 0
            for tile, r0, n, ap in vec_dma[N_EARLY:]:
                sp.dma_start(vrow[r0:r0 + n, tile, :], ap).then_inc(sg("vec_in"), 16)
                nv += 1
            for i, nm in enumerate(("a_q_g_2", "a_k_g_2")):
                for half in range(2):
                    sp.dma_start(vrow[R_G + i:R_G + i + 1, 0, 64 * half:64 * half + 64], IN[nm]).then_inc(sg("vec_in"), 16)
                    nv += 1
            for i, (c0, n) in enumerate(((C_AF, AH), (C_BI, BH), (C_BF, BH))):
                for half in range(2):
                    sp.dma_start(vrow[R_G + 2 + i:R_G + 3 + i, 0, 64 * half:64 * half + n],
                                 IN["b_in_2"][0:1, c0:c0 + n]).then_inc(sg("vec_in"), 16)
                    nv += 1
            assert nv == N_VEC, nv
            for i in range(NR, N_PRE):
                split_done(sp, i - NR)
                load(i)
                if i == pos["f1", 2, "g"]:
                    sp.dma_start(wrt[:, :, :], kpn(IN["moe_w_router"][0])).then_inc(sg("rt_in"), 16)
                    sp.wait_ge(sg("ws_zero"), 1)
                    for j, (c0, n) in enumerate(((C_AF, AH), (C_BI, BH), (C_BF, BH))):
                        for half in range(2):
                            d0 = 64 * half + WS0[j]
                            sp.dma_start(ws[:, :, d0:d0 + n], kpn(w2[:, c0:c0 + n]),
                                         allow_slow_non_contiguous=True).then_inc(sg("ws_in"), 16)
            for c in range(NR):
                split_done(sp, N_PRE - NR + c)
                load_expert(c, 0)
            for hp in range(SH // 2):
                see(sp, ("so", hp))
            for c in range(NR, NRX):
                load_expert(c, 0)
            sp.wait_ge(sg("more_ready"), 1)
            more = sp.value_load(more_i[0:1, 0:1], min_val=0, max_val=NPAIR)
            with sp.Fori(0, more + (NPAIR - 1)) as p:
                e = (p % NPAIR) * 2
                for c in range(NRX, PC):
                    moe_split(sp, lambda a, b: p * a + b, c - NRX)
                    load_expert(c, e)
                e2 = ((p + 1) % NPAIR) * 2
                for c in range(NRX):
                    moe_split(sp, lambda a, b: p * a + b, c + PC - NRX)
                    load_expert(c, e2)
            for c in range(NRX, PC + NR):
                moe_split(sp, lambda a, b: more * a + ((NPAIR - 1) * a + b), c - NRX)
                if c < PC:
                    load_expert(c, NE - 2)
                else:
                    load(N_PRE + c - PC)
            for i in range(N_PRE + NR, len(pieces)):
                split_done(sp, i - NR)
                load(i)
            for t in range(TT):
                for half in range(2):
                    gone(sp, ("f2", "acc", t, half))
                sp.dma_start(ov[:, t, :], h[:, t, :]).then_inc(sg("out_done"), 16)
            sp.wait_ge(sg("out_done"), 16 * TT)

        @block.gpsimd
        def _(pool):
            G = Order(pool, "pool_order")
            V = nc.gpsimd
            G(V.memset(vrow, 0.0), "vrow_zero")
            G(V.memset(ident[:, :], 0.0))
            G(V.affine_select(out=ident[:, :], in_=ident[:, :], compare_op=ALU.not_equal, fill=1.0, base=0,
                              pattern=[[-1, P]], channel_multiplier=1), "const")
            G(V.memset(cst[:, 0:1], EPS))
            G(V.memset(cst[:, 1:2], 1.0))
            G(V.memset(c_half, -0.5), "const")
            for mm in (g["E"],):
                G(V.memset(mm, 0.0))
            G(V.memset(lmask[:, :, :], 0.0))
            for i, mh in enumerate(LEVELS[1:-1]):
                n = P // (2 * mh)
                v = lmask[:, i, :].rearrange("p (n two m) -> p n two m", two=2, m=mh)[:, :, 1, :]
                G(V.memset(v, 1.0))
                G(V.affine_select(out=v, in_=v, compare_op=ALU.is_ge, fill=0.0, base=0,
                                  pattern=[[-2 * mh, n], [0, mh]], channel_multiplier=1))
                G(V.affine_select(out=v, in_=v, compare_op=ALU.is_ge, fill=0.0, base=mh - 1,
                                  pattern=[[2 * mh, n], [0, mh]], channel_multiplier=-1))
            G(V.memset(g["qt"], 0.0))
            G(V.memset(g["kt"], 0.0), "masks")
            lo = Lo(pool, lambda i: i in by_pool)

            turn_of = [0]

            def rsqrt(n):
                turn_of[0] += 1
                pool.wait_ge(sg("ms_ready"), turn_of[0])
                G(V.tensor_tensor(rstd[:, 0:n], ms[:, 0:n], c_half[:, 0:n], ALU.pow), "rstd_ready")

            def halves(a, mh):
                v = a.rearrange("p (n two m) -> p n two m", two=2, m=mh)
                return v[:, :, 0, :], v[:, :, 1, :]

            def grow(pre, T):
                for i, mh in enumerate(LEVELS[1:]):
                    Al, Ar = halves(T["A"], mh)
                    El, Er = halves(T["E"], mh)
                    pool.wait_ge(sg(pre + "_exp"), 2 * (i + 1))
                    G(V.tensor_tensor(El, El, Ar[:, :, mh - 1:mh].to_broadcast(list(El.shape)), ALU.add))
                    G(V.tensor_tensor(Ar, Ar, Al[:, :, mh - 1:mh].to_broadcast(list(Ar.shape)), ALU.add), pre + "_sums")

            rsqrt(TT)
            G(V.memset(after[:, :], 1.0))
            G(V.affine_select(out=after[:, :], in_=after[:, :], compare_op=ALU.is_ge, fill=0.0, base=-1,
                              pattern=[[-1, P]], channel_multiplier=1))
            G(V.memset(before3[:, :, :], 1.0))
            for i in (0, 2):
                G(V.affine_select(out=before3[:, i, :], in_=before3[:, i, :], compare_op=ALU.is_ge, fill=0.0,
                                  base=-1, pattern=[[1, P]], channel_multiplier=-1))
            G(V.memset(rowneg3[:, :, :], 0.0))
            G(V.memset(colneg3[:, :, :], 0.0))
            for i in (0, 2):
                G(V.affine_select(out=rowneg3[:, i, :], in_=rowneg3[:, i, :], compare_op=ALU.is_ge, fill=NEG,
                                  base=0, pattern=[[-1, P]], channel_multiplier=1))
                G(V.affine_select(out=colneg3[:, i, :], in_=colneg3[:, i, :], compare_op=ALU.is_ge, fill=NEG,
                                  base=0, pattern=[[1, P]], channel_multiplier=-1))
            G(V.memset(pair64[:, :], 0.0))
            G(V.memset(pair64[0:64, 0:64], 1.0))
            G(V.memset(pair64[64:P, 64:P], 1.0))
            G(V.memset(sel[:, :, :], 0.0))
            for b0 in (0, 64):
                G(V.affine_select(out=sel[:, :, :], in_=sel[:, :, :], compare_op=ALU.not_equal, fill=1.0, base=-b0,
                                  pattern=[[-1, AH], [0, P]], channel_multiplier=1))
            G(V.iota(iota[:, :], pattern=[[1, P]], base=0, channel_multiplier=0, allow_small_or_imprecise_dtypes=True))
            G(V.memset(tri8[:, :, :], 1.0))
            G(V.affine_select(out=tri8[:, :, :], in_=tri8[:, :, :], compare_op=ALU.is_ge, fill=0.0, base=-1,
                              pattern=[[1, NE], [-1, NE]], channel_multiplier=0), "masks2")
            G(V.memset(ws[:, :, :], 0.0), "ws_zero")
            pool.wait_ge(sg("gl_A"), 1)
            grow("gl", g)
            lo.upto(pos[("wo", 1), 1])
            rsqrt(GH * TT)
            rsqrt(TT)
            rsqrt(TT)
            rsqrt(TT)
            pool.wait_ge(sg("more_ready"), 1)

            def rests(at, more_follow):
                for c in range(PC):
                    s = (M0 + c) % NW
                    pool.wait_ge(sg("hi_moe"), at(PC, c + 1))
                    V.tensor_tensor(wl[:, s, LO_V:PIECE], moe_raw(c)[0][:, LO_V:PIECE], wh[:, s, LO_V:PIECE].bitcast(F32),
                                    ALU.subtract).then_inc(lo_moe[1], 1)

            pairs(pool, rests)
            rsqrt(TT)
            rsqrt(TT)
            pool.wait_ge(sg("xn_ready"), 5 * TT)
            G(V.memset(m["kt"], 0.0))
            G(V.memset(bv[:, :, :, 64:65], 1.0), "mix_zero")
            pool.wait_ge(sg("hl_A"), 1)
            grow("hl", m)
            lo.upto(pos[("w2", 1), 1])
            rsqrt(TT * 16)
            rsqrt(TT)

        @block.scalar
        def _(act):
            A = Order(act, "act_order")
            V = nc.scalar
            act.wait_ge(sg("vrow_zero"), 1)
            for tile, r0, n, ap in vec_dma[0:N_EARLY]:
                act.dma_start(vrow[r0:r0 + n, tile, :], ap).then_inc(sg("vec_first"), 16)
            act.dma_start(wglr[:, :, :], kpn(w1[:, 2 * GQK + GV:2 * GQK + GV + GR])).then_inc(sg("glr_in"), 16)
            act.dma_start(wgu, IN["gla_w_gate_up"][0]).then_inc(sg("glr_in"), 16)
            hi = Hi(act, lambda i: True)

            def split_x(blocks, src=xT):
                for lab, ix in blocks:
                    gone(act, lab)
                    A(V.activation(xTh[ix], src[ix], ACT.Copy), "xh_ready")

            def norm(before):
                for t in range(TT):
                    for lab in before(t):
                        gone(act, lab)
                    A(V.activation(xn[:, t, :], h[:, t, :], ACT.Square, accum_out=ssq[:, t:t + 1]), "ssq_ready")

            def exps(pre, T):
                for i, mh in enumerate(LEVELS[1:] + [P]):
                    def half(a, j):
                        return a.rearrange("p (n two m) -> p n two m", two=2, m=mh)[:, :, j, :]
                    if i:
                        act.wait_ge(sg(pre + "_sums"), i)
                        act.wait_ge(sg(pre + "_qk"), 2 * i)
                    A(V.activation(half(T["W"], 1), half(T["A"], 1), ACT.Exp), pre + "_exp")
                    A(V.activation(half(T["W"], 0), half(T["E"], 0), ACT.Exp), pre + "_exp")

            act.wait_ge(sg("x_in"), 16)
            norm(lambda t: [])
            hi.upto(1)
            split_x(quarters("n0"))
            hi.upto(3)
            act.wait_ge(sg("gl_abs"), 1)
            A(V.activation(g["W"], g["W"], ACT.Exp, scale=-1.0))
            A(V.activation(g["W"], g["W"], ACT.Ln, bias=c_one), "gl_ln")
            for b in range(2):
                A(V.activation(g["Q"][:, b * 512:(b + 1) * 512], see(act, ("q", b))[:, :], ACT.Copy, scale=GDK ** -0.5),
                  frees=("q", b))
                hi.upto(pos["q", b] + NW)
            for b in range(2):
                A(V.activation(g["K"][:, b * 512:(b + 1) * 512], see(act, ("k", b))[:, :], ACT.Copy), frees=("k", b))
                hi.upto(pos["k", b] + NW)
            for nm, dst in (("v", gv), ("r", gr)):
                for c in range(2):
                    for t in range(TT):
                        A(V.activation(dst[:, t, c * 512:(c + 1) * 512], see(act, (nm, c, t))[:, :], ACT.Copy),
                          frees=(nm, c, t))
                    hi.upto(pos[(nm, c), 1] + NW)
            act.wait_ge(sg("gl_A"), 1)
            act.wait_ge(sg("masks"), 1)
            exps("gl", g)
            A(V.activation(gr[:, :, :], gr[:, :, :], ACT.Silu), "gr_ready")
            for t in range(TT):
                for hp in range(2):
                    o = see(act, ("o", t, hp))
                    for i in range(2):
                        k = t * GH + 2 * hp + i
                        A(V.activation(xn[:, t, (2 * hp + i) * GDV:(2 * hp + i + 1) * GDV], o[:, i * GDV:(i + 1) * GDV],
                                       ACT.Square, accum_out=ssq[:, k:k + 1]), "gssq_ready")
            split_x(quarters("y"))
            hi.upto(pos[("wo", 1), 1] + 2)
            norm(lambda t: [("wo", 0, t), ("wo", 1, t)])

            def ffn(f, conv):
                for j in range(NJ1):
                    hi.upto(pos[f, j, "g"] + NW - 1)
                    gp = see(act, (f, j, "g"))
                    if conv:
                        up = see(act, (f, j, "u"))
                        if j >= 2:
                            act.wait_ge(sg("act_" + f), j - 1)
                        for i, ps in enumerate((gp, up)):
                            for b in range(2):
                                r = i * (F2 // P) + 2 * j + b
                                A(V.activation(f_cu[:, j % 2, (2 * i + b) * S:(2 * i + b + 1) * S], ps[:, b * S:(b + 1) * S],
                                               ACT.Identity, scale=col("tap2", r), bias=col("conv_b", r)), "conv0")
                        act.wait_ge(sg("conv_done"), j + 1)
                        A(V.activation(f_sg[:, j % 2, :], f_cu[:, j % 2, 0:512], ACT.Silu), "silu_" + f)
                    else:
                        if j >= 2:
                            act.wait_ge(sg("act_" + f), j - 1)
                        A(V.activation(f_sg[:, j % 2, :], gp[:, :], ACT.Silu), frees=(f, j, "g"))
                    hi.upto(min(pos[f, j, "g"] + NW, len(pieces) - 1))
                    act.wait_ge(sg("act_" + f), j + 1)
                    A(V.activation(acth[:, j % 2, :], f_act[:, j % 2, :], ACT.Copy), "acth_" + f)
                hi.upto(min(pos[f, NJ1 - 1, "d"] + NW - 1, len(pieces) - 1))

            hi.upto(pos[("wo", 1), 1] + NW)
            split_x(quarters("n1"))
            ffn("f1", False)
            norm(lambda t: [("f1", "acc", t, 0), ("f1", "acc", t, 1)])
            hi.upto(pos["sk", 3])
            split_x(quarters("n2"))
            for b in range(4):
                A(V.activation(skT[:, 2 * b:2 * b + 2, :].rearrange("p h s -> p (h s)"), see(act, ("sk", b))[:, :], ACT.Copy),
                  frees=("sk", b))
                hi.upto(pos["sk", b] + NW)
            for c in range(2):
                for t in range(TT):
                    A(V.activation(sv[:, t, c * 512:(c + 1) * 512], see(act, ("sv", c, t))[:, :], ACT.Copy),
                      frees=("sv", c, t))
                if c == 0:
                    hi.upto(pos[("sv", c), 1] + NW)
            split_x(quarters("n2"), xq)
            hi.upto(pos["sq", 3])
            for b in range(4):
                A(V.activation(sqT[:, 2 * b:2 * b + 2, :].rearrange("p h s -> p (h s)"), see(act, ("sq", b))[:, :],
                               ACT.Copy, scale=float(P) ** -0.5), frees=("sq", b))
                hi.upto(pos["sq", b] + NW)
            for hd in range(SH):
                A(V.activation(sE[:, hd, :], see(act, ("z", hd))[:, 0:384], ACT.Abs), "sb_abs")
            A(V.activation(sE[:, :, :], sE[:, :, :], ACT.Exp, scale=-1.0))
            A(V.activation(sE[:, :, :], sE[:, :, :], ACT.Ln, bias=c_one), "sb_ln")
            for hd in range(SH):
                gone(act, ("stay", hd))
                A(V.activation(sU[:, hd, :], sU[:, hd, :], ACT.Exp), "sb_w")
            split_x(head_pairs)

            def moe_hi(at, c):
                s = (M0 + c) % NW
                src, arrived = moe_raw(c)
                act.wait_ge(arrived, at(16 * (PC // NRX), 16 * (c // NRX + 1)))
                if c >= NW:
                    act.wait_ge(sg("moe_used"), at(PC, c - NW + 1))
                V.activation(wh[:, s, :], src, ACT.Copy).then_inc(sg("hi_moe"), 1)

            def at_first(a, b):
                return b

            for c in range(2):
                released(act, N_PRE - NW + c)
                moe_hi(at_first, c)
            norm(lambda t: [("swo", 0, t), ("swo", 1, t)])
            for c in range(2, NW):
                released(act, N_PRE - NW + c)
                moe_hi(at_first, c)
            act.wait_ge(sg("rt_max"), 1)
            A(V.activation(ex[:, :, :], ex[:, :, :], ACT.Exp), "rt_exp")
            act.dma_start(fgain, IN["final_norm"].rearrange("(a d) -> a d", a=1).to_broadcast([P, D])).then_inc(sg("fg_in"), 16)
            act.wait_ge(sg("more_ready"), 1)

            def xg_hi(value):
                for half in range(2):
                    act.wait_ge(sg("moe_xg"), value + half)
                    V.activation(xgh[:, 4 * half:4 * half + 4, :], xg[:, 4 * half:4 * half + 4, :], ACT.Copy).then_inc(sg("moe_xh"), 1)

            xg_hi(1)

            def experts(at, more_follow):
                for i in range(2):
                    def actT_hi(j):
                        n = NEJ * i + j
                        act.wait_ge(sg("moe_Tfull"), at(2 * NEJ, n + 1))
                        V.activation(eactTh[:, 4 * (n % 2):4 * (n % 2) + 4, :], bank[4][:, :].rearrange("p (k s) -> p k s", k=4),
                                     ACT.Copy).then_inc(sg("moe_actTh"), 1)

                    for q, (kind, j, k) in enumerate(uorder):
                        c = UC * i + q
                        if kind == "g" and k == 1:
                            n = NEJ * i + j
                            act.wait_ge(sg("moe_used"), at(PC, c + 1))
                            act.wait_ge(sg("moe_act"), at(2 * NEJ, n + 1))
                            V.activation(esg[:, n % 2, :], bank[n % 2][:, :], ACT.Silu).then_inc(sg("moe_silu"), 1)
                        tail = (kind, j, k) == ("d", NEJ - 2, 1)
                        if tail:
                            actT_hi(NEJ - 1)
                        if (kind, j, k) == ("d", NEJ - 1, 1):
                            act.wait_ge(sg("moe_used"), at(PC, UC * (i + 1)))
                            V.activation(ey[:, 0:512], bank[5][:, :], ACT.Copy).then_inc(sg("moe_y0"), 1)
                        if c + NW < PC or more_follow:
                            moe_hi(at, c + NW)
                        if kind == "g" and k == 1:
                            if j >= 1:
                                actT_hi(j - 1)
                            if j == 4:
                                act.wait_ge(sg("moe_ohfull"), at(2, i + 1))
                                V.activation(ohT, bank[7][:, 0:S], ACT.Copy).then_inc(sg("moe_ohT"), 1)
                        if tail:
                            xg_hi(at(4, 2 * i + 3))

            hi.more = more = pairs(act, experts)
            hi.upto(N_PRE + 1)
            act.wait_ge(sg("moe_h"), more * 8 + (8 * NPAIR + 1))
            norm(lambda t: [])
            hi.upto(N_PRE + NW - 1)
            act.wait_ge(sg("h_final"), TT)
            norm(lambda t: [])
            nb = 0
            for c0, n, d0 in ((C_AV, AD, 0), (C_BV, BD, 512), (C_BO, BD, 768), (C_CI, 2 * BD, 1024)):
                act.dma_start(tmb[:, d0:d0 + n], IN["b_in_2"][0:1, c0:c0 + n].to_broadcast([P, n])).then_inc(sg("tmb_in"), 16)
                nb += 1
            split_x(quarters("n4"))
            act.wait_ge(sg("c_pre"), 1)
            A(V.activation(m["Q"], m["Q"], ACT.Silu))
            A(V.activation(m["K"], m["E"], ACT.Sigmoid, scale=-1.0), "c_sig")
            A(V.activation(m["qt"], m["W"], ACT.Exp, scale=-1.0))
            A(V.activation(lbp, lbp, ACT.Exp), "c_lb")
            A(V.activation(m["qt"], m["qt"], ACT.Ln, bias=c_one), "c_ln")
            hi.upto(pos["aq", 1])
            act.wait_ge(sg("c_ls"), 1)
            A(V.activation(m["W"], m["W"], ACT.Exp), "c_exp")
            act.wait_ge(sg("c_mixd"), 1)
            A(V.activation(m["W"], m["W"], ACT.Ln), "c_ln2")
            hi.upto(pos["ak", 1])
            act.wait_ge(sg("hl_A"), 1)
            exps("hl", m)
            hi.upto(pos["bqk", 1])
            act.wait_ge(sg("aqk"), 1)
            A(V.activation(rs[:, 0:4 * S], aq.rearrange("p b s -> p (b s)"), ACT.Square))
            A(V.activation(rs[:, 4 * S:8 * S], ak.rearrange("p b s -> p (b s)"), ACT.Square), "qk_sq")
            hi.upto(pos[("bvo",), 1])
            act.wait_ge(sg("row_abs"), 1)
            A(V.activation(cS[0:72, :], cS[0:72, :], ACT.Exp, scale=-1.0))
            A(V.activation(mS[0:72, :], mS[0:72, :], ACT.Exp, scale=-1.0))
            A(V.activation(cS[0:72, :], cS[0:72, :], ACT.Ln, bias=c_one[0:72, :]))
            A(V.activation(mS[0:72, :], mS[0:72, :], ACT.Ln, bias=c_one[0:72, :]), "row_ln")
            for i in range(4):
                A(V.activation(rs[:, i * 512:(i + 1) * 512], see(act, ("qkss", i))[:, :], ACT.Ln, scale=1.0 / HD, bias=c_eps),
                  frees=("qkss", i))
            A(V.activation(rs, rs, ACT.Exp, scale=-0.5), "qk_rstd")
            hi.upto(pos[("w2", 1), 1])
            act.wait_ge(sg("b_pre"), 1)
            A(V.activation(bc[:, :, :], bc[:, :, :], ACT.Silu), "b_act")
            for hd in range(AH):
                act.wait_ge(sg("s_max"), hd + 1)
                for t in range(TT):
                    sl = sS[:, hd % 2, 0:P] if t == 0 else sS[:, hd % 2, P:3 * P]
                    k = hd * TT + t
                    A(V.activation(sl, sl, ACT.Exp, bias=nmx[:, k:k + 1], accum_out=asum[:, k:k + 1]), "s_exp")
                A(V.activation(pTs[:, hd % 2, :], see(act, ("pT", hd))[:, 0:384], ACT.Copy), frees=("pT", hd))
            mt = see(act, "mT")
            A(V.activation(em.rearrange("p (t h) -> p t h", t=TT),
                           mt[:, 0:TT * P].rearrange("p (t r) -> p t r", t=TT)[:, :, 0:BH], ACT.Exp, scale=-1.0), frees="mT")
            for hd in range(BH):
                act.wait_ge(sg("d_arg"), hd + 1)
                A(V.activation(Dm[:, hd % 2, :], Dm[:, hd % 2, :], ACT.Exp), "d_exp")
            act.wait_ge(sg("o_all"), 1)
            A(V.activation(rs, xn.rearrange("p t d -> p (t d)"), ACT.Square), "o_sq")
            A(V.activation(bog[:, :, :], bog[:, :, :], ACT.Sigmoid))
            A(V.activation(cg[:, :, :], cg[:, :, :], ACT.Silu), "gates")
            split_x(quarters("yy"))
            hi.upto(pos[("w2", 1), 1] + 2)
            norm(lambda t: [("w2", 0, t), ("w2", 1, t)])
            hi.upto(pos[("w2", 1), 1] + NW)
            split_x(quarters("n5"))
            ffn("f2", True)

        @block.vector
        def _(dve):
            C = Order(dve, "dve_order")
            V = nc.vector
            n_norm = [0]

            lo = Lo(dve, lambda i: i not in by_pool)

            def split_x(blocks, src=xT):
                for lab, ix in blocks:
                    n_x[0] += 1
                    dve.wait_ge(sg("xh_ready"), n_x[0])
                    C(V.tensor_tensor(xTl[ix], src[ix], xTh[ix].bitcast(F32), ALU.subtract), "xl_ready")

            n_x = [0]

            def norm(n, dsts, meanwhile=None):
                n_norm[0] += 1
                k = n_norm[0]
                dve.wait_ge(sg("ssq_ready"), TT * k)
                C(V.tensor_scalar(ms[:, 0:TT], ssq[:, 0:TT], 1.0 / D, EPS, ALU.mult, ALU.add), "ms_ready")
                rst[0] += 1
                dve.wait_ge(sg("rstd_ready"), rst[0])
                for t in range(TT):
                    C(V.tensor_scalar(xn[:, t, :], h[:, t, :], rstd[:, t:t + 1], None, ALU.mult), "xn_ready")
                if meanwhile is not None:
                    lo.upto(meanwhile)
                evac(n, dsts)

            rst = [0]

            def tick(name=None, frees=None):
                C(V.tensor_copy(scr[:, :], c_one), name, frees)

            def evac(n, dsts, gain=None):
                for t in range(TT):
                    for half in range(2):
                        ps = see(dve, (n, t, half))[:, :].rearrange("p (k s) -> p k s", k=4)
                        for i, (dst, nm, r0) in enumerate(dsts):
                            gains = cols(nm, r0 + 4 * half, 4) if gain is None else gain(half)
                            ins = V.tensor_tensor(dst[:, 4 * half:4 * half + 4, t * P:(t + 1) * P], ps,
                                                  gains.unsqueeze(2).to_broadcast([P, 4, P]), ALU.mult)
                            if i == len(dsts) - 1:
                                C(ins, frees=(n, t, half))
                            else:
                                C(ins)

            def add_h(nm, between):
                for c in range(2):
                    if c:
                        between()
                    for t in range(TT):
                        hs = h[:, t, c * 512:(c + 1) * 512]
                        C(V.tensor_tensor(hs, hs, see(dve, (nm, c, t))[:, :], ALU.add), frees=(nm, c, t))

            def levels(pre, T, cross):
                def half(a, mh, j):
                    return a.rearrange("p (n two m) -> p n two m", two=2, m=mh)[:, :, j, :]

                def qk(i):
                    mh = (LEVELS[1:] + [P])[i]
                    dve.wait_ge(sg(pre + "_exp"), 2 * (i + 1))
                    C(V.tensor_tensor(half(T["qt"], mh, 1), half(T["Q"], mh, 1), half(T["W"], mh, 1), ALU.mult), pre + "_qk")
                    C(V.tensor_tensor(half(T["kt"], mh, 0), half(T["K"], mh, 0), half(T["W"], mh, 0), ALU.mult), pre + "_qk")

                qk(0)
                for i, mh in enumerate(LEVELS):
                    ps = [see(dve, (pre, mh, gg))[:, :].rearrange("p (e s) -> p e s", e=4) for gg in range(2)]
                    if i:
                        qk(i)
                    if mh == P // 2:
                        for gg in range(2):
                            a4 = T["att"][0:mh, gg, :].rearrange("p (e s) -> p e s", e=4)[:, :, mh:P]
                            C(V.tensor_tensor(a4, a4, ps[gg][0:mh, :, mh:P], ALU.add), frees=(pre, mh, gg))
                        continue
                    for gg in range(2):
                        mask = (ident[:, :] if i == 0 else lmask[:, i - 1, :]).unsqueeze(1).to_broadcast([P, 4, P])
                        a4 = T["att"][:, gg, :].rearrange("p (e s) -> p e s", e=4)
                        m4 = T["mt"].rearrange("p (e s) -> p e s", e=4)
                        if i == 0:
                            C(V.tensor_tensor(a4, ps[gg], mask, ALU.mult), frees=(pre, mh, gg))
                        else:
                            C(V.tensor_tensor(m4, ps[gg], mask, ALU.mult), frees=(pre, mh, gg))
                            C(V.tensor_tensor(a4, a4, m4, ALU.add), pre + "_att")
                w = 512 // cross
                for gg in range(cross):
                    C(V.tensor_copy(T["crs"][:, gg * w:(gg + 1) * w], see(dve, (pre, P, gg))[:, 0:w]), frees=(pre, P, gg))

            def bcast(a, shape):
                return a.unsqueeze(len(shape) - 1).to_broadcast(shape)

            dve.wait_ge(sg("const"), 2)
            C(V.tensor_copy(vT[:, 0, 0:V_EARLY], see(dve, ("vec", "early"))[:, 0:V_EARLY]), frees=("vec", "early"))
            norm("n0", [(xT, "attn_norm", 0)], 0)
            split_x(quarters("n0"))
            lo.upto(1)
            C(V.tensor_copy(glrT, see(dve, "glr")[0:GR, 0:S]), frees="glr")
            dve.wait_ge(sg("masks"), 1)
            for b in range(2):
                C(V.tensor_tensor(g["A"][:, b * 512:(b + 1) * 512].rearrange("p (e s) -> p e s", e=2),
                                  see(dve, ("gate", b))[:, :].rearrange("p (e s) -> p e s", e=2),
                                  bcast(cols("gla_b_gate", 2 * b, 2), [P, 2, S]), ALU.add), frees=("gate", b))
            C(V.scalar_tensor_tensor(g["W"], g["A"], -1.0, g["A"], ALU.mult, ALU.max), "gl_abs")
            lo.upto(3)
            dve.wait_ge(sg("gl_ln"), 1)
            C(V.scalar_tensor_tensor(g["A"], g["A"], 0.0, g["W"], ALU.min, ALU.subtract))
            C(V.tensor_scalar(g["A"], g["A"], 1.0 / GATE_NORM, None, ALU.mult), "gl_A")
            for lab in (("q", 0), ("q", 1), ("k", 0), ("k", 1)):
                gone(dve, lab)
            lo.upto(pos[("r", 0), 1])
            for i in range(3):
                r0 = 32 if i == 0 else 0
                C(V.tensor_copy(vT[:, i, r0:V_ROWS[i]], see(dve, ("vec", i))[:, r0:V_ROWS[i]]), frees=("vec", i))
            lo.upto(pos[("wo", 0), 1])
            levels("gl", g, 1)
            dve.wait_ge(sg("gssq_ready"), GH * TT)
            C(V.tensor_scalar(ms[:, 0:GH * TT], ssq[:, 0:GH * TT], 1.0 / GDV, EPS, ALU.mult, ALU.add), "ms_ready")
            rst[0] += 1
            dve.wait_ge(sg("rstd_ready"), rst[0])
            for t in range(TT):
                for hp in range(2):
                    o = see(dve, ("o", t, hp))
                    for i in range(2):
                        hd = 2 * hp + i
                        cs = slice(hd * GDV, (hd + 1) * GDV)
                        ins = V.scalar_tensor_tensor(xn[:, t, cs], o[:, i * GDV:(i + 1) * GDV], rstd[:, t * GH + hd:t * GH + hd + 1],
                                                     gr[:, t, cs], ALU.mult, ALU.mult)
                        if i == 1:
                            C(ins, frees=("o", t, hp))
                        else:
                            C(ins)
            evac("y", [(xT, "gla_head_norm", 0)],
                 lambda half: cols("gla_head_norm", 0, 4))
            split_x(quarters("y"))
            add_h("wo", lambda: lo.upto(pos[("wo", 1), 1] + 2))
            norm("n1", [(xT, "ffn_norm", 0)])
            split_x(quarters("n1"))
            lo.upto(pos[("wo", 1), 1] + NW)

            def ffn(f, conv):
                for j in range(NJ1):
                    lo.upto(pos[f, j, "g"] + NW - 1)
                    if conv:
                        gp, up = see(dve, (f, j, "g")), see(dve, (f, j, "u"))
                        dve.wait_ge(sg("conv0"), 4 * (j + 1))
                        for i, ps in enumerate((gp, up)):
                            for b in range(2):
                                r = i * (F2 // P) + 2 * j + b
                                cu = f_cu[:, j % 2, (2 * i + b) * S:(2 * i + b + 1) * S]
                                x = ps[:, b * S:(b + 1) * S]
                                C(V.scalar_tensor_tensor(cu[:, 1:S], x[:, 0:S - 1], col("tap01", NF2 + r), cu[:, 1:S],
                                                         ALU.mult, ALU.add))
                                ins = V.scalar_tensor_tensor(cu[:, 2:S], x[:, 0:S - 2], col("tap01", r), cu[:, 2:S],
                                                             ALU.mult, ALU.add)
                                if b == 1:
                                    C(ins, frees=(f, j, "gu"[i]))
                                else:
                                    C(ins)
                        tick("conv_done")
                        dve.wait_ge(sg("silu_" + f), j + 1)
                        lhs, rhs = f_sg[:, j % 2, :], f_cu[:, j % 2, 512:1024]
                    else:
                        gone(dve, (f, j, "g"))
                        lhs, rhs = f_sg[:, j % 2, :], see(dve, (f, j, "u"))[:, :]
                    if j >= 2:
                        dve.wait_ge(sg("down_done_" + f), j - 1)
                    ins = V.tensor_tensor(f_act[:, j % 2, :], lhs, rhs, ALU.mult)
                    C(ins, "act_" + f)
                    if not conv:
                        tick(frees=(f, j, "u"))
                    lo.upto(min(pos[f, j, "g"] + NW, len(pieces) - 1))
                    dve.wait_ge(sg("acth_" + f), j + 1)
                    C(V.tensor_tensor(actl[:, j % 2, :], f_act[:, j % 2, :], acth[:, j % 2, :].bitcast(F32), ALU.subtract),
                      "actl_" + f)
                lo.upto(min(pos[f, NJ1 - 1, "d"] + NW - 1, len(pieces) - 1))
                for t in range(TT):
                    for half in range(2):
                        hs = h[:, t, half * 512:(half + 1) * 512]
                        C(V.tensor_tensor(hs, hs, see(dve, (f, "acc", t, half))[:, :], ALU.add), frees=(f, "acc", t, half))

            ffn("f1", False)
            norm("n2", [(xT, "kv_norm", 0), (xq, "attn_norm", KD)])
            split_x(quarters("n2"))
            lo.upto(pos["sq", 1])
            split_x(quarters("n2"), xq)
            lo.upto(pos[("swo", 0), 1])
            dve.wait_ge(sg("masks2"), 1)
            for hd in range(SH):
                z = see(dve, ("z", hd))[:, 0:384]
                dve.wait_ge(sg("sb_abs"), hd + 1)
                C(V.tensor_scalar(sT[:, hd, :], z, 0.0, None, ALU.max))
                C(V.tensor_scalar(sU[:, hd, :], z, 0.0, None, ALU.min), frees=("z", hd))
            lo.upto(pos[("swo", 1), 1])
            dve.wait_ge(sg("sb_ln"), 1)
            C(V.tensor_tensor(sT[:, :, :], sT[:, :, :], sE[:, :, :], ALU.add))
            C(V.tensor_tensor(sT[:, :, :], sT[:, :, :],
                              before3.rearrange("p a s -> p (a s)").unsqueeze(1).to_broadcast([P, SH, 384]), ALU.mult), "sb_keep")
            C(V.tensor_tensor(sU[:, :, :], sU[:, :, :], sE[:, :, :], ALU.subtract))
            for hd in range(SH):
                C(V.tensor_tensor(sU[:, hd, :], sU[:, hd, :], see(dve, ("stay", hd))[:, 0:384], ALU.subtract),
                  frees=("stay", hd))
            for hd in range(SH):
                dve.wait_ge(sg("sb_w"), hd + 1)
                C(V.tensor_tensor(sU[:, hd, :], sU[:, hd, :], before3.rearrange("p a s -> p (a s)"), ALU.mult), "sb_wm")
            for hp in range(SH // 2):
                C(V.tensor_copy(xT[:, 2 * hp:2 * hp + 2, :].rearrange("p k s -> p (k s)"), see(dve, ("so", hp))[:, :]),
                  frees=("so", hp))
            split_x(head_pairs)

            def moe_lo_one(at, c):
                s = (M0 + c) % NW
                dve.wait_ge(sg("hi_moe"), at(PC, c + 1))
                V.tensor_tensor(wl[:, s, 0:LO_V], moe_raw(c)[0][:, 0:LO_V], wh[:, s, 0:LO_V].bitcast(F32),
                                ALU.subtract).then_inc(lo_moe[0], 1)

            def at_first(a, b):
                return b

            add_h("swo", lambda: [moe_lo_one(at_first, c) for c in range(2)])
            norm("n3", [(xT, "ffn_norm", KD)])
            C(V.tensor_copy(lg, see(dve, "lg")[:, 0:TT * NE].rearrange("p (t e) -> p t e", t=TT)), frees="lg")
            for t in range(TT):
                le = lg[:, t, :].unsqueeze(2).to_broadcast([P, NE, NE])
                lj = lg[:, t, :].unsqueeze(1).to_broadcast([P, NE, NE])
                C(V.tensor_tensor(cmp1[:, t], lj, le, ALU.is_gt))
                C(V.tensor_tensor(cmp2[:, t], lj, le, ALU.is_equal))
                C(V.tensor_tensor(cmp2[:, t], cmp2[:, t], tri8[:, :, :], ALU.mult))
                C(V.tensor_tensor(cmp1[:, t], cmp1[:, t], cmp2[:, t], ALU.add))
                C(V.tensor_reduce(rank[:, t, :], cmp1[:, t], AX.X, ALU.add))
            C(V.tensor_scalar(selx, rank, 1.5, None, ALU.is_lt), "rt_sel")
            C(V.tensor_reduce(mx, lg, AX.X, ALU.max))
            C(V.tensor_tensor(ex, lg, bcast(mx, [P, TT, NE]), ALU.subtract), "rt_max")
            dve.wait_ge(sg("rt_exp"), 1)
            C(V.tensor_tensor(ex, ex, selx, ALU.mult))
            C(V.tensor_reduce(exs, ex, AX.X, ALU.add))
            C(V.reciprocal(exs, exs))
            C(V.memset(pm, -1.0))
            C(V.memset(gt, 0.0))
            for t in range(TT):
                for r in range(2):
                    C(V.tensor_scalar(gt[:, r * NE:(r + 1) * NE, t], ex[:, t, :], exs[:, t:t + 1], None, ALU.mult))
            pp = see(dve, "pos")[:, 0:TT * NE].rearrange("p (t e) -> p t e", t=TT)
            C(V.scalar_tensor_tensor(lg, pp, 1.0, selx, ALU.add, ALU.mult), frees="pos")
            for t in range(TT):
                for r in range(2):
                    C(V.tensor_scalar(pm[:, r * NE:(r + 1) * NE, t], lg[:, t, :], -1.0 - P * r, None, ALU.add))
            C(V.tensor_reduce(cmax[0:1, 0:1], see(dve, "cnt")[0:1, 0:NE], AX.X, ALU.max), frees="cnt")
            C(V.tensor_scalar(cmax[0:1, 1:2], cmax[0:1, 0:1], P + 0.5, float(NPAIR), ALU.is_gt, ALU.mult))
            C(V.tensor_copy(more_i[0:1, 0:1], cmax[0:1, 1:2]), "more_ready")

            iota2 = iota[:, :].unsqueeze(1).to_broadcast([P, TT, P])

            def onehot(u, value):
                pmu = pm[:, bass.ds(u, 1), :].rearrange("p a t -> p (a t)")
                gtu = gt[:, bass.ds(u, 1), :].rearrange("p a t -> p (a t)")
                V.tensor_tensor(oh, iota2, pmu.unsqueeze(2).to_broadcast([P, TT, P]), ALU.is_equal).then_inc(sg("moe_oh"), 1)
                dve.wait_ge(sg("moe_oh"), value)
                V.tensor_tensor(ohg, oh, gtu.unsqueeze(2).to_broadcast([P, TT, P]), ALU.mult).then_inc(sg("moe_oh"), 1)
                dve.wait_ge(sg("moe_oh"), value + 1)

            def gather_out(half, b, value):
                dve.wait_ge(sg("moe_xgfull"), value)
                V.tensor_tensor(xg[:, 4 * half:4 * half + 4, :], b[:, :].rearrange("p (k s) -> p k s", k=4),
                                cols("ffn_norm", KD + 4 * half, 4).unsqueeze(2).to_broadcast([P, 4, P]),
                                ALU.mult).then_inc(sg("moe_xg"), 1)

            def xg_lo(half, value):
                hs = slice(4 * half, 4 * half + 4)
                dve.wait_ge(sg("moe_xh"), value)
                V.tensor_tensor(xgl[:, hs, :], xg[:, hs, :], xgh[:, hs, :].bitcast(F32), ALU.subtract).then_inc(sg("moe_xl"), 1)

            onehot(0, 1)
            gather_out(0, bank[7], 1)
            gather_out(1, bank[0], 2)
            xg_lo(0, 1)
            xg_lo(1, 2)
            for c in range(2, NW):
                moe_lo_one(at_first, c)
            tick("moe_act")
            tick("moe_act")
            tick("moe_h")

            def experts(at, more_follow):
                for i in range(2):
                    def actT_lo(j):
                        n = NEJ * i + j
                        ks = slice(4 * (n % 2), 4 * (n % 2) + 4)
                        dve.wait_ge(sg("moe_actTh"), at(2 * NEJ, n + 1))
                        V.tensor_tensor(eactTl[:, ks, :], bank[4][:, :].rearrange("p (k s) -> p k s", k=4),
                                        eactTh[:, ks, :].bitcast(F32), ALU.subtract).then_inc(sg("moe_actTl"), 1)

                    def weights_lo(q):
                        if UC * i + q + NW < PC or more_follow:
                            moe_lo_one(at, UC * i + q + NW)

                    for q, (kind, j, k) in enumerate(uorder[:-2]):
                        tail = (kind, j, k) == ("d", NEJ - 2, 1)
                        if tail:
                            gather_out(0, bank[7], at(4, 2 * i + 3))
                            actT_lo(NEJ - 1)
                            gather_out(1, bank[(NEJ * (i + 1)) % 2], at(4, 2 * i + 4))
                        weights_lo(q)
                        if tail:
                            for half in range(2):
                                xg_lo(half, at(4, 2 * i + 3 + half))
                        if kind == "g" and k == 1 and j >= 1:
                            actT_lo(j - 1)
                        if kind == "u" and k == 1:
                            n = NEJ * i + j
                            dve.wait_ge(sg("moe_used"), at(PC, UC * i + q + 1))
                            dve.wait_ge(sg("moe_silu"), at(2 * NEJ, n + 1))
                            V.tensor_tensor(eact[:, n % 2, :], esg[:, n % 2, :], bank[2 + n % 2][:, :],
                                            ALU.mult).then_inc(sg("moe_act"), 1)
                            if j == 4:
                                dve.wait_ge(sg("moe_ohfull"), at(2, i + 1))
                                onehot(at(2, i + 1), at(4, 2 * i + 3))
                    dve.wait_ge(sg("moe_used"), at(PC, UC * (i + 1)))
                    V.tensor_copy(ey[:, 512:1024], bank[6][:, :]).then_inc(sg("moe_y1"), 1)
                    for q in range(4):
                        t, half = q // 2, q % 2
                        dve.wait_ge(sg("moe_scfull"), at(8, 4 * i + q + 1))
                        hs = h[:, t, half * 512:(half + 1) * 512]
                        V.tensor_tensor(hs, hs, bank[7 if q % 2 == 0 else 4][:, :], ALU.add).then_inc(sg("moe_h"), 1)
                    weights_lo(UC - 2)
                    weights_lo(UC - 1)

            more = pairs(dve, experts)
            lo.upto(N_PRE + 1)
            dve.wait_ge(sg("moe_h"), more * 8 + (8 * NPAIR + 1))
            n_norm[0] += 1
            dve.wait_ge(sg("ssq_ready"), TT * n_norm[0])
            C(V.tensor_scalar(ms[:, 0:TT], ssq[:, 0:TT], 1.0 / D, EPS, ALU.mult, ALU.add), "ms_ready")
            rst[0] += 1
            dve.wait_ge(sg("rstd_ready"), rst[0])
            dve.wait_ge(sg("fg_in"), 16)
            for t in range(TT):
                C(V.scalar_tensor_tensor(h[:, t, :], h[:, t, :], rstd[:, t:t + 1], fgain, ALU.mult, ALU.mult), "h_final")
            norm("n4", [(xT, "norm_mix_g_2", 0)])
            split_x(quarters("n4"))
            lo.upto(N_PRE + NW - 1)
            dve.wait_ge(sg("mix_zero"), 1)

            def fm_bias(dst, lab, nm, r0):
                C(V.tensor_tensor(dst, see(dve, lab)[:, :].rearrange("p (e s) -> p e s", e=2),
                                  bcast(cols(nm, r0, 2), [P, 2, S]), ALU.add), frees=lab)

            q3 = m["Q"].rearrange("p (e s) -> p e s", e=2)
            f3 = m["E"].rearrange("p (e s) -> p e s", e=2)
            fm_bias(q3, ("cqf", 0), "cqf_b", 0)
            fm_bias(f3, ("cqf", 1), "cqf_b", 2)
            lbl = cols("lb_logits_2", 0, 2)
            C(V.tensor_tensor(lbp, lbl, lbl, ALU.subtract))
            C(V.scalar_tensor_tensor(m["W"], m["E"], -1.0, m["E"], ALU.mult, ALU.max), "c_pre")
            dve.wait_ge(sg("c_lb"), 1)
            C(V.reciprocal(lb1, lbp))
            C(V.tensor_tensor(lbp, lbp, lb1, ALU.mult))
            C(V.tensor_tensor(lbp, lbp, lbp, ALU.subtract))
            C(V.tensor_scalar(lbp, lbp, 0.0, None, ALU.max))
            C(V.tensor_scalar(lb1, lbp, -1.0, 1.0, ALU.mult, ALU.add))
            dve.wait_ge(sg("c_ln"), 1)
            C(V.scalar_tensor_tensor(m["A"], m["E"], 0.0, m["qt"], ALU.min, ALU.subtract))
            C(V.tensor_scalar(m["W"], m["A"], -1.0, 80.0, ALU.mult, ALU.min), "c_ls")
            dve.wait_ge(sg("c_exp"), 1)
            for b in range(2):
                bs = slice(b * S, (b + 1) * S)
                C(V.tensor_scalar(m["W"][:, bs], m["W"][:, bs], lbp[:, b:b + 1], lb1[:, b:b + 1], ALU.mult, ALU.add))
                C(V.tensor_scalar(m["K"][:, bs], m["K"][:, bs], lb1[:, b:b + 1], None, ALU.mult))
            tick("c_mixd")
            dve.wait_ge(sg("c_ln2"), 1)
            C(V.tensor_tensor(m["A"], m["A"], m["W"], ALU.add))
            C(V.memset(m["E"], 0.0))
            C(V.memset(m["qt"], 0.0), "hl_A")
            dve.wait_ge(sg("tmb_in"), 64)
            for t in range(TT):
                ps = see(dve, ("cig", t))
                C(V.tensor_tensor(ci[:, t, :], ps[:, 0:BD], tmb[:, 1024:1024 + BD], ALU.add), "ci")
                C(V.tensor_tensor(cg[:, t, :], ps[:, BD:2 * BD], tmb[:, 1280:1280 + BD], ALU.add), frees=("cig", t))
            lo.upto(pos["ak", 1])
            levels("hl", m, 2)
            for t in range(TT):
                C(V.tensor_copy(o_all[:, t, AD + BD:AD + 2 * BD], see(dve, ("co", t))[:, 0:BD]), frees=("co", t))
            for dst, nm in ((aq, "aq"), (ak, "ak")):
                for b in range(2):
                    fm_bias(dst[:, 2 * b:2 * b + 2, :], (nm, b), nm + "_b", 2 * b)
                    lo.upto(pos[nm, b] + NW)
            C(V.tensor_copy(gq[:, 1:2], vT[:, 0, R_G + 1:R_G + 2]))
            C(V.tensor_scalar(gq[:, 0:1], vT[:, 0, R_G:R_G + 1], HD ** -0.5, None, ALU.mult), "aqk")
            for t in range(TT):
                C(V.tensor_tensor(av[:, t, :], see(dve, ("av", t))[:, :], tmb[:, 0:AD], ALU.add), frees=("av", t))
            lo.upto(pos[("bvo",), 1])
            for b in range(2):
                fm_bias(bz[:, 2 * b:2 * b + 2, :], ("bqk", b), "bqk_b", 2 * b)
            for t in range(TT):
                ps = see(dve, ("bvo", t))
                C(V.tensor_tensor(bv[:, t, :, 0:HD], ps[:, 0:BD].rearrange("p (h n) -> p h n", h=BH),
                                  tmb[:, 512:512 + BD].rearrange("p (h n) -> p h n", h=BH), ALU.add), "bv")
                C(V.tensor_tensor(bog[:, t, :], ps[:, BD:2 * BD], tmb[:, 768:768 + BD], ALU.add), frees=("bvo", t))
            rw = slice(0, 72)
            for nm in ("cf", "bi", "bf"):
                see(dve, nm)
            for a in (cS, ncS, iF, nM, mS):
                C(V.memset(a, 0.0))
            for nm, dst, i in (("cf", ncS, 0), ("bi", iF, 1), ("bf", nM, 2)):
                C(V.tensor_scalar(dst[rw, :], see(dve, nm)[rw, 0:S], vT[rw, 0, R_G + 2 + i:R_G + 3 + i], None, ALU.add), frees=nm)
            C(V.scalar_tensor_tensor(cS[rw, :], ncS[rw, :], -1.0, ncS[rw, :], ALU.mult, ALU.max))
            C(V.scalar_tensor_tensor(mS[rw, :], nM[rw, :], -1.0, nM[rw, :], ALU.mult, ALU.max), "row_abs")
            for b in range(4):
                C(V.tensor_scalar(bc[:, b, :], bz[:, b, :], col("b_conv", 12 + b), None, ALU.mult))
                for k in range(1, 4):
                    C(V.scalar_tensor_tensor(bc[:, b, k:S], bz[:, b, 0:S - k], col("b_conv", 4 * (3 - k) + b), bc[:, b, k:S],
                                             ALU.mult, ALU.add))
            tick("b_pre")
            dve.wait_ge(sg("row_ln"), 1)
            C(V.scalar_tensor_tensor(cS[rw, :], ncS[rw, :], 0.0, cS[rw, :], ALU.min, ALU.subtract))
            C(V.scalar_tensor_tensor(mS[rw, :], nM[rw, :], 0.0, mS[rw, :], ALU.min, ALU.subtract))
            C(V.memset(row1, 1.0))
            C(V.tensor_tensor_scan(ncS[rw, :], row1[rw, :], cS[rw, :], 0.0, ALU.mult, ALU.add))
            C(V.tensor_tensor_scan(nM[rw, :], row1[rw, :], mS[rw, :], 0.0, ALU.mult, ALU.add))
            C(V.tensor_copy(cS[rw, :], ncS[rw, :]))
            C(V.tensor_scalar(ncS[rw, :], ncS[rw, :], -1.0, None, ALU.mult), "c_rows")
            C(V.tensor_tensor(iF[rw, :], iF[rw, :], nM[rw, :], ALU.subtract))
            C(V.tensor_tensor_scan(row1[rw, :], iF[rw, :], iF[rw, :], -3.0e38, ALU.max, ALU.max))
            C(V.tensor_tensor(mS[rw, :], nM[rw, :], row1[rw, :], ALU.add))
            C(V.tensor_scalar(nM[rw, :], row1[rw, :], -1.0, None, ALU.mult), "m_rows")
            dve.wait_ge(sg("qk_rstd"), 1)
            for dst, i in ((aq, 0), (ak, 1)):
                d2 = dst.rearrange("p b s -> p (b s)")
                C(V.scalar_tensor_tensor(d2, d2, gq[:, i:i + 1], rs[:, i * 4 * S:(i + 1) * 4 * S], ALU.mult, ALU.mult), "qk_n")
            r3 = rowneg3.rearrange("p a s -> p (a s)")

            for hd in range(AH):
                if hd >= 2:
                    see(dve, ("pT", hd - 2))
                C(V.tensor_tensor(sS[:, hd % 2, :], see(dve, ("s", hd))[:, 0:384], r3, ALU.add), frees=("s", hd))
                C(V.tensor_reduce(nmx[:, hd * TT:hd * TT + 1], sS[:, hd % 2, 0:P], AX.X, ALU.max, negate=True))
                C(V.tensor_reduce(nmx[:, hd * TT + 1:hd * TT + 2], sS[:, hd % 2, P:3 * P], AX.X, ALU.max, negate=True), "s_max")
            dve.wait_ge(sg("s_exp"), AH * TT)
            C(V.reciprocal(arec, asum))
            for t in range(TT):
                C(V.tensor_tensor(o_all[:, t, 0:AD].rearrange("p (h n) -> p h n", h=AH),
                                  see(dve, ("ao", t))[:, :].rearrange("p (h n) -> p h n", h=AH),
                                  bcast(arec.rearrange("p (h t) -> p h t", t=TT)[:, :, t], [P, AH, HD]), ALU.mult), frees=("ao", t))
            c3 = colneg3.rearrange("p a s -> p (a s)")
            for hd in range(BH):
                C(V.tensor_tensor(Dm[:, hd % 2, :], see(dve, ("P2", hd))[:, 0:384], c3, ALU.add), "d_arg")
                p1 = see(dve, ("P1", hd))[:, 0:384]
                dve.wait_ge(sg("d_exp"), hd + 1)
                if hd >= 2:
                    dve.wait_ge(sg("b_pv"), hd - 1)
                C(V.scalar_tensor_tensor(sS[:, hd % 2, :], p1, HD ** -0.5, Dm[:, hd % 2, :], ALU.mult, ALU.mult), "d_w")
                tick(frees=("P2", hd))
                tick(frees=("P1", hd))
            gone(dve, "mT")
            for t in range(TT):
                ps = see(dve, ("bo", t))[:, 0:BH * 65].rearrange("p (h n) -> p h n", h=BH)
                dn = den[:, t * BH:(t + 1) * BH]
                C(V.tensor_copy(dn, ps[:, :, HD]))
                C(V.scalar_tensor_tensor(dn, dn, -1.0, dn, ALU.mult, ALU.max))
                C(V.tensor_tensor(dn, dn, em[:, t * BH:(t + 1) * BH], ALU.max))
                C(V.reciprocal(dn, dn))
                C(V.tensor_tensor(o_all[:, t, AD:AD + BD].rearrange("p (h n) -> p h n", h=BH), ps[:, :, 0:HD],
                                  bcast(dn, [P, BH, HD]), ALU.mult), frees=("bo", t))
            tick("o_all")
            dve.wait_ge(sg("o_sq"), 1)
            C(V.tensor_reduce(ssq[:, 0:32], rs.rearrange("p (g n) -> p g n", n=HD), AX.X, ALU.add))
            C(V.tensor_scalar(ms[:, 0:32], ssq[:, 0:32], 1.0 / HD, EPS, ALU.mult, ALU.add), "ms_ready")
            rst[0] += 1
            dve.wait_ge(sg("rstd_ready"), rst[0])
            o3 = o_all.rearrange("p t (g n) -> p (t g) n", n=HD)
            C(V.tensor_tensor(o3, o3, bcast(rstd[:, 0:32], [P, 32, HD]), ALU.mult))
            dve.wait_ge(sg("gates"), 1)
            C(V.tensor_tensor(o_all[:, :, AD:AD + BD], o_all[:, :, AD:AD + BD], bog, ALU.mult))
            C(V.tensor_tensor(o_all[:, :, AD + BD:AD + 2 * BD], o_all[:, :, AD + BD:AD + 2 * BD], cg, ALU.mult), "o_done")
            evac("yy", [(xT, "out_g_2", 0)])
            split_x(quarters("yy"))
            add_h("w2", lambda: lo.upto(pos[("w2", 1), 1] + 2))
            norm("n5", [(xT, "norm_ffn_g_2", 0)])
            split_x(quarters("n5"))
            lo.upto(pos[("w2", 1), 1] + NW)
            ffn("f2", True)

        @block.tensor
        def _(pe):
            T = nc.tensor

            def take(label):
                b, n = turns[label]
                if n:
                    pe.wait_ge(freed[b], n)
                return bank[b]

            def done(ins, label):
                ins.then_inc(full[turns[label][0]], 1)

            n_xn = [0]

            def transposes(n):
                for t in range(TT):
                    for half in range(2):
                        ps = take((n, t, half))
                        for k in range(4):
                            kk = 4 * half + k
                            ins = T.transpose(ps[:, k * P:(k + 1) * P], xn[:, t, kk * P:(kk + 1) * P], ident[:, :])
                        done(ins, (n, t, half))
                for t in range(TT):
                    for half in range(2):
                        gone(pe, (n, t, half))

            def x_split():
                n_x[0] += 4
                pe.wait_ge(sg("xl_ready"), n_x[0])

            n_x = [0]

            def norm(n):
                n_xn[0] += TT
                pe.wait_ge(sg("xn_ready"), n_xn[0])
                transposes(n)

            def mm3(o, xh, xl, yh, yl, first, last):
                T.matmul(o, xh, yh, start=first, stop=False)
                T.matmul(o, xh, yl, start=False, stop=False)
                return T.matmul(o, xl, yh, start=False, stop=last)

            def fm(label):
                ps, i = take(label), pos[label]
                split_done(pe, i)
                h_, l_ = of(wh, i, KD), of(wl, i, KD)
                for j in range(2):
                    js = slice(j * P, (j + 1) * P)
                    for k in range(KD):
                        ins = mm3(ps[:, j * S:(j + 1) * S], h_[:, k, js], l_[:, k, js], xTh[:, k, :], xTl[:, k, :],
                                  k == 0, k == KD - 1)
                done(ins, label)

            def tm(nm):
                for t in range(TT):
                    ts = slice(t * P, (t + 1) * P)
                    ps = take(nm + (t,))
                    for half in range(2):
                        i = pos[nm, half]
                        split_done(pe, i)
                        h_, l_ = of(wh, i, 4), of(wl, i, 4)
                        for k in range(4):
                            kk = 4 * half + k
                            ins = mm3(ps[:, :], xTh[:, kk, ts], xTl[:, kk, ts], h_[:, k, :], l_[:, k, :],
                                      kk == 0, kk == KD - 1)
                    done(ins, nm + (t,))

            def out_proj(nm):
                x_split()
                for c in range(2):
                    tm((nm, c))

            def levels(pre, T_, heads):
                ent = [[(h_, st) for h_ in range(4)] for st in range(2)] if heads else \
                      [[(2 * b + hf, st) for st in range(2) for b in range(2)] for hf in range(2)]

                def operands(hd, lo, hi, level):
                    rws = slice(0, P) if heads else slice(64 * (hd % 2), 64 * (hd % 2) + 64)
                    o = (hd if heads else hd // 2) * S
                    kk, qq = (T_["K"], T_["Q"]) if level == 0 else (T_["kt"], T_["qt"])
                    return kk[rws, o + lo * P:o + (lo + 1) * P], qq[rws, o + hi * P:o + (hi + 1) * P]

                for i, mh in enumerate(LEVELS):
                    if i:
                        pe.wait_ge(sg(pre + "_qk"), 2 * i)
                    for gg in range(2):
                        ps = take((pre, mh, gg))
                        for e, (hd, st) in enumerate(ent[gg]):
                            kk, qq = operands(hd, st, st, i)
                            if mh == P // 2:
                                ins = T.matmul(ps[0:mh, e * P + mh:(e + 1) * P], kk[:, 0:mh], qq[:, mh:P], start=True, stop=True)
                            else:
                                ins = T.matmul(ps[:, e * P:(e + 1) * P], kk, qq, start=True, stop=True)
                        done(ins, (pre, mh, gg))
                pe.wait_ge(sg(pre + "_qk"), 2 * len(LEVELS))
                for gg in range(1 if heads else 2):
                    ps = take((pre, P, gg))
                    hds = range(4) if heads else [2 * b + gg for b in range(2)]
                    for e, hd in enumerate(hds):
                        kk, qq = operands(hd, 0, 1, 1)
                        ins = T.matmul(ps[:, e * P:(e + 1) * P], kk, qq, start=True, stop=True)
                    done(ins, (pre, P, gg))
                pe.wait_ge(sg(pre + "_att"), 2 * (len(LEVELS) - 2))
                for gg in range(2):
                    gone(pe, (pre, P // 2, gg))
                for gg in range(1 if heads else 2):
                    gone(pe, (pre, P, gg))

            pe.wait_ge(sg("const"), 1)
            pe.wait_ge(sg("vec_first"), 16 * N_EARLY)
            done(T.transpose(take(("vec", "early"))[:, 0:V_EARLY], vrow[0:V_EARLY, 0, :], ident[0:V_EARLY, 0:V_EARLY]),
                 ("vec", "early"))
            norm("n0")
            pe.wait_ge(sg("glr_in"), 32)
            ps = take("glr")
            for k in range(KD):
                ins = T.matmul(ps[0:GR, 0:S], wglr[:, k, :], xT[:, k, :], start=(k == 0), stop=(k == KD - 1))
            done(ins, "glr")
            gone(pe, "glr")
            for b in range(2):
                ps = take(("gate", b))
                for j in range(2):
                    hd = 2 * b + j
                    ins = T.matmul(ps[:, j * S:(j + 1) * S], wgu[:, hd * P:(hd + 1) * P], glrT, start=True, stop=True)
                done(ins, ("gate", b))
            x_split()
            for nm in ("q", "k"):
                for b in range(2):
                    fm((nm, b))
            for nm in "vr":
                for c in range(2):
                    tm((nm, c))
                if nm == "v":
                    pe.wait_ge(sg("vec_in"), 16 * N_VEC)
                    for i in range(3):
                        n = V_ROWS[i]
                        done(T.transpose(take(("vec", i))[:, 0:n], vrow[0:n, i, :], ident[0:n, 0:n]), ("vec", i))
            for lab in (("q", 0), ("q", 1), ("k", 0), ("k", 1)):
                gone(pe, lab)
            levels("gl", g, True)
            for c in range(2):
                for t in range(TT):
                    gone(pe, ("v", c, t))
            for t in range(TT):
                for hp in range(2):
                    ps = take(("o", t, hp))
                    for i in range(2):
                        hd = 2 * hp + i
                        cs = slice(hd * GDV, (hd + 1) * GDV)
                        o = ps[:, i * GDV:(i + 1) * GDV]
                        if t:
                            T.matmul(o, g["crs"][:, hd * P:(hd + 1) * P], gv[:, 0, cs], start=True, stop=False)
                        ins = T.matmul(o, g["att"][:, t, hd * P:(hd + 1) * P], gv[:, t, cs], start=(t == 0), stop=True)
                    done(ins, ("o", t, hp))
            for t in range(TT):
                for hp in range(2):
                    gone(pe, ("o", t, hp))
            transposes("y")
            out_proj("wo")
            norm("n1")
            x_split()

            def ffn(f):
                def down(j):
                    pe.wait_ge(sg("actl_" + f), j + 1)
                    i = pos[f, j, "d"]
                    split_done(pe, i)
                    h_, l_ = of(wh, i, 2), of(wl, i, 2)
                    for t in range(TT):
                        for half in range(2):
                            lab = (f, "acc", t, half)
                            ps = take(lab) if j == 0 else bank[turns[lab][0]]
                            hs = slice(half * 512, (half + 1) * 512)
                            for b in range(2):
                                ts = slice(b * S + t * P, b * S + (t + 1) * P)
                                ins = mm3(ps[:, :], acth[:, j % 2, ts], actl[:, j % 2, ts], h_[:, b, hs], l_[:, b, hs],
                                          j == 0 and b == 0, j == NJ1 - 1 and b == 1)
                            if j == NJ1 - 1:
                                done(ins, lab)
                    if j < NJ1 - 1:
                        ins.then_inc(sg("down_done_" + f), 1)

                for j in range(NJ1):
                    fm((f, j, "g"))
                    fm((f, j, "u"))
                    if j:
                        down(j - 1)
                down(NJ1 - 1)

            ffn("f1")
            norm("n2")
            x_split()
            for b in range(4):
                fm(("sk", b))
            for c in range(2):
                tm(("sv", c))
            x_split()
            for b in range(4):
                fm(("sq", b))
            for b in range(4):
                gone(pe, ("sk", b))
                gone(pe, ("sq", b))
            for hd in range(SH):
                ps = take(("z", hd))
                T.matmul(ps[:, 0:S], skT[:, hd, 0:P], sqT[:, hd, :], start=True, stop=True)
                done(T.matmul(ps[:, S:384], skT[:, hd, P:S], sqT[:, hd, P:S], start=True, stop=True), ("z", hd))
            pe.wait_ge(sg("sb_keep"), 1)
            pe.wait_ge(sg("masks2"), 1)
            for hd in range(SH):
                ps = take(("stay", hd))
                T.matmul(ps[:, 0:P], after[:, :], sT[:, hd, 0:P], start=True, stop=True)
                T.matmul(ps[:, P:S], after[:, :], sT[:, hd, P:S], start=True, stop=False)
                T.matmul(ps[:, P:S], before3[:, 1, :], sT[:, hd, S:384], start=False, stop=True)
                done(T.matmul(ps[:, S:384], after[:, :], sT[:, hd, S:384], start=True, stop=True), ("stay", hd))
            for c in range(2):
                for t in range(TT):
                    gone(pe, ("sv", c, t))
            for hp in range(SH // 2):
                ps = take(("so", hp))
                for i in range(2):
                    hd = 2 * hp + i
                    pe.wait_ge(sg("sb_wm"), hd + 1)
                    vs = slice(hd * P, (hd + 1) * P)
                    T.matmul(ps[:, i * S:i * S + P], sv[:, 0, vs], sU[:, hd, 0:P], start=True, stop=True)
                    T.matmul(ps[:, i * S + P:(i + 1) * S], sv[:, 0, vs], sU[:, hd, P:S], start=True, stop=False)
                    ins = T.matmul(ps[:, i * S + P:(i + 1) * S], sv[:, 1, vs], sU[:, hd, S:384], start=False, stop=True)
                done(ins, ("so", hp))
            for hp in range(SH // 2):
                gone(pe, ("so", hp))
            out_proj("swo")
            norm("n3")
            pe.wait_ge(sg("rt_in"), 16)
            ps = take("lg")
            for t in range(TT):
                for k in range(KD):
                    ins = T.matmul(ps[:, t * NE:(t + 1) * NE], xT[:, k, t * P:(t + 1) * P], wrt[:, k, :],
                                   start=(k == 0), stop=(k == KD - 1))
            done(ins, "lg")
            pe.wait_ge(sg("rt_sel"), 1)
            ps = take("pos")
            T.matmul(ps[:, 0:NE], before3[:, 0, :], selx[:, 0, :], start=True, stop=True)
            T.matmul(ps[:, NE:2 * NE], before3[:, 1, :], selx[:, 0, :], start=True, stop=False)
            done(T.matmul(ps[:, NE:2 * NE], before3[:, 0, :], selx[:, 1, :], start=False, stop=True), "pos")
            ps = take("cnt")
            T.matmul(ps[:, 0:NE], before3[:, 1, :], selx[:, 0, :], start=True, stop=False)
            done(T.matmul(ps[:, 0:NE], before3[:, 1, :], selx[:, 1, :], start=False, stop=True), "cnt")

            for b in range(8):
                pe.wait_ge(freed[b], uses_before_moe[b])
            pe.wait_ge(sg("more_ready"), 1)
            def gather(half, b):
                for k in range(4):
                    kk = 4 * half + k
                    for t in range(TT):
                        ins = T.matmul(b[:, k * P:(k + 1) * P], xn[:, t, kk * P:(kk + 1) * P], oh[:, t, :],
                                       start=(t == 0), stop=(t == TT - 1))
                ins.then_inc(sg("moe_xgfull"), 1)

            pe.wait_ge(sg("moe_oh"), 1)
            gather(0, bank[7])
            gather(1, bank[0])

            def used(ins):
                ins.then_inc(sg("moe_used"), 1)

            def experts(at, more_follow):
                def here(c, k):
                    moe_split(pe, at, c)
                    return of(wh, M0 + c, k), of(wl, M0 + c, k)

                for i in range(2):
                    def gate_up(b, kind, j):
                        for half in range(2):
                            h_, l_ = here(UC * i + upos[kind, j, half], 4)
                            for k in range(4):
                                kk = 4 * half + k
                                ins = mm3(b[:, :], xgh[:, kk, :], xgl[:, kk, :], h_[:, k, :], l_[:, k, :], kk == 0, kk == KD - 1)
                            used(ins)

                    def transposed(j):
                        n = NEJ * i + j
                        pe.wait_ge(sg("moe_act"), at(2 * NEJ, n + 3))
                        for k in range(4):
                            ins = T.transpose(bank[4][:, k * P:(k + 1) * P], eact[:, n % 2, k * P:(k + 1) * P], ident[:, :])
                        ins.then_inc(sg("moe_Tfull"), 1)

                    def down(j):
                        n = NEJ * i + j
                        pe.wait_ge(sg("moe_actTl"), at(2 * NEJ, n + 1))
                        for part in range(2):
                            h_, l_ = here(UC * i + upos["d", j, part], 2)
                            for k in range(2):
                                kk = 4 * (n % 2) + 2 * part + k
                                for half in range(2):
                                    hs = slice(half * 512, (half + 1) * 512)
                                    ins = mm3(bank[5 + half][:, :], eactTh[:, kk, :], eactTl[:, kk, :], h_[:, k, hs], l_[:, k, hs],
                                              j == 0 and part == 0 and k == 0, j == NEJ - 1 and part == 1 and k == 1)
                            used(ins)

                    pe.wait_ge(sg("moe_xl"), at(4, 2 * i + 2))
                    for j in range(NEJ):
                        n = NEJ * i + j
                        pe.wait_ge(sg("moe_act"), at(2 * NEJ, n + 1))
                        gate_up(bank[n % 2], "g", j)
                        if j == 1:
                            pe.wait_ge(sg("moe_h"), at(8, 4 * i + 1))
                        if j:
                            transposed(j - 1)
                        gate_up(bank[2 + n % 2], "u", j)
                        if j:
                            down(j - 1)
                        if j == 3:
                            pe.wait_ge(sg("moe_oh"), at(4, 2 * i + 2))
                            for t in range(TT):
                                ins = T.transpose(bank[7][:, t * P:(t + 1) * P], ohg[:, t, :], ident[:, :])
                            ins.then_inc(sg("moe_ohfull"), 1)
                    pe.wait_ge(sg("moe_oh"), at(4, 2 * i + 3))
                    pe.wait_ge(sg("moe_ohT"), at(2, i + 1))
                    gather(0, bank[7])
                    transposed(NEJ - 1)
                    gather(1, bank[(NEJ * (i + 1)) % 2])
                    down(NEJ - 1)
                    pe.wait_ge(sg("moe_y0"), at(2, i + 1))
                    pe.wait_ge(sg("moe_y1"), at(2, i + 1))
                    pe.wait_ge(sg("moe_xg"), at(4, 2 * i + 4))
                    for q in range(4):
                        t, half = q // 2, q % 2
                        if q >= 2:
                            pe.wait_ge(sg("moe_h"), at(8, 4 * i + q))
                        T.matmul(bank[7 if q % 2 == 0 else 4][:, :], ohT[:, t * P:(t + 1) * P],
                                 ey[:, half * 512:(half + 1) * 512], start=True, stop=True).then_inc(sg("moe_scfull"), 1)

            more = pairs(pe, experts)
            pe.wait_ge(sg("moe_h"), more * 8 + (8 * NPAIR + 1))
            norm("n4")
            x_split()
            for b in range(2):
                fm(("cqf", b))
            tm(("cig",))
            pe.wait_ge(sg("hl_A"), 1)
            levels("hl", m, False)
            pe.wait_ge(sg("ci"), TT)
            for t in range(TT):
                ps = take(("co", t))
                for hd in range(CH):
                    b, hf = hd // 2, hd % 2
                    o = ps[:, hd * HD:(hd + 1) * HD]
                    cs = slice(hd * HD, (hd + 1) * HD)
                    if t:
                        T.matmul(o, m["crs"][:, hf * 256 + b * P:hf * 256 + (b + 1) * P], ci[:, 0, cs], start=True, stop=False)
                    ins = T.matmul(o, m["att"][:, hf, (2 * t + b) * P:(2 * t + b + 1) * P], ci[:, t, cs], start=(t == 0), stop=True)
                done(ins, ("co", t))
            for nm in ("aq", "ak"):
                for b in range(2):
                    fm((nm, b))
            tm(("av",))
            for b in range(2):
                fm(("bqk", b))
            tm(("bvo",))
            pe.wait_ge(sg("ws_in"), 96)
            for i, nm in enumerate(("cf", "bi", "bf")):
                ps = take(nm)
                for k in range(KD):
                    ins = T.matmul(ps[0:72, 0:S], ws[:, k, WS0[i]:WS0[i] + 72], xT[:, k, :], start=(k == 0), stop=(k == KD - 1))
                done(ins, nm)
            pe.wait_ge(sg("qk_sq"), 1)
            for i in range(4):
                done(T.matmul(take(("qkss", i))[:, :], pair64[:, :], rs[:, i * 512:(i + 1) * 512], start=True, stop=True),
                     ("qkss", i))
            pe.wait_ge(sg("qk_n"), 2)
            pe.wait_ge(sg("c_rows"), 1)
            ao = [take(("ao", t)) for t in range(TT)]

            def fox_scores(hd):
                b, r = hd // 2, slice(64 * (hd % 2), 64 * (hd % 2) + 64)
                ps = take(("s", hd))
                for i, (qt_, kt_) in enumerate(((0, 0), (1, 0), (1, 1))):
                    o = ps[:, i * P:(i + 1) * P]
                    qs, ks = slice(qt_ * P, (qt_ + 1) * P), slice(kt_ * P, (kt_ + 1) * P)
                    T.matmul(o, aq[r, b, qs], ak[r, b, ks], start=True, stop=False)
                    T.matmul(o, cS[r, qs], sel[r, hd, :], start=False, stop=False)
                    ins = T.matmul(o, sel[r, hd, :], ncS[r, ks], start=False, stop=True)
                done(ins, ("s", hd))

            def fox_values(hd):
                ps = take(("pT", hd))
                pe.wait_ge(sg("s_exp"), TT * (hd + 1))
                for i in range(3):
                    ins = T.transpose(ps[:, i * P:(i + 1) * P], sS[:, hd % 2, i * P:(i + 1) * P], ident[:, :])
                done(ins, ("pT", hd))
                gone(pe, ("pT", hd))
                cs = slice(hd * HD, (hd + 1) * HD)
                i0 = T.matmul(ao[0][:, cs], pTs[:, hd % 2, 0:P], av[:, 0, cs], start=True, stop=True)
                T.matmul(ao[1][:, cs], pTs[:, hd % 2, P:S], av[:, 0, cs], start=True, stop=False)
                i1 = T.matmul(ao[1][:, cs], pTs[:, hd % 2, S:384], av[:, 1, cs], start=False, stop=True)
                if hd == AH - 1:
                    done(i0, ("ao", 0))
                    done(i1, ("ao", 1))

            fox_scores(0)
            for hd in range(AH):
                if hd + 1 < AH:
                    fox_scores(hd + 1)
                fox_values(hd)
            pe.wait_ge(sg("m_rows"), 1)
            pe.wait_ge(sg("b_act"), 1)
            ps = take("mT")
            for t in range(TT):
                ins = T.transpose(ps[:, t * P:(t + 1) * P], mS[:, t * P:(t + 1) * P], ident[:, :])
            done(ins, "mT")
            bo = [take(("bo", t)) for t in range(TT)]

            def lstm_scores(hd):
                b, r = hd // 2, slice(64 * (hd % 2), 64 * (hd % 2) + 64)
                ps = take(("P2", hd))
                for i, (st, tt) in enumerate(((0, 0), (0, 1), (1, 1))):
                    o = ps[:, i * P:(i + 1) * P]
                    T.matmul(o, sel[r, hd, :], nM[r, tt * P:(tt + 1) * P], start=True, stop=False)
                    ins = T.matmul(o, iF[r, st * P:(st + 1) * P], sel[r, hd, :], start=False, stop=True)
                done(ins, ("P2", hd))
                ps = take(("P1", hd))
                for i, (st, tt) in enumerate(((0, 0), (0, 1), (1, 1))):
                    ins = T.matmul(ps[:, i * P:(i + 1) * P], bc[r, 2 + b, st * P:(st + 1) * P], bc[r, b, tt * P:(tt + 1) * P],
                                   start=True, stop=True)
                done(ins, ("P1", hd))

            def lstm_values(hd):
                pe.wait_ge(sg("d_w"), hd + 1)
                cs = slice(hd * 65, (hd + 1) * 65)
                w = sS[:, hd % 2, :]
                i0 = T.matmul(bo[0][:, cs], w[:, 0:P], bv[:, 0, hd, :], start=True, stop=True)
                T.matmul(bo[1][:, cs], w[:, P:S], bv[:, 0, hd, :], start=True, stop=False)
                i1 = T.matmul(bo[1][:, cs], w[:, S:384], bv[:, 1, hd, :], start=False, stop=True)
                if hd == BH - 1:
                    done(i0, ("bo", 0))
                    done(i1, ("bo", 1))
                else:
                    i1.then_inc(sg("b_pv"), 1)

            lstm_scores(0)
            for hd in range(BH):
                if hd + 1 < BH:
                    lstm_scores(hd + 1)
                lstm_values(hd)
            pe.wait_ge(sg("o_done"), 1)
            transposes("yy")
            out_proj("w2")
            norm("n5")
            x_split()
            ffn("f2")


def kernel(**inputs):
    import numpy as np
    import concourse.bacc as bacc
    from concourse import mybir
    from concourse.bass_utils import run_bass_kernel_spmd

    nc = bacc.Bacc("TRN2", target_bir_lowering=False, num_devices=1)
    arrays, aps = {}, {}
    for name, a in inputs.items():
        a = np.ascontiguousarray(a)
        arrays[f"in_{name}"] = a
        aps[name] = nc.dram_tensor(f"in_{name}", a.shape, mybir.dt.from_np(a.dtype), kind="ExternalInput").ap()
    shape = inputs["x"].shape
    out = nc.dram_tensor("out_0", shape, mybir.dt.float32, kind="ExternalOutput").ap()
    build(nc, aps, out)
    r = run_bass_kernel_spmd(nc, [arrays], core_ids=[0])
    return r.results[0]["out_0"]
```

```python
def build(nc, IN, out):
    import concourse.bass as bass
    from concourse import mybir
    from contextlib import ExitStack

    F32, F32R, I32 = mybir.dt.float32, mybir.dt.float32r, mybir.dt.int32
    ACT, ALU, AX = mybir.ActivationFunctionType, mybir.AluOpType, mybir.AxisListType
    P = 128
    _, S, D = IN["x"].shape
    TT = S // P
    KD = D // P
    EPS = 1e-6
    NEG = -1e30
    F1 = IN["ffn_w_gate"].shape[2]
    F2 = IN["w_down_2"].shape[1]
    _, NE, _, FE = IN["moe_w_gate"].shape
    GH, GDK, GDV = 4, 128, 256
    GR = IN["gla_w_gate_up"].shape[1]
    GQK, GV = GH * GDK, GH * GDV
    GATE_NORM = 16.0
    SH = 8
    AH, BH, CH, HD = 8, 4, 4, 64
    AD, BD = AH * HD, BH * HD
    FJ = 256
    NJ1, NJ2 = F1 // FJ, F2 // FJ
    assert NJ1 == NJ2 and NJ1 % 2 == 1
    EJ = 512
    NEJ = FE // EJ
    PIECE = 2048
    NR, NRX, NW = 4, 6, 4
    LO_V = 1536
    AR = 11392
    LEVELS = [0, 1, 2, 4, 8, 16, 32, 64]
    C_AQ, C_AK, C_AV, C_AF = 0, AD, 2 * AD, 3 * AD
    C_BQK = 3 * AD + AH
    C_BV = C_BQK + 2 * BD
    C_BI = C_BV + BD
    C_BF = C_BI + BH
    C_BO = C_BF + BH
    C_CQ = C_BO + BD
    C_CI = C_CQ + 2 * BD
    C_CG = C_CI + BD

    ctx = ExitStack()
    with ctx:
        def sb(name, shape, dt=F32):
            return ctx.enter_context(nc.sbuf_tensor(name, shape, dt))

        sems = {}

        def sg(name):
            if name not in sems:
                sems[name] = ctx.enter_context(nc.semaphore(name))
            return sems[name]

        raw = sb("raw", [P, NR, PIECE])
        wh = sb("wh", [P, NW, PIECE], F32R)
        wl = sb("wl", [P, NW, PIECE], F32R)
        h = sb("h", [P, TT, D])
        xT = sb("xT", [P, KD, S])
        xTh = sb("xTh", [P, KD, S], F32R)
        xTl = sb("xTl", [P, KD, S], F32R)
        acth = sb("acth", [P, 2, 512], F32R)
        actl = sb("actl", [P, 2, 512], F32R)
        xn = sb("xn", [P, TT, D])
        arena = sb("arena", [P, AR])
        ident = sb("ident", [P, P])
        lmask = sb("lmask", [P, len(LEVELS) - 2, P])
        nafter = sb("nafter", [P, P])
        before3 = sb("before3", [P, 3, P])
        rowneg3 = sb("rowneg3", [P, 3, P])
        colneg3 = sb("colneg3", [P, 3, P])
        pair64 = sb("pair64", [P, P])
        sel = sb("sel", [P, AH, P])
        iota = sb("iota", [P, P])
        tri8 = sb("tri8", [P, NE, NE])
        cst = sb("cst", [P, 34])
        c_eps, c_one, c_half = cst[:, 0:1], cst[:, 1:2], cst[:, 2:34]
        WS0 = (0, AH, AH + BH)
        ws = sb("ws", [P, KD, WS0[2] + 72])
        wglr = sb("wglr", [P, KD, GR])
        wrt = sb("wrt", [P, KD, NE])
        vT = sb("vT", [P, 3, P])
        ssq = sb("ssq", [P, 32])
        ms = sb("ms", [P, 32])
        rstd = sb("rstd", [P, 32])
        scr = sb("scr", [P, 1])
        bank = [ctx.enter_context(nc.psum_tensor(f"bank{b}", [P, 512], F32)) for b in range(8)]

        ar_at = [0]

        def ar_reset(at=0):
            ar_at[0] = at

        def ar(n):
            a = arena[:, ar_at[0]:ar_at[0] + n]
            ar_at[0] += n
            assert ar_at[0] <= AR, ar_at[0]
            return a

        vec_rows = {}
        vec_dma = []
        at = [0, 0, 0]

        def rows(name, tile, ap, n):
            vec_rows[name] = (tile, at[tile])
            vec_dma.append((tile, at[tile], n, ap))
            at[tile] += n

        names = (("attn_norm", 2 * KD), ("gla_b_gate", GQK // P), ("gla_head_norm", GDV // P),
                 ("gla_head_norm again", GDV // P),
                 ("ffn_norm", 2 * KD), ("kv_norm", KD), ("norm_mix_g_2", KD), ("norm_ffn_g_2", KD), ("out_g_2", KD),
                 ("lb_logits_2", 2))
        N_EARLY = 4
        for nm, n in names:
            a = IN[nm.split()[0]]
            a = a.rearrange("(r p) -> r p", p=P) if len(a.shape) == 1 else a.rearrange("a (r p) -> (a r) p", p=P)
            rows(nm, 0, a, n)
            if len(vec_dma) == N_EARLY:
                V_EARLY = at[0]
                at[0] = 32
        for nm, c0, n in (("aq_b", C_AQ, 4), ("ak_b", C_AK, 4), ("bqk_b", C_BQK, 4), ("cqf_b", C_CQ, 4)):
            rows(nm, 0, IN["b_in_2"][0, c0:c0 + n * P].rearrange("(r p) -> r p", p=P), n)
        rows("b_conv", 0, IN["b_conv_w_2"].rearrange("a k (r p) -> (a k r) p", p=P), 16)
        R_G = at[0]
        at[0] += 5
        NF2 = 2 * F2 // P
        rows("tap01", 1, IN["ffn_conv_w_2"][0, 0:2, :].rearrange("k (r p) -> (k r) p", p=P), 2 * NF2)
        rows("tap2", 2, IN["ffn_conv_w_2"][0, 2:3, :].rearrange("k (r p) -> (k r) p", p=P), NF2)
        rows("conv_b", 2, IN["ffn_conv_b_2"].rearrange("k (r p) -> (k r) p", p=P), NF2)
        V_ROWS = [at[0], at[1], at[2]]
        N_VEC = len(vec_dma) - N_EARLY + 10

        def col(name, i=0):
            tile, r = vec_rows[name]
            return vT[:, tile, r + i:r + i + 1]

        def cols(name, i, n):
            tile, r = vec_rows[name]
            return vT[:, tile, r + i:r + i + n]

        turns, uses, rr = {}, [0] * 8, [0]

        def turn(label, b=None):
            if b is None:
                b = rr[0] % 8
                rr[0] += 1
            turns[label] = (b, uses[b])
            uses[b] += 1

        def order(halves):
            return [(t, half) for half in range(2) for t in range(TT)] if halves else \
                   [(t, half) for t in range(TT) for half in range(2)]

        full = [sg(f"full{b}") for b in range(8)]
        freed = [sg(f"freed{b}") for b in range(8)]

        def plan_norm(n, halves=False):
            for t, half in order(halves):
                turn((n, t, half))

        def plan_ffn(f):
            def gu(j):
                turn((f, j, "g"), 2 * (j % 2))
                turn((f, j, "u"), 2 * (j % 2) + 1)
            gu(0)
            for t in range(TT):
                for half in range(2):
                    turn((f, "acc", t, half), 4 + 2 * t + half)
            for j in range(1, NJ1):
                gu(j)
            rr[0] = 0

        turn(("vec", "early"))
        plan_norm("n0")
        for lab in ("glr", ("gate", 0), ("gate", 1), ("q", 0), ("q", 1), ("k", 0), ("k", 1)):
            turn(lab)
        def plan_levels(pre, cross, between):
            for i, m in enumerate(LEVELS):
                for lab in between.get(i, []):
                    turn(lab)
                for g in range(2):
                    turn((pre, m, g))
            for g in range(cross):
                turn((pre, P, g))

        gl_tm = [(nm, c, t) for nm in ("v", "r") for c in range(2) for t in range(TT)]
        plan_levels("gl", 1, {i: ([("vec", j) for j in range(3)] if i == 4 else []) + [lab] for i, lab in enumerate(gl_tm)})
        for t, hp in order(True):
            turn(("o", t, hp))
        plan_norm("y", True)
        for c in range(2):
            for t in range(TT):
                turn(("wo", c, t))
        plan_norm("n1")
        plan_ffn("f1")
        plan_norm("n2")
        for t in range(TT):
            turn(("sv", 0, t))
        for b in range(4):
            turn(("sk", b))
        for t in range(TT):
            turn(("sv", 1, t))
        for b in range(4):
            turn(("sq", b), 6 + b % 2)
            if b:
                for hd in (2 * b - 2, 2 * b - 1):
                    turn(("z", hd), hd)
        for lab, b in ((("stay", 0), 0), (("z", 6), 6), (("z", 7), 7)):
            turn(lab, b)
        for hd in range(1, SH):
            turn(("stay", hd), hd)
        rr[0] = 0
        for hp in range(SH // 2):
            turn(("so", hp))
        for c in range(2):
            for t in range(TT):
                turn(("swo", c, t))
        plan_norm("n3")
        turn("lg")
        turn("pos")
        turn("cnt")
        uses_before_moe = list(uses)
        plan_norm("n4")
        for t in range(TT):
            turn(("cig", t))
        for b in range(2):
            turn(("cqf", b))
        hl_pieces = {0: [("aq", 0), ("aq", 1), "rows"], 1: [("ak", 0)], 2: [("ak", 1)], 3: [("bqk", 0)], 4: [("bqk", 1)],
                     5: [("av", 0)], 6: [("av", 1)]}

        def results(nm):
            return ["cf", "bi", "bf"] if nm == "rows" else [nm]

        plan_levels("hl", 2, {i: [lab for nm in nms for lab in results(nm)] for i, nms in hl_pieces.items()})
        turn(("bvo", 0))
        for i in range(4):
            turn(("qkss", i))
        turn(("bvo", 1))
        for t in range(TT):
            turn(("co", t))
        rr[0] = 0
        for t in range(TT):
            turn(("ao", t), 6 + t)
        for hd in range(AH):
            turn(("s", hd), hd % 3)
            turn(("pT", hd), 3 + hd % 3)
        turn("mT", 0)
        for t in range(TT):
            turn(("bo", t), 6 + t)
        for hd in range(BH):
            turn(("P2", hd), (1, 2, 5)[hd % 3])
            turn(("P1", hd), (3, 4, 0)[hd % 3])
        rr[0] = 0
        plan_norm("yy", True)
        for c in range(2):
            for t in range(TT):
                turn(("w2", c, t))
        plan_norm("n5")
        plan_ffn("f2")

        def see(eng, label):
            b, n = turns[label]
            eng.wait_ge(full[b], n + 1)
            return bank[b]

        def gone(eng, label):
            b, n = turns[label]
            eng.wait_ge(freed[b], n + 1)

        class Order:

            def __init__(self, eng, name):
                self.eng, self.own, self.count = eng, sg(name), {}

            def __call__(self, ins, name=None, frees=None):
                if frees is not None:
                    b, n = turns[frees]
                    ins.then_inc(freed[b], 1)
                    self.eng.wait_ge(freed[b], n + 1)
                    return
                s = self.own if name is None else sg(name)
                n = self.count[name] = self.count.get(name, 0) + 1
                ins.then_inc(s, 1)
                self.eng.wait_ge(s, n)

        def kpn(ap):
            return ap.rearrange("(k p) n -> p k n", p=P)

        pieces, pos = [], {}

        def piece(nm, parts, last, phase):
            pos[nm] = len(pieces)
            pieces.append((parts, last, phase))

        def fm_pieces(nm, src, phase, n):
            for b in range(n):
                piece((nm, b), [kpn(src[:, b * 256:(b + 1) * 256])], (nm, b), phase)

        def tm_pieces(nm, srcs, phase):
            for k in range(2):
                piece((nm, k), [kpn(a[k * 512:(k + 1) * 512, :]) for a in srcs], nm + (TT - 1,), phase)

        def out_pieces(nm, src, phase):
            for k in range(2):
                for c in range(2):
                    piece(((nm, c), k), [kpn(src[k * 512:(k + 1) * 512, 512 * c:512 * (c + 1)])],
                          ("down", nm, c + 1) if k == 0 else (nm, c, TT - 1), phase)

        def ffn_pieces(f, gate, up, down, phase):
            for j in range(NJ1 + 1):
                if j < NJ1:
                    js = slice(j * FJ, (j + 1) * FJ)
                    piece((f, j, "g"), [kpn(gate[:, js])], (f, j, "g"), phase)
                    piece((f, j, "u"), [kpn(up[:, js])], (f, j, "u"), phase)
                if j:
                    piece((f, j - 1, "d"), [kpn(down[(j - 1) * FJ:j * FJ, :])],
                          ("down", f, j) if j < NJ1 else (f, "acc", TT - 1, 1), phase)

        w1 = IN["gla_w_in"][0]
        fm_pieces("q", w1[:, 0:GQK], 0, 2)
        fm_pieces("k", w1[:, GQK:2 * GQK], 0, 2)
        for nm, c0 in (("v", 2 * GQK), ("r", 2 * GQK + GV + GR)):
            for c in range(2):
                tm_pieces((nm, c), [w1[:, c0 + 512 * c:c0 + 512 * (c + 1)]], 0)
        out_pieces("wo", IN["gla_w_out"][0], 0)
        ffn_pieces("f1", IN["ffn_w_gate"][0], IN["ffn_w_up"][0], IN["ffn_w_down"][0], 0)
        tm_pieces(("sv", 0), [IN["sb_w_kv"][:, D:D + 512]], 0)
        fm_pieces("sk", IN["sb_w_kv"][:, 0:D], 0, 4)
        tm_pieces(("sv", 1), [IN["sb_w_kv"][:, D + 512:D + 1024]], 0)
        fm_pieces("sq", IN["sb_w_q"][0], 0, 4)
        out_pieces("swo", IN["sb_w_out"][0], 0)
        N_PRE = len(pieces)
        w2 = IN["w_in_2"][0]
        tm_pieces(("cig",), [w2[:, C_CI:C_CI + 2 * BD]], 1)
        fm_pieces("cqf", w2[:, C_CQ:C_CQ + 2 * BD], 1, 2)
        fm_pieces("aq", w2[:, C_AQ:C_AQ + AD], 1, 2)
        fm_pieces("ak", w2[:, C_AK:C_AK + AD], 1, 2)
        fm_pieces("bqk", w2[:, C_BQK:C_BQK + 2 * BD], 1, 2)
        tm_pieces(("av",), [w2[:, C_AV:C_AV + AD]], 1)
        tm_pieces(("bvo",), [w2[:, C_BV:C_BV + BD], w2[:, C_BO:C_BO + BD]], 1)
        out_pieces("w2", IN["w_out_2"][0], 1)
        ffn_pieces("f2", IN["w_up_2"][0][:, 0:F2], IN["w_up_2"][0][:, F2:2 * F2], IN["w_down_2"][0], 1)
        by_pool = {pos[("wo", c), 1] for c in range(2)} | {pos[("w2", c), k] for c in range(2) for k in range(2)}

        raw_in = [[sg(f"raw_in{s}") for s in range(NR)], [sg(f"raw_in2_{s}") for s in range(NR)]]
        hi_ready = [sg("hi_ready"), sg("hi_ready2")]
        lo_ready = [sg("lo_ready"), sg("lo_ready2")]
        lo_pool = [sg("lo_pool"), sg("lo_pool2")]
        arrive, filled, lo_of, los = [], [[0] * NR, [0] * NR], [], {}
        for i, (parts, last, ph) in enumerate(pieces):
            filled[ph][i % NR] += 16 * len(parts)
            arrive.append(filled[ph][i % NR])
            s = (lo_pool if i in by_pool else lo_ready)[ph]
            los[s.name] = los.get(s.name, 0) + 1
            lo_of.append((s, los[s.name]))

        def of(slots, i, k):
            return slots[:, i % NW, :].rearrange("p (k n) -> p k n", k=k)

        def split_done(eng, i):
            eng.wait_ge(lo_of[i][0], lo_of[i][1])

        def released(eng, i):
            last = pieces[i][1]
            if last[0] == "down":
                eng.wait_ge(sg("down_done_" + last[1]), last[2])
            else:
                see(eng, last)

        class Split:

            def __init__(self, eng, mine):
                self.eng, self.mine, self.next = eng, mine, 0

            def upto(self, n):
                for i in range(self.next, n + 1):
                    if self.mine(i):
                        self.one(i)
                self.next = max(self.next, n + 1)

        class Hi(Split):
            def one(self, i):
                ph = pieces[i][2]
                self.eng.wait_ge(raw_in[ph][i % NR], arrive[i])
                if ph == 0 and i >= NW or i >= N_PRE + NW:
                    released(self.eng, i - NW)
                elif ph == 1:
                    self.eng.wait_ge(sg("moe_used"), self.more * PC + (NPAIR * PC - NW + 1 + i - N_PRE))
                nc.scalar.activation(wh[:, i % NW, :], raw[:, i % NR, :], ACT.Copy).then_inc(hi_ready[ph], 1)

        class Lo(Split):
            def one(self, i):
                ph = pieces[i][2]
                self.eng.wait_ge(hi_ready[ph], i + 1 if ph == 0 else i - N_PRE + 1)
                V = nc.gpsimd if i in by_pool else nc.vector
                V.tensor_tensor(wl[:, i % NW, :], raw[:, i % NR, :], wh[:, i % NW, :].bitcast(F32),
                                ALU.subtract).then_inc(lo_of[i][0], 1)

        uorder = []
        for j in range(NEJ):
            uorder += [("g", j, 0), ("g", j, 1), ("u", j, 0), ("u", j, 1)]
            if j:
                uorder += [("d", j - 1, 0), ("d", j - 1, 1)]
        uorder += [("d", NEJ - 1, 0), ("d", NEJ - 1, 1)]
        UC = len(uorder)
        PC = 2 * UC
        assert PC % NRX == 0 and PC % NW == 0
        upos = {c: i for i, c in enumerate(uorder)}
        NPAIR = NE // 2
        M0 = N_PRE
        lo_moe = [sg("lo_moe_v"), sg("lo_moe_p")]

        def moe_split(eng, at, c):
            n = at(PC, c + 1)
            for s in lo_moe:
                eng.wait_ge(s, n)

        def moe_raw(c):
            s = c % NRX
            return (raw[:, (M0 + s) % NR, :] if s < NR else extra[:, s - NR, :]), raw_moe[s]

        raw_moe = [sg(f"raw_moe{s}") for s in range(NRX)]

        def pairs(eng, body, split=None):
            more = eng.value_load(more_i[0:1, 0:1], min_val=0, max_val=NPAIR)
            if split is not None:
                split.more = more
            with eng.Fori(0, more + (NPAIR - 1)) as p:
                body(lambda a, b: p * a + b, True)
            body(lambda a, b: more * a + ((NPAIR - 1) * a + b), False)
            return more

        ar_reset()
        g = {}
        for nm in ("Q", "K", "A", "E", "W", "qt", "kt"):
            g[nm] = ar(GH * S)
        g["att"] = ar(2 * 512).rearrange("p (g n) -> p g n", g=2)
        g["crs"] = ar(512)
        g["mt"] = ar(512)
        gr = ar(TT * GV).rearrange("p (t n) -> p t n", t=TT)
        gv = xT.rearrange("p k s -> p (k s)").rearrange("p (t n) -> p t n", t=TT)
        wgu = g["mt"][0:GR, :]
        glrT = g["att"].rearrange("p g n -> p (g n)")[0:GR, 0:S]
        vrow = gr.rearrange("p t n -> p (t n)")[:, 0:3 * P].rearrange("p (a b) -> p a b", a=3)
        ar_reset()
        f_sg = ar(2 * 512).rearrange("p (a n) -> p a n", a=2)
        f_act = ar(2 * 512).rearrange("p (a n) -> p a n", a=2)
        f_cu = ar(2 * 1024).rearrange("p (a n) -> p a n", a=2)
        ar_reset()
        skT = xT
        sqT = ar(SH * S).rearrange("p (h s) -> p h s", h=SH)
        xq = arena[:, ar_at[0]:ar_at[0] + KD * S].rearrange("p (k s) -> p k s", k=KD)
        sE, sT, sU = (ar(SH * 384).rearrange("p (h s) -> p h s", h=SH) for _ in range(3))
        sv = xn
        nones = ar(P)
        ar_reset()
        lg = ar(TT * NE).rearrange("p (t e) -> p t e", t=TT)
        cmp1 = ar(TT * NE * NE).rearrange("p (t e j) -> p t e j", t=TT, e=NE)
        cmp2 = ar(TT * NE * NE).rearrange("p (t e j) -> p t e j", t=TT, e=NE)
        rank = ar(TT * NE).rearrange("p (t e) -> p t e", t=TT)
        selx = ar(TT * NE).rearrange("p (t e) -> p t e", t=TT)
        mx = ar(TT)
        ex = ar(TT * NE).rearrange("p (t e) -> p t e", t=TT)
        exs = ar(TT)
        NU = 2 * NE + 2
        pm = ar(NU * TT).rearrange("p (u t) -> p u t", u=NU)
        gt = ar(NU * TT).rearrange("p (u t) -> p u t", u=NU)
        cmax = ar(2)
        more_i = ar(1).bitcast(I32)
        oh = ar(TT * P).rearrange("p (t s) -> p t s", t=TT)
        ohg = ar(TT * P).rearrange("p (t s) -> p t s", t=TT)
        ohT = ar(S)
        xg = ar(KD * P).rearrange("p (k s) -> p k s", k=KD)
        xgh, xgl = xTh[:, :, 0:P], xTl[:, :, 0:P]
        eactTh, eactTl = xTh[:, :, P:S], xTl[:, :, P:S]
        esg = ar(2 * EJ).rearrange("p (a n) -> p a n", a=2)
        eact = ar(2 * EJ).rearrange("p (a n) -> p a n", a=2)
        ey = ar(D)
        junk = arena[:, ar_at[0] - 2 * D:ar_at[0] - D]
        assert 2 * EJ == D
        fgain = ar(D)
        assert ar_at[0] <= AR - (NRX - NR) * PIECE
        ar_reset(AR - (NRX - NR) * PIECE)
        extra = ar((NRX - NR) * PIECE).rearrange("p (a n) -> p a n", n=PIECE)
        ar_reset()
        m = {}
        for nm in ("Q", "K", "A", "E", "W", "qt", "kt"):
            m[nm] = ar(2 * S)
        m["att"] = ar(2 * 512).rearrange("p (g n) -> p g n", g=2)
        m["crs"] = ar(512)
        m["mt"] = ar(512)
        ar_reset()
        bc = ar(4 * S).rearrange("p (b s) -> p b s", b=4)
        mix0 = ar_at[0]
        rs = ar(8 * S)
        ar_reset(mix0)
        sS = ar(3 * 384).rearrange("p (a n) -> p a n", a=3)
        pTs, Dm = (ar(2 * 384).rearrange("p (a n) -> p a n", a=2) for _ in range(2))
        ar_reset(7 * 2 * S + 1024 + 1024)
        aq, ak = (ar(4 * S).rearrange("p (b s) -> p b s", b=4) for _ in range(2))
        osq = arena[:, ar_at[0] - 8 * S:ar_at[0]]
        av = ar(TT * AD).rearrange("p (t n) -> p t n", t=TT)
        bz = ar(4 * S).rearrange("p (b s) -> p b s", b=4)
        bv = ar(TT * BH * 65).rearrange("p (t h n) -> p t h n", t=TT, h=BH)
        bog = ar(TT * BD).rearrange("p (t n) -> p t n", t=TT)
        cg = ar(TT * BD).rearrange("p (t n) -> p t n", t=TT)
        lbp, lb1 = ar(2), ar(2)
        nmx, asum, arec = ar(AH * TT), ar(AH * TT), ar(AH * TT)
        em, den, iT = ar(TT * BH), ar(TT * BH), ar(TT * BH)
        gq = ar(2)
        xn1 = xn.rearrange("p t d -> p (t d)")
        b_av, b_bv, b_ci, b_bo, b_cg = (xn1[:, a:a + n] for a, n in ((0, AD), (AD, BD), (AD + BD, BD),
                                                                     (D + AD, BD), (D + AD + BD, BD)))
        ci = xn1[:, D:D + TT * BD].rearrange("p (t n) -> p t n", t=TT)
        cS, ncS, iF, nM, mS, row1 = (xT[:, i, :] for i in range(6))
        o_all = xn

        def quarters(n, halves=False):
            return [((n, t, half), (slice(None), slice(4 * half, 4 * half + 4), slice(t * P, (t + 1) * P)))
                    for t, half in order(halves)]

        X_HALF = 2
        head_pairs = [(("so", hp), (slice(None), slice(2 * hp, 2 * hp + 2), slice(None))) for hp in range(SH // 2)]

        block = ctx.enter_context(nc.Block())
        xv = IN["x"][0].rearrange("(t p) d -> p t d", p=P)
        ov = out[0].rearrange("(t p) d -> p t d", p=P)

        @block.sync
        def _(sp):
            for t in range(TT):
                sp.dma_start(h[:, t, :], xv[:, t, :]).then_inc(sg(f"x_in{t}"), 16)

            def load(i):
                parts, _, ph = pieces[i]
                n0 = 0
                for part in parts:
                    k, n = part.shape[1], part.shape[2]
                    sp.dma_start(of(raw, i, k)[:, :, n0:n0 + n], part).then_inc(raw_in[ph][i % NR], 16)
                    n0 += n

            def load_expert(c, e):
                kind, j, k = uorder[c % UC]
                ee = e + c // UC
                to, arrived = moe_raw(c)
                if kind == "d":
                    r0 = j * EJ + k * (EJ // 2)
                    src = IN["moe_w_down"][0].rearrange("e f n -> (e f) n")[bass.ds(ee * FE + r0, EJ // 2), :]
                    src = kpn(src)
                else:
                    src = IN["moe_w_gate" if kind == "g" else "moe_w_up"][0, bass.ds(ee, 1), k * (D // 2):(k + 1) * (D // 2),
                                                                          j * EJ:(j + 1) * EJ]
                    src = src.rearrange("a (k p) n -> p (a k) n", p=P)
                sp.dma_start(to.rearrange("p (k n) -> p k n", k=src.shape[1]), src).then_inc(arrived, 16)

            sp.wait_ge(sg("vrow_zero"), 1)
            for tile, r0, n, ap in vec_dma[0:N_EARLY]:
                sp.dma_start(vrow[r0:r0 + n, tile, :], ap).then_inc(sg("vec_first"), 16)
            sp.dma_start(wglr[:, :, :], kpn(w1[:, 2 * GQK + GV:2 * GQK + GV + GR])).then_inc(sg("glr_in"), 16)
            sp.dma_start(wgu, IN["gla_w_gate_up"][0]).then_inc(sg("glr_in"), 16)
            for i in range(NR):
                load(i)
            nv = 0
            for tile, r0, n, ap in vec_dma[N_EARLY:]:
                sp.dma_start(vrow[r0:r0 + n, tile, :], ap).then_inc(sg("vec_in"), 16)
                nv += 1
            for i, nm in enumerate(("a_q_g_2", "a_k_g_2")):
                for half in range(2):
                    sp.dma_start(vrow[R_G + i:R_G + i + 1, 0, 64 * half:64 * half + 64], IN[nm]).then_inc(sg("vec_in"), 16)
                    nv += 1
            for i, (c0, n) in enumerate(((C_AF, AH), (C_BI, BH), (C_BF, BH))):
                for half in range(2):
                    sp.dma_start(vrow[R_G + 2 + i:R_G + 3 + i, 0, 64 * half:64 * half + n],
                                 IN["b_in_2"][0:1, c0:c0 + n]).then_inc(sg("vec_in"), 16)
                    nv += 1
            assert nv == N_VEC, nv
            for i in range(NR, N_PRE):
                split_done(sp, i - NR)
                load(i)
                if i == pos["f1", 2, "g"]:
                    sp.dma_start(wrt[:, :, :], kpn(IN["moe_w_router"][0])).then_inc(sg("rt_in"), 16)
                    sp.wait_ge(sg("ws_zero"), 1)
                    for j, (c0, n) in enumerate(((C_AF, AH), (C_BI, BH), (C_BF, BH))):
                        for half in range(2):
                            d0 = 64 * half + WS0[j]
                            sp.dma_start(ws[:, :, d0:d0 + n], kpn(w2[:, c0:c0 + n]),
                                         allow_slow_non_contiguous=True).then_inc(sg("ws_in"), 16)
            for c in range(NR):
                split_done(sp, N_PRE - NR + c)
                load_expert(c, 0)
            for hp in range(SH // 2):
                see(sp, ("so", hp))
            for c in range(NR, NRX):
                load_expert(c, 0)
            sp.wait_ge(sg("more_ready"), 1)
            more = sp.value_load(more_i[0:1, 0:1], min_val=0, max_val=NPAIR)
            with sp.Fori(0, more + (NPAIR - 1)) as p:
                e = (p % NPAIR) * 2
                for c in range(NRX, PC):
                    moe_split(sp, lambda a, b: p * a + b, c - NRX)
                    load_expert(c, e)
                e2 = ((p + 1) % NPAIR) * 2
                for c in range(NRX):
                    moe_split(sp, lambda a, b: p * a + b, c + PC - NRX)
                    load_expert(c, e2)
            for c in range(NRX, PC + NR):
                moe_split(sp, lambda a, b: more * a + ((NPAIR - 1) * a + b), c - NRX)
                if c < PC:
                    load_expert(c, NE - 2)
                else:
                    load(N_PRE + c - PC)
            for i in range(N_PRE + NR, len(pieces)):
                split_done(sp, i - NR)
                load(i)
            for t in range(TT):
                for half in range(2):
                    gone(sp, ("f2", "acc", t, half))
                sp.dma_start(ov[:, t, :], h[:, t, :]).then_inc(sg("out_done"), 16)
            sp.wait_ge(sg("out_done"), 16 * TT)

        @block.gpsimd
        def _(pool):
            G = Order(pool, "pool_order")
            V = nc.gpsimd
            G(V.memset(vrow, 0.0), "vrow_zero")
            G(V.memset(ident[:, :], 0.0))
            G(V.affine_select(out=ident[:, :], in_=ident[:, :], compare_op=ALU.not_equal, fill=1.0, base=0,
                              pattern=[[-1, P]], channel_multiplier=1), "const")
            G(V.memset(cst[:, 0:1], EPS))
            G(V.memset(cst[:, 1:2], 1.0))
            G(V.memset(c_half, -0.5), "const")
            turn_of = [0]

            def rsqrt(c0, n):
                turn_of[0] += 1
                pool.wait_ge(sg("ms_ready"), turn_of[0])
                G(V.tensor_tensor(rstd[:, c0:c0 + n], ms[:, c0:c0 + n], c_half[:, 0:n], ALU.pow), "rstd_ready")

            def norm(blocks=None, last=False):
                for t in range(TT):
                    rsqrt(t, 1)
                if blocks is not None:
                    split_x(blocks, last=last)

            n_x = [0]

            def split_x(blocks, src=xT, last=False):
                for i, (lab, ix) in enumerate(blocks):
                    n_x[0] += 1
                    if (i >= X_HALF) == last:
                        pool.wait_ge(sg("xh_ready"), n_x[0])
                        G(V.tensor_tensor(xTl[ix], src[ix], xTh[ix].bitcast(F32), ALU.subtract), "xl_pool")

            norm()
            G(V.memset(g["E"], 0.0))
            G(V.memset(lmask[:, :, :], 0.0))
            for i, mh in enumerate(LEVELS[1:-1]):
                n = P // (2 * mh)
                v = lmask[:, i, :].rearrange("p (n two m) -> p n two m", two=2, m=mh)[:, :, 1, :]
                G(V.memset(v, 1.0))
                G(V.affine_select(out=v, in_=v, compare_op=ALU.is_ge, fill=0.0, base=0,
                                  pattern=[[-2 * mh, n], [0, mh]], channel_multiplier=1))
                G(V.affine_select(out=v, in_=v, compare_op=ALU.is_ge, fill=0.0, base=mh - 1,
                                  pattern=[[2 * mh, n], [0, mh]], channel_multiplier=-1))
            G(V.memset(g["qt"], 0.0))
            G(V.memset(g["kt"], 0.0), "masks")
            lo = Lo(pool, lambda i: i in by_pool)

            def halves(a, mh):
                v = a.rearrange("p (n two m) -> p n two m", two=2, m=mh)
                return v[:, :, 0, :], v[:, :, 1, :]

            def grow(pre, T):
                for i, mh in enumerate(LEVELS[1:]):
                    Al, Ar = halves(T["A"], mh)
                    El, Er = halves(T["E"], mh)
                    pool.wait_ge(sg(pre + "_exp"), 2 * (i + 1))
                    G(V.tensor_tensor(El, El, Ar[:, :, mh - 1:mh].to_broadcast(list(El.shape)), ALU.add))
                    G(V.tensor_tensor(Ar, Ar, Al[:, :, mh - 1:mh].to_broadcast(list(Ar.shape)), ALU.add), pre + "_sums")

            split_x(quarters("n0"))
            G(V.memset(nones, -1.0))
            G(V.memset(nafter[:, :], -1.0))
            G(V.affine_select(out=nafter[:, :], in_=nafter[:, :], compare_op=ALU.is_ge, fill=0.0, base=-1,
                              pattern=[[-1, P]], channel_multiplier=1))
            G(V.memset(before3[:, :, :], 1.0))
            for i in (0, 2):
                G(V.affine_select(out=before3[:, i, :], in_=before3[:, i, :], compare_op=ALU.is_ge, fill=0.0,
                                  base=-1, pattern=[[1, P]], channel_multiplier=-1))
            G(V.memset(rowneg3[:, :, :], 0.0))
            G(V.memset(colneg3[:, :, :], 0.0))
            for i in (0, 2):
                G(V.affine_select(out=rowneg3[:, i, :], in_=rowneg3[:, i, :], compare_op=ALU.is_ge, fill=NEG,
                                  base=0, pattern=[[-1, P]], channel_multiplier=1))
                G(V.affine_select(out=colneg3[:, i, :], in_=colneg3[:, i, :], compare_op=ALU.is_ge, fill=NEG,
                                  base=0, pattern=[[1, P]], channel_multiplier=-1))
            G(V.memset(pair64[:, :], 0.0))
            G(V.memset(pair64[0:64, 0:64], 1.0))
            G(V.memset(pair64[64:P, 64:P], 1.0))
            G(V.memset(sel[:, :, :], 0.0))
            for b0 in (0, 64):
                G(V.affine_select(out=sel[:, :, :], in_=sel[:, :, :], compare_op=ALU.not_equal, fill=1.0, base=-b0,
                                  pattern=[[-1, AH], [0, P]], channel_multiplier=1))
            G(V.iota(iota[:, :], pattern=[[1, P]], base=0, channel_multiplier=0, allow_small_or_imprecise_dtypes=True))
            G(V.memset(tri8[:, :, :], 1.0))
            G(V.affine_select(out=tri8[:, :, :], in_=tri8[:, :, :], compare_op=ALU.is_ge, fill=0.0, base=-1,
                              pattern=[[1, NE], [-1, NE]], channel_multiplier=0), "masks2")
            G(V.memset(ws[:, :, :], 0.0), "ws_zero")
            pool.wait_ge(sg("gl_A"), 1)
            grow("gl", g)
            lo.upto(pos[("wo", 1), 1])
            for hp in range(2):
                rsqrt(hp * GH, GH)
            split_x(quarters("y", True), last=True)
            norm(quarters("n1"))
            norm(quarters("n2"), True)
            split_x(quarters("n2"), xq)
            split_x(head_pairs, last=True)
            norm()
            pool.wait_ge(sg("more_ready"), 1)

            def rests(at, more_follow):
                for c in range(PC):
                    s = (M0 + c) % NW
                    pool.wait_ge(sg("hi_moe"), at(PC, c + 1))
                    V.tensor_tensor(wl[:, s, LO_V:PIECE], moe_raw(c)[0][:, LO_V:PIECE], wh[:, s, LO_V:PIECE].bitcast(F32),
                                    ALU.subtract).then_inc(lo_moe[1], 1)

            pairs(pool, rests)
            for t in range(TT):
                rsqrt(2 * t, 2)
            split_x(quarters("n4"), last=True)
            pool.wait_ge(sg("xn_ready"), 5 * TT)
            G(V.memset(m["kt"], 0.0))
            G(V.memset(bv[:, :, :, 64:65], 1.0), "mix_zero")
            pool.wait_ge(sg("hl_A"), 1)
            grow("hl", m)
            pool.wait_ge(sg("hl_qk"), 2 * len(LEVELS))
            for b in range(4):
                gone(pool, ("bqk", b // 2))
                G(V.tensor_scalar(bc[:, b, :], bz[:, b, :], col("b_conv", 12 + b), None, ALU.mult))
                for k in range(1, 4):
                    G(V.tensor_scalar(m["mt"][:, k:S], bz[:, b, 0:S - k], col("b_conv", 4 * (3 - k) + b), None, ALU.mult))
                    G(V.tensor_tensor(bc[:, b, k:S], bc[:, b, k:S], m["mt"][:, k:S], ALU.add), "b_pre")
            lo.upto(pos[("w2", 1), 1])
            rsqrt(0, 24)
            rsqrt(24, 8)
            split_x(quarters("yy", True), last=True)
            norm(quarters("n5"))

        @block.scalar
        def _(act):
            A = Order(act, "act_order")
            V = nc.scalar
            hi = Hi(act, lambda i: True)

            def split_x(blocks, src=xT, written=None):
                for i, (lab, ix) in enumerate(blocks):
                    if written is None:
                        gone(act, lab)
                    else:
                        act.wait_ge(sg(written), i + 1)
                    A(V.activation(xTh[ix], src[ix], ACT.Copy), "xh_ready")

            def norm(before, after=None):
                for t in range(TT):
                    if after is not None:
                        act.wait_ge(sg(after), t + 1)
                    for lab in before(t):
                        gone(act, lab)
                    A(V.activation(xn[:, t, :], h[:, t, :], ACT.Square, accum_out=ssq[:, t:t + 1]), "ssq_ready")

            def exps(pre, T, between):
                for i, mh in enumerate(LEVELS[1:] + [P]):
                    def half(a, j):
                        return a.rearrange("p (n two m) -> p n two m", two=2, m=mh)[:, :, j, :]
                    between(i)
                    if i:
                        act.wait_ge(sg(pre + "_sums"), i)
                        act.wait_ge(sg(pre + "_qk"), 2 * i)
                    A(V.activation(half(T["W"], 1), half(T["A"], 1), ACT.Exp), pre + "_exp")
                    A(V.activation(half(T["W"], 0), half(T["E"], 0), ACT.Exp), pre + "_exp")

            act.wait_ge(sg("const"), 2)
            A(V.activation(scr[:, :], c_one, ACT.Square))

            def arrived(t):
                act.wait_ge(sg(f"x_in{t}"), 16)
                return []

            norm(arrived)
            hi.upto(0)
            split_x(quarters("n0"))
            hi.upto(3)
            act.wait_ge(sg("gl_abs"), 1)
            A(V.activation(g["W"], g["W"], ACT.Exp, scale=-1.0))
            A(V.activation(g["W"], g["W"], ACT.Ln, bias=c_one), "gl_ln")
            for b in range(2):
                A(V.activation(g["Q"][:, b * 512:(b + 1) * 512], see(act, ("q", b))[:, :], ACT.Copy, scale=GDK ** -0.5),
                  frees=("q", b))
                hi.upto(pos["q", b] + NW)
            for b in range(2):
                A(V.activation(g["K"][:, b * 512:(b + 1) * 512], see(act, ("k", b))[:, :], ACT.Copy), frees=("k", b))
            act.wait_ge(sg("gl_A"), 1)
            act.wait_ge(sg("masks"), 1)

            def values(i):
                if i == 1:
                    hi.upto(pos["k", 1] + NW)
                if i:
                    nm, c, t = gl_tm[i - 1]
                    A(V.activation((gv if nm == "v" else gr)[:, t, c * 512:(c + 1) * 512], see(act, (nm, c, t))[:, :],
                                   ACT.Copy), frees=(nm, c, t))
                    if t == TT - 1:
                        hi.upto(pos[(nm, c), 1] + NW)

            exps("gl", g, values)
            values(len(LEVELS))
            A(V.activation(gr[:, :, :], gr[:, :, :], ACT.Silu), "gr_ready")
            for t, hp in order(True):
                    o = see(act, ("o", t, hp))
                    for i in range(2):
                        k = hp * GH + 2 * t + i
                        A(V.activation(xn[:, t, (2 * hp + i) * GDV:(2 * hp + i + 1) * GDV], o[:, i * GDV:(i + 1) * GDV],
                                       ACT.Square, accum_out=ssq[:, k:k + 1]), "gssq_ready")
            split_x(quarters("y", True))
            hi.upto(pos[("wo", 1), 1] + 2)
            norm(lambda t: [("wo", 0, t), ("wo", 1, t)])

            def ffn(f, conv):
                for j in range(NJ1):
                    hi.upto(pos[f, j, "g"] + NW - 1)
                    gp = see(act, (f, j, "g"))
                    if conv:
                        def last_tap(i, ps):
                            for b in range(2):
                                k = i * (F2 // P) + 2 * j + b
                                A(V.activation(f_cu[:, j % 2, (2 * i + b) * S:(2 * i + b + 1) * S], ps[:, b * S:(b + 1) * S],
                                               ACT.Identity, scale=col("tap2", k), bias=col("conv_b", k)), "conv0")

                        if j >= 2:
                            act.wait_ge(sg("act_" + f), j - 1)
                        last_tap(0, gp)
                        hi.upto(min(pos[f, j, "g"] + NW, len(pieces) - 1))
                        gone(act, (f, j, "g"))
                        A(V.activation(f_sg[:, j % 2, :], f_cu[:, j % 2, 0:512], ACT.Silu), "silu_" + f)
                        last_tap(1, see(act, (f, j, "u")))
                    else:
                        if j >= 2:
                            act.wait_ge(sg("act_" + f), j - 1)
                        A(V.activation(f_sg[:, j % 2, :], gp[:, :], ACT.Silu), frees=(f, j, "g"))
                    hi.upto(min(pos[f, j, "g"] + NW, len(pieces) - 1))
                    act.wait_ge(sg("act_" + f), j + 1)
                    A(V.activation(acth[:, j % 2, :], f_act[:, j % 2, :], ACT.Copy), "acth_" + f)
                hi.upto(min(pos[f, NJ1 - 1, "d"] + NW - 1, len(pieces) - 1))

            split_x(quarters("n1"))
            hi.upto(pos[("wo", 1), 1] + NW)
            ffn("f1", False)
            norm(lambda t: [("f1", "acc", t, 0), ("f1", "acc", t, 1)])
            split_x(quarters("n2"), written="kv_x")
            hi.upto(pos["sk", 1])

            def value(c, t):
                A(V.activation(sv[:, t, c * 512:(c + 1) * 512], see(act, ("sv", c, t))[:, :], ACT.Copy), frees=("sv", c, t))

            for t in range(TT):
                value(0, t)
            hi.upto(pos[("sv", 0), 1] + NW)
            for b in range(4):
                A(V.activation(skT[:, 2 * b:2 * b + 2, :].rearrange("p h s -> p (h s)"), see(act, ("sk", b))[:, :], ACT.Copy),
                  frees=("sk", b))
                hi.upto(pos["sk", b] + NW)
            for t in range(TT):
                value(1, t)
                split_x(quarters("n2")[2 * t:2 * t + 2], xq)
            hi.upto(pos["sq", 3])

            def decays(hp):
                h2 = slice(2 * hp, 2 * hp + 2)
                for hd in (2 * hp, 2 * hp + 1):
                    A(V.activation(sE[:, hd, :], see(act, ("z", hd))[:, 0:384], ACT.Abs))
                A(V.activation(sE[:, h2, :], sE[:, h2, :], ACT.Exp, scale=-1.0))

            def logs(hp):
                h2 = slice(2 * hp, 2 * hp + 2)
                A(V.activation(sE[:, h2, :], sE[:, h2, :], ACT.Ln, bias=c_one), "sb_ln")

            for b in range(4):
                A(V.activation(sqT[:, 2 * b:2 * b + 2, :].rearrange("p h s -> p (h s)"), see(act, ("sq", b))[:, :],
                               ACT.Copy, scale=float(P) ** -0.5), frees=("sq", b))
                if b < 3:
                    hi.upto(pos["sq", b] + NW)
                if b:
                    decays(b - 1)
                if b == 2:
                    for hp in range(2):
                        logs(hp)
            decays(3)
            for hp in range(2, 4):
                logs(hp)
            for hd in range(SH):
                A(V.activation(sU[:, hd, :], see(act, ("stay", hd))[:, 0:384], ACT.Exp), frees=("stay", hd))
            split_x(head_pairs)
            hi.upto(pos["sq", 3] + NW)

            def moe_hi(at, c):
                s = (M0 + c) % NW
                src, arrived = moe_raw(c)
                act.wait_ge(arrived, at(16 * (PC // NRX), 16 * (c // NRX + 1)))
                if c >= NW:
                    act.wait_ge(sg("moe_used"), at(PC, c - NW + 1))
                V.activation(wh[:, s, :], src, ACT.Copy).then_inc(sg("hi_moe"), 1)

            def at_first(a, b):
                return b

            for c in range(2):
                released(act, N_PRE - NW + c)
                moe_hi(at_first, c)
            norm(lambda t: [("swo", 0, t), ("swo", 1, t)])
            for c in range(2, NW):
                released(act, N_PRE - NW + c)
                moe_hi(at_first, c)
            act.wait_ge(sg("rt_max"), 1)
            A(V.activation(ex[:, :, :], ex[:, :, :], ACT.Exp), "rt_exp")
            act.dma_start(fgain, IN["final_norm"].rearrange("(a d) -> a d", a=1).to_broadcast([P, D])).then_inc(sg("fg_in"), 16)
            act.wait_ge(sg("more_ready"), 1)

            def xg_hi(value):
                for half in range(2):
                    act.wait_ge(sg("moe_xg"), value + half)
                    V.activation(xgh[:, 4 * half:4 * half + 4, :], xg[:, 4 * half:4 * half + 4, :], ACT.Copy).then_inc(sg("moe_xh"), 1)

            xg_hi(1)

            def experts(at, more_follow):
                for i in range(2):
                    def actT_hi(j):
                        n = NEJ * i + j
                        act.wait_ge(sg("moe_Tfull"), at(2 * NEJ, n + 1))
                        V.activation(eactTh[:, 4 * (n % 2):4 * (n % 2) + 4, :], bank[4][:, :].rearrange("p (k s) -> p k s", k=4),
                                     ACT.Copy).then_inc(sg("moe_actTh"), 1)

                    for q, (kind, j, k) in enumerate(uorder):
                        c = UC * i + q
                        if kind == "g" and k == 1:
                            n = NEJ * i + j
                            act.wait_ge(sg("moe_used"), at(PC, c + 1))
                            act.wait_ge(sg("moe_act"), at(2 * NEJ, n + 1))
                            V.activation(esg[:, n % 2, :], bank[n % 2][:, :], ACT.Silu).then_inc(sg("moe_silu"), 1)
                        tail = (kind, j, k) == ("d", NEJ - 2, 1)
                        if tail:
                            actT_hi(NEJ - 1)
                        if (kind, j, k) == ("d", NEJ - 1, 1):
                            act.wait_ge(sg("moe_used"), at(PC, UC * (i + 1)))
                            V.activation(ey[:, 0:512], bank[5][:, :], ACT.Copy).then_inc(sg("moe_y0"), 1)
                        if c + NW < PC or more_follow:
                            moe_hi(at, c + NW)
                        else:
                            hi.upto(N_PRE + c + NW - PC)
                        if kind == "g" and k == 1:
                            if j >= 1:
                                actT_hi(j - 1)
                            if j == 4:
                                act.wait_ge(sg("moe_ohfull"), at(2, i + 1))
                                V.activation(ohT, bank[7][:, 0:S], ACT.Copy).then_inc(sg("moe_ohT"), 1)
                        if tail:
                            xg_hi(at(4, 2 * i + 3))

            more = pairs(act, experts, hi)
            for t in range(TT):
                act.wait_ge(sg("moe_h"), more * 8 + (8 * NPAIR + 1 - 2 * (TT - 1 - t)))
                A(V.activation(junk, h[:, t, :], ACT.Square, accum_out=ssq[:, 2 * t:2 * t + 1]), "ssq_ready")
                act.wait_ge(sg("hg"), t + 1)
                A(V.activation(junk, xn[:, t, :], ACT.Square, accum_out=ssq[:, 2 * t + 1:2 * t + 2]), "ssq_ready")
            split_x(quarters("n4"))
            for c0, n, to in ((C_AV, AD, b_av), (C_BV, BD, b_bv), (C_BO, BD, b_bo), (C_CI, BD, b_ci), (C_CG, BD, b_cg)):
                act.dma_start(to, IN["b_in_2"][0:1, c0:c0 + n].to_broadcast([P, n])).then_inc(sg("tmb_in"), 16)
            hi.upto(pos["ak", 0])
            act.wait_ge(sg("c_pre"), 1)
            A(V.activation(m["Q"], m["Q"], ACT.Silu))
            A(V.activation(m["K"], m["E"], ACT.Sigmoid, scale=-1.0), "c_sig")
            A(V.activation(m["qt"], m["W"], ACT.Exp, scale=-1.0))
            A(V.activation(lbp, lbp, ACT.Exp), "c_lb")
            A(V.activation(m["qt"], m["qt"], ACT.Ln, bias=c_one), "c_ln")
            hi.upto(pos["ak", 1])
            act.wait_ge(sg("c_ls"), 1)
            A(V.activation(m["W"], m["W"], ACT.Exp), "c_exp")
            act.wait_ge(sg("c_mixd"), 1)
            A(V.activation(m["W"], m["W"], ACT.Ln), "c_ln2")
            act.wait_ge(sg("hl_A"), 1)

            def ahead(i):
                for nm in hl_pieces.get(i - 1, []):
                    if nm in pos:
                        hi.upto(pos[nm] + NW)
                if i == 4:
                    act.wait_ge(sg("row_abs"), 1)
                    A(V.activation(cS[0:72, :], cS[0:72, :], ACT.Exp, scale=-1.0))
                    A(V.activation(mS[0:72, :], mS[0:72, :], ACT.Exp, scale=-1.0))

            exps("hl", m, ahead)
            hi.upto(pos[("av",), 1] + NW)
            act.wait_ge(sg("aqk"), 1)
            A(V.activation(rs[:, 0:4 * S], aq.rearrange("p b s -> p (b s)"), ACT.Square))
            A(V.activation(rs[:, 4 * S:8 * S], ak.rearrange("p b s -> p (b s)"), ACT.Square), "qk_sq")
            A(V.activation(cS[0:72, :], cS[0:72, :], ACT.Ln, bias=c_one[0:72, :]))
            A(V.activation(mS[0:72, :], mS[0:72, :], ACT.Ln, bias=c_one[0:72, :]), "row_ln")
            for i in range(4):
                A(V.activation(rs[:, i * 512:(i + 1) * 512], see(act, ("qkss", i))[:, :], ACT.Ln, scale=1.0 / HD, bias=c_eps),
                  frees=("qkss", i))
            for i in range(2):
                A(V.activation(rs[:, i * 4 * S:(i + 1) * 4 * S], rs[:, i * 4 * S:(i + 1) * 4 * S], ACT.Exp, scale=-0.5), "qk_rstd")
            A(V.activation(cg[:, :, :], cg[:, :, :], ACT.Silu))
            for t in range(TT):
                gone(act, ("bvo", t))
            A(V.activation(bog[:, :, :], bog[:, :, :], ACT.Sigmoid), "gates")

            def probs(hd):
                act.wait_ge(sg("s_max"), hd + 1)
                for t in range(TT):
                    sl = sS[:, hd % 3, 0:P] if t == 0 else sS[:, hd % 3, P:3 * P]
                    k = hd * TT + t
                    A(V.activation(sl, sl, ACT.Exp, bias=nmx[:, k:k + 1], accum_out=asum[:, k:k + 1]), "s_exp")

            probs(0)
            for hd in range(AH):
                if hd + 1 < AH:
                    probs(hd + 1)
                if hd == 2:
                    hi.upto(pos[("w2", 1), 1])
                A(V.activation(pTs[:, hd % 2, :], see(act, ("pT", hd))[:, 0:384], ACT.Copy), frees=("pT", hd))
            act.wait_ge(sg("b_pre"), 12)
            A(V.activation(bc[:, :, :], bc[:, :, :], ACT.Silu), "b_act")
            act.wait_ge(sg("o_fox"), 1)
            A(V.activation(osq[:, 0:TT * AD].rearrange("p (t n) -> p t n", t=TT), o_all[:, :, 0:AD], ACT.Square))
            A(V.activation(osq[:, TT * AD:TT * (AD + BD)].rearrange("p (t n) -> p t n", t=TT), o_all[:, :, AD + BD:D], ACT.Square),
              "o_sq")
            mt = see(act, "mT")[:, :].rearrange("p (a t r) -> p a t r", a=2, t=TT)
            A(V.activation(em.rearrange("p (t h) -> p t h", t=TT), mt[:, 0, :, 0:BH], ACT.Exp, scale=-1.0))
            A(V.activation(iT.rearrange("p (t h) -> p t h", t=TT), mt[:, 1, :, 0:BH], ACT.Copy), frees="mT")
            for hd in range(BH):
                gone(act, ("P2", hd))
                for st in range(TT):
                    sl = Dm[:, hd % 2, 0:S] if st == 0 else Dm[:, hd % 2, S:384]
                    A(V.activation(sl, sl, ACT.Exp, bias=iT[:, st * BH + hd:st * BH + hd + 1]), "d_exp")
            split_x(quarters("yy", True)[0:2])
            act.wait_ge(sg("o_lstm"), 1)
            A(V.activation(osq[:, TT * (AD + BD):TT * D].rearrange("p (t n) -> p t n", t=TT), o_all[:, :, AD:AD + BD], ACT.Square),
              "o_sq")
            split_x(quarters("yy", True)[2:4])
            hi.upto(pos[("w2", 1), 1] + 2)
            norm(lambda t: [("w2", 0, t), ("w2", 1, t)])
            split_x(quarters("n5"))
            hi.upto(pos[("w2", 1), 1] + NW)
            ffn("f2", True)

        @block.vector
        def _(dve):
            C = Order(dve, "dve_order")
            V = nc.vector
            ssqs = [0]

            lo = Lo(dve, lambda i: i not in by_pool)

            def split_x(blocks, src=xT, first=False):
                for i, (lab, ix) in enumerate(blocks):
                    n_x[0] += 1
                    if (i < X_HALF) != first:
                        continue
                    dve.wait_ge(sg("xh_ready"), n_x[0])
                    C(V.tensor_tensor(xTl[ix], src[ix], xTh[ix].bitcast(F32), ALU.subtract), "xl_ready")

            n_x = [0]

            def mean_square(t, k):
                dve.wait_ge(sg("ssq_ready"), k)
                C(V.tensor_scalar(ms[:, t:t + 1], ssq[:, t:t + 1], 1.0 / D, EPS, ALU.mult, ALU.add), "ms_ready")

            def root():
                rst[0] += 1
                dve.wait_ge(sg("rstd_ready"), rst[0])

            def norm(n, dsts, add=lambda t: None, ahead=False, written=None, early=True):
                k = ssqs[0] = ssqs[0] + TT

                def scale(t):
                    root()
                    C(V.tensor_scalar(xn[:, t, :], h[:, t, :], rstd[:, t:t + 1], None, ALU.mult), "xn_ready")

                add(0)
                mean_square(0, k - 1)
                if early:
                    scale(0)
                    add(1)
                else:
                    add(1)
                    scale(0)
                if early and not ahead:
                    evac(n, dsts, None, order(False)[0:2])
                mean_square(1, k)
                if ahead:
                    tile_first(n, dsts, lambda: scale(1), written, n != "n3")
                else:
                    scale(1)
                    evac(n, dsts, None, order(False)[2 if early else 0:4])

            def tile_first(n, dsts, between, written=None, split=True):
                evac(n, dsts, None, order(False)[0:2], written)
                between()
                if split:
                    split_x(quarters(n), first=True)
                evac(n, dsts, None, order(False)[2:4], written)

            rst = [0]

            def tick(name=None, frees=None):
                C(V.tensor_copy(scr[:, :], c_one), name, frees)

            def evac(n, dsts, gain=None, parts=order(False), written=None):
                for t, half in parts:
                        ps = see(dve, (n, t, half))[:, :].rearrange("p (k s) -> p k s", k=4)
                        for i, (dst, nm, r0) in enumerate(dsts):
                            gains = cols(nm, r0 + 4 * half, 4) if gain is None else gain(half)
                            ins = V.tensor_tensor(dst[:, 4 * half:4 * half + 4, t * P:(t + 1) * P], ps,
                                                  gains.unsqueeze(2).to_broadcast([P, 4, P]), ALU.mult)
                            if written is not None:
                                C(ins, written)
                            elif i == len(dsts) - 1:
                                C(ins, frees=(n, t, half))
                            else:
                                C(ins)

            def add_h(nm, between):
                def part(c, t):
                    hs = h[:, t, c * 512:(c + 1) * 512]
                    C(V.tensor_tensor(hs, hs, see(dve, (nm, c, t))[:, :], ALU.add), frees=(nm, c, t))

                between()
                return lambda t: [part(c, t) for c in range(2)]

            def levels(pre, T, cross, between):
                def half(a, mh, j):
                    return a.rearrange("p (n two m) -> p n two m", two=2, m=mh)[:, :, j, :]

                def qk(i):
                    mh = (LEVELS[1:] + [P])[i]
                    dve.wait_ge(sg(pre + "_exp"), 2 * (i + 1))
                    C(V.tensor_tensor(half(T["qt"], mh, 1), half(T["Q"], mh, 1), half(T["W"], mh, 1), ALU.mult), pre + "_qk")
                    C(V.tensor_tensor(half(T["kt"], mh, 0), half(T["K"], mh, 0), half(T["W"], mh, 0), ALU.mult), pre + "_qk")

                qk(0)
                for i, mh in enumerate(LEVELS):
                    between(i)
                    ps = [see(dve, (pre, mh, gg))[:, :].rearrange("p (e s) -> p e s", e=4) for gg in range(2)]
                    if i:
                        qk(i)
                    if mh == P // 2:
                        for gg in range(2):
                            a4 = T["att"][0:mh, gg, :].rearrange("p (e s) -> p e s", e=4)[:, :, mh:P]
                            C(V.tensor_tensor(a4, a4, ps[gg][0:mh, :, mh:P], ALU.add), frees=(pre, mh, gg))
                        continue
                    for gg in range(2):
                        a4 = T["att"][:, gg, :].rearrange("p (e s) -> p e s", e=4)
                        if i == 0:
                            C(V.tensor_tensor(a4, ps[gg], ident[:, :].unsqueeze(1).to_broadcast([P, 4, P]), ALU.mult),
                              frees=(pre, mh, gg))
                        else:
                            mask = lmask[:, i - 1, :].bitcast(I32).unsqueeze(1).to_broadcast([P, 4, P])
                            C(V.copy_predicated(a4, mask, ps[gg]), frees=(pre, mh, gg))
                w = 512 // cross
                for gg in range(cross):
                    C(V.tensor_copy(T["crs"][:, gg * w:(gg + 1) * w], see(dve, (pre, P, gg))[:, 0:w]), frees=(pre, P, gg))

            def bcast(a, shape):
                return a.unsqueeze(len(shape) - 1).to_broadcast(shape)

            dve.wait_ge(sg("const"), 2)

            def first_vectors():
                C(V.tensor_copy(vT[:, 0, 0:V_EARLY], see(dve, ("vec", "early"))[:, 0:V_EARLY]), frees=("vec", "early"))

            norm("n0", [(xT, "attn_norm", 0)], lambda t: first_vectors() if t == 0 else None, early=False)
            split_x(quarters("n0"))
            lo.upto(0)
            C(V.tensor_copy(glrT, see(dve, "glr")[0:GR, 0:S]), frees="glr")
            lo.upto(1)
            dve.wait_ge(sg("masks"), 1)
            for b in range(2):
                C(V.tensor_tensor(g["A"][:, b * 512:(b + 1) * 512].rearrange("p (e s) -> p e s", e=2),
                                  see(dve, ("gate", b))[:, :].rearrange("p (e s) -> p e s", e=2),
                                  bcast(cols("gla_b_gate", 2 * b, 2), [P, 2, S]), ALU.add), frees=("gate", b))
            C(V.scalar_tensor_tensor(g["W"], g["A"], -1.0, g["A"], ALU.mult, ALU.max), "gl_abs")
            lo.upto(3)
            dve.wait_ge(sg("gl_ln"), 1)
            C(V.scalar_tensor_tensor(g["A"], g["A"], 0.0, g["W"], ALU.min, ALU.subtract))
            C(V.tensor_scalar(g["A"], g["A"], 1.0 / GATE_NORM, None, ALU.mult), "gl_A")
            lo.upto(pos[("v", 0), 1])
            for lab in (("q", 0), ("q", 1), ("k", 0), ("k", 1)):
                gone(dve, lab)

            def ahead(i):
                nm, c, t = gl_tm[i]
                if t == TT - 1:
                    lo.upto(pos[(nm, c), 1] + 2)
                if i == 4:
                    for k in range(3):
                        r0 = 32 if k == 0 else 0
                        C(V.tensor_copy(vT[:, k, r0:V_ROWS[k]], see(dve, ("vec", k))[:, r0:V_ROWS[k]]), frees=("vec", k))

            levels("gl", g, 1, ahead)
            def head_means(hp):
                cs = slice(hp * GH, (hp + 1) * GH)
                dve.wait_ge(sg("gssq_ready"), GH * (hp + 1))
                C(V.tensor_scalar(ms[:, cs], ssq[:, cs], 1.0 / GDV, EPS, ALU.mult, ALU.add), "ms_ready")

            head_means(0)
            dve.wait_ge(sg("gr_ready"), 1)

            def gated(t, hp):
                o = see(dve, ("o", t, hp))
                for i in range(2):
                    cs = slice((2 * hp + i) * GDV, (2 * hp + i + 1) * GDV)
                    k = hp * GH + 2 * t + i
                    ins = V.scalar_tensor_tensor(xn[:, t, cs], o[:, i * GDV:(i + 1) * GDV], rstd[:, k:k + 1],
                                                 gr[:, t, cs], ALU.mult, ALU.mult)
                    if i == 1:
                        C(ins, frees=("o", t, hp))
                    else:
                        C(ins)

            def two_gains(half):
                return cols("gla_head_norm", 0, 4)

            root()
            for t in range(TT):
                gated(t, 0)
            head_means(1)
            evac("y", [(xT, "gla_head_norm", 0)], two_gains, order(True)[0:2])
            split_x(quarters("y", True), first=True)
            root()
            for t in range(TT):
                gated(t, 1)
            evac("y", [(xT, "gla_head_norm", 0)], two_gains, order(True)[2:4])
            last = add_h("wo", lambda: lo.upto(pos[("wo", 1), 1] + 2))
            norm("n1", [(xT, "ffn_norm", 0)], last)
            split_x(quarters("n1"))
            lo.upto(pos[("wo", 1), 1] + NW)

            def ffn(f, conv):
                for j in range(NJ1):
                    lo.upto(pos[f, j, "g"] + NW - 1)
                    if conv:
                        for i in range(2):
                            ps = see(dve, (f, j, "gu"[i]))
                            dve.wait_ge(sg("conv0"), 4 * j + 2 * (i + 1))
                            for b in range(2):
                                k = i * (F2 // P) + 2 * j + b
                                cu = f_cu[:, j % 2, (2 * i + b) * S:(2 * i + b + 1) * S]
                                x = ps[:, b * S:(b + 1) * S]
                                C(V.scalar_tensor_tensor(cu[:, 1:S], x[:, 0:S - 1], col("tap01", NF2 + k), cu[:, 1:S],
                                                         ALU.mult, ALU.add))
                                ins = V.scalar_tensor_tensor(cu[:, 2:S], x[:, 0:S - 2], col("tap01", k), cu[:, 2:S],
                                                             ALU.mult, ALU.add)
                                if b == 1:
                                    C(ins, frees=(f, j, "gu"[i]))
                                else:
                                    C(ins)
                            if i == 0:
                                lo.upto(min(pos[f, j, "g"] + NW, len(pieces) - 1))
                        dve.wait_ge(sg("silu_" + f), j + 1)
                        lhs, rhs = f_sg[:, j % 2, :], f_cu[:, j % 2, 512:1024]
                    else:
                        gone(dve, (f, j, "g"))
                        lhs, rhs = f_sg[:, j % 2, :], see(dve, (f, j, "u"))[:, :]
                    if j >= 2:
                        dve.wait_ge(sg("down_done_" + f), j - 1)
                    ins = V.tensor_tensor(f_act[:, j % 2, :], lhs, rhs, ALU.mult)
                    C(ins, "act_" + f)
                    if not conv:
                        tick(frees=(f, j, "u"))
                    lo.upto(min(pos[f, j, "g"] + NW, len(pieces) - 1))
                    dve.wait_ge(sg("acth_" + f), j + 1)
                    C(V.tensor_tensor(actl[:, j % 2, :], f_act[:, j % 2, :], acth[:, j % 2, :].bitcast(F32), ALU.subtract),
                      "actl_" + f)
                lo.upto(min(pos[f, NJ1 - 1, "d"] + 2, len(pieces) - 1))

                def last(t):
                    for half in range(2):
                        hs = h[:, t, half * 512:(half + 1) * 512]
                        C(V.tensor_tensor(hs, hs, see(dve, (f, "acc", t, half))[:, :], ALU.add), frees=(f, "acc", t, half))

                return last

            last = ffn("f1", False)
            norm("n2", [(xT, "kv_norm", 0)], last, True, "kv_x", False)
            evac("n2", [(xq, "attn_norm", KD)])
            lo.upto(pos["sq", 1])
            split_x(quarters("n2"), xq)
            lo.upto(pos["sq", 2] + NW)
            dve.wait_ge(sg("masks2"), 1)

            def two(a):
                return a.rearrange("p (a s) -> p a s", a=3)[:, 0::2, :]

            def weights(hd):
                gone(dve, ("stay", hd))
                C(V.tensor_tensor(two(sU[:, hd, :]), two(sU[:, hd, :]), before3[:, 0::2, :], ALU.mult), "sb_wm")

            for hd in range(SH):
                dve.wait_ge(sg("sb_ln"), hd // 2 + 1)
                z = see(dve, ("z", hd))[:, 0:384]
                C(V.scalar_tensor_tensor(sU[:, hd, :], z, 0.0, sE[:, hd, :], ALU.min, ALU.subtract))
                C(V.scalar_tensor_tensor(sT[:, hd, :], z, 0.0, sE[:, hd, :], ALU.max, ALU.add), frees=("z", hd))
                C(V.tensor_tensor(two(sT[:, hd, :]), two(sT[:, hd, :]), before3[:, 0::2, :], ALU.mult), "sb_keep")
                if hd >= 4:
                    weights(hd - 4)
            for hd in range(SH - 4, SH):
                weights(hd)
            for hp in range(SH // 2):
                C(V.tensor_copy(xT[:, 2 * hp:2 * hp + 2, :].rearrange("p k s -> p (k s)"), see(dve, ("so", hp))[:, :]),
                  frees=("so", hp))
                if hp == 1:
                    split_x(head_pairs, first=True)
            lo.upto(pos["sq", 3] + NW)

            def moe_lo_one(at, c):
                s = (M0 + c) % NW
                dve.wait_ge(sg("hi_moe"), at(PC, c + 1))
                V.tensor_tensor(wl[:, s, 0:LO_V], moe_raw(c)[0][:, 0:LO_V], wh[:, s, 0:LO_V].bitcast(F32),
                                ALU.subtract).then_inc(lo_moe[0], 1)

            def at_first(a, b):
                return b

            last = add_h("swo", lambda: [moe_lo_one(at_first, c) for c in range(2)])
            norm("n3", [(xT, "ffn_norm", KD)], last, True)
            C(V.memset(pm, -1.0))
            C(V.memset(gt, 0.0))
            C(V.tensor_copy(lg, see(dve, "lg")[:, 0:TT * NE].rearrange("p (t e) -> p t e", t=TT)), frees="lg")
            le = lg.unsqueeze(3).to_broadcast([P, TT, NE, NE])
            lj = lg.unsqueeze(2).to_broadcast([P, TT, NE, NE])
            C(V.tensor_tensor(cmp1, lj, le, ALU.is_gt))
            C(V.tensor_tensor(cmp2, lj, le, ALU.is_equal))
            C(V.tensor_tensor(cmp2, cmp2, tri8[:, :, :].unsqueeze(1).to_broadcast([P, TT, NE, NE]), ALU.mult))
            C(V.tensor_tensor(cmp1, cmp1, cmp2, ALU.add))
            C(V.tensor_reduce(rank, cmp1, AX.X, ALU.add))
            C(V.tensor_scalar(selx, rank, 1.5, None, ALU.is_lt), "rt_sel")
            C(V.tensor_reduce(mx, lg, AX.X, ALU.max))
            C(V.tensor_tensor(ex, lg, bcast(mx, [P, TT, NE]), ALU.subtract), "rt_max")
            pp = see(dve, "pos")[:, 0:TT * NE].rearrange("p (t e) -> p t e", t=TT)
            C(V.scalar_tensor_tensor(lg, pp, 1.0, selx, ALU.add, ALU.mult), frees="pos")
            for k in range(2):
                C(V.tensor_scalar(pm[:, k * NE:(k + 1) * NE, :], lg.rearrange("p t e -> p e t"), -1.0 - P * k, None, ALU.add))
            iota2 = iota[:, :].unsqueeze(1).to_broadcast([P, TT, P])

            def onehot(u, value):
                pmu = pm[:, bass.ds(u, 1), :].rearrange("p a t -> p (a t)")
                V.tensor_tensor(oh, iota2, pmu.unsqueeze(2).to_broadcast([P, TT, P]), ALU.is_equal).then_inc(sg("moe_oh"), 1)
                dve.wait_ge(sg("moe_oh"), value)

            def onehot_gate(u, value):
                gtu = gt[:, bass.ds(u, 1), :].rearrange("p a t -> p (a t)")
                V.tensor_tensor(ohg, oh, gtu.unsqueeze(2).to_broadcast([P, TT, P]), ALU.mult).then_inc(sg("moe_oh"), 1)
                dve.wait_ge(sg("moe_oh"), value)

            def gather_out(half, b, value):
                dve.wait_ge(sg("moe_xgfull"), value)
                V.tensor_tensor(xg[:, 4 * half:4 * half + 4, :], b[:, :].rearrange("p (k s) -> p k s", k=4),
                                cols("ffn_norm", KD + 4 * half, 4).unsqueeze(2).to_broadcast([P, 4, P]),
                                ALU.mult).then_inc(sg("moe_xg"), 1)

            def xg_lo(half, value):
                hs = slice(4 * half, 4 * half + 4)
                dve.wait_ge(sg("moe_xh"), value)
                V.tensor_tensor(xgl[:, hs, :], xg[:, hs, :], xgh[:, hs, :].bitcast(F32), ALU.subtract).then_inc(sg("moe_xl"), 1)

            onehot(0, 1)
            C(V.tensor_reduce(cmax[0:1, 0:1], see(dve, "cnt")[0:1, 0:NE], AX.X, ALU.max), frees="cnt")
            C(V.tensor_scalar(cmax[0:1, 1:2], cmax[0:1, 0:1], P + 0.5, float(NPAIR), ALU.is_gt, ALU.mult))
            C(V.tensor_copy(more_i[0:1, 0:1], cmax[0:1, 1:2]), "more_ready")
            tick("moe_act")
            tick("moe_act")
            tick("moe_h")
            for half in range(2):
                gather_out(half, bank[7 if half == 0 else 0], half + 1)
            for half in range(2):
                xg_lo(half, half + 1)
            dve.wait_ge(sg("rt_exp"), 1)
            C(V.tensor_tensor(ex, ex, selx, ALU.mult))
            C(V.tensor_reduce(exs, ex, AX.X, ALU.add))
            C(V.reciprocal(exs, exs))
            for k in range(2):
                C(V.tensor_tensor(gt[:, k * NE:(k + 1) * NE, :], ex.rearrange("p t e -> p e t"),
                                  exs.unsqueeze(1).to_broadcast([P, NE, TT]), ALU.mult))
            onehot_gate(0, 2)
            for c in range(2, NW):
                moe_lo_one(at_first, c)

            def experts(at, more_follow):
                for i in range(2):
                    def actT_lo(j):
                        n = NEJ * i + j
                        ks = slice(4 * (n % 2), 4 * (n % 2) + 4)
                        dve.wait_ge(sg("moe_actTh"), at(2 * NEJ, n + 1))
                        V.tensor_tensor(eactTl[:, ks, :], bank[4][:, :].rearrange("p (k s) -> p k s", k=4),
                                        eactTh[:, ks, :].bitcast(F32), ALU.subtract).then_inc(sg("moe_actTl"), 1)

                    def weights_lo(q):
                        if UC * i + q + NW < PC or more_follow:
                            moe_lo_one(at, UC * i + q + NW)

                    for q, (kind, j, k) in enumerate(uorder[:-2]):
                        tail = (kind, j, k) == ("d", NEJ - 2, 1)
                        if tail:
                            gather_out(0, bank[7], at(4, 2 * i + 3))
                            actT_lo(NEJ - 1)
                            gather_out(1, bank[(NEJ * (i + 1)) % 2], at(4, 2 * i + 4))
                        weights_lo(q)
                        if not more_follow and UC * i + q + NW >= PC:
                            lo.upto(N_PRE + UC * i + q + NW - PC)
                        if tail:
                            for half in range(2):
                                xg_lo(half, at(4, 2 * i + 3 + half))
                        if kind == "g" and k == 1 and j >= 1:
                            actT_lo(j - 1)
                        if kind == "u" and k == 1:
                            n = NEJ * i + j
                            dve.wait_ge(sg("moe_used"), at(PC, UC * i + q + 1))
                            dve.wait_ge(sg("moe_silu"), at(2 * NEJ, n + 1))
                            V.tensor_tensor(eact[:, n % 2, :], esg[:, n % 2, :], bank[2 + n % 2][:, :],
                                            ALU.mult).then_inc(sg("moe_act"), 1)
                            if j == 4:
                                dve.wait_ge(sg("moe_ohfull"), at(2, i + 1))
                                onehot(at(2, i + 1), at(4, 2 * i + 3))
                                onehot_gate(at(2, i + 1), at(4, 2 * i + 4))
                    dve.wait_ge(sg("moe_used"), at(PC, UC * (i + 1)))
                    V.tensor_copy(ey[:, 512:1024], bank[6][:, :]).then_inc(sg("moe_y1"), 1)
                    for q in range(4):
                        t, half = q // 2, q % 2
                        dve.wait_ge(sg("moe_scfull"), at(8, 4 * i + q + 1))
                        hs = h[:, t, half * 512:(half + 1) * 512]
                        V.tensor_tensor(hs, hs, bank[7 if q % 2 == 0 else 4][:, :], ALU.add).then_inc(sg("moe_h"), 1)
                    weights_lo(UC - 2)
                    weights_lo(UC - 1)

            more = pairs(dve, experts)
            dve.wait_ge(sg("fg_in"), 16)
            for t in range(TT):
                dve.wait_ge(sg("moe_h"), more * 8 + (8 * NPAIR + 1 - 2 * (TT - 1 - t)))
                C(V.tensor_tensor(xn[:, t, :], h[:, t, :], fgain, ALU.mult), "hg")

            def both_means(t):
                a, b = slice(2 * t, 2 * t + 1), slice(2 * t + 1, 2 * t + 2)
                dve.wait_ge(sg("ssq_ready"), ssqs[0] + 2 * (t + 1))
                C(V.tensor_scalar(ms[:, a], ssq[:, a], 1.0 / D, EPS, ALU.mult, ALU.add))
                C(V.tensor_scalar(ms[:, b], ssq[:, b], 1.0 / D, None, ALU.mult))
                C(V.scalar_tensor_tensor(ms[:, b], ms[:, a], EPS, ms[:, b], ALU.mult, ALU.add), "ms_ready")

            def scale_both(t):
                root()
                C(V.tensor_scalar(xn[:, t, :], xn[:, t, :], rstd[:, 2 * t + 1:2 * t + 2], None, ALU.mult), "xn_ready")

            both_means(0)
            scale_both(0)
            both_means(1)
            ssqs[0] += 2 * TT
            tile_first("n4", [(xT, "norm_mix_g_2", 0)], lambda: scale_both(1))
            for t in range(TT):
                C(V.scalar_tensor_tensor(h[:, t, :], h[:, t, :], rstd[:, 2 * t:2 * t + 1], fgain, ALU.mult, ALU.mult))
            lo.upto(N_PRE + NW - 1)
            dve.wait_ge(sg("mix_zero"), 1)

            def fm_bias(dst, lab, nm, r0):
                C(V.tensor_tensor(dst, see(dve, lab)[:, :].rearrange("p (e s) -> p e s", e=2),
                                  bcast(cols(nm, r0, 2), [P, 2, S]), ALU.add), frees=lab)

            q3 = m["Q"].rearrange("p (e s) -> p e s", e=2)
            f3 = m["E"].rearrange("p (e s) -> p e s", e=2)
            fm_bias(q3, ("cqf", 0), "cqf_b", 0)
            lo.upto(pos["aq", 1])
            fm_bias(f3, ("cqf", 1), "cqf_b", 2)
            lbl = cols("lb_logits_2", 0, 2)
            C(V.tensor_tensor(lbp, lbl, lbl, ALU.subtract))
            C(V.scalar_tensor_tensor(m["W"], m["E"], -1.0, m["E"], ALU.mult, ALU.max), "c_pre")
            dve.wait_ge(sg("c_lb"), 1)
            C(V.reciprocal(lb1, lbp))
            C(V.tensor_tensor(lbp, lbp, lb1, ALU.mult))
            C(V.tensor_tensor(lbp, lbp, lbp, ALU.subtract))
            C(V.tensor_scalar(lbp, lbp, 0.0, None, ALU.max))
            C(V.tensor_scalar(lb1, lbp, -1.0, 1.0, ALU.mult, ALU.add))
            dve.wait_ge(sg("c_ln"), 1)
            C(V.scalar_tensor_tensor(m["A"], m["E"], 0.0, m["qt"], ALU.min, ALU.subtract))
            C(V.tensor_scalar(m["W"], m["A"], -1.0, 80.0, ALU.mult, ALU.min), "c_ls")
            C(V.memset(m["E"], 0.0))
            C(V.memset(m["qt"], 0.0))
            dve.wait_ge(sg("c_exp"), 1)
            for b in range(2):
                bs = slice(b * S, (b + 1) * S)
                C(V.tensor_scalar(m["W"][:, bs], m["W"][:, bs], lbp[:, b:b + 1], lb1[:, b:b + 1], ALU.mult, ALU.add))
                C(V.tensor_scalar(m["K"][:, bs], m["K"][:, bs], lb1[:, b:b + 1], None, ALU.mult))
            tick("c_mixd")
            dve.wait_ge(sg("c_ln2"), 1)
            C(V.tensor_tensor(m["A"], m["A"], m["W"], ALU.add), "hl_A")
            rw = slice(0, 72)
            dve.wait_ge(sg("tmb_in"), 16 * 5)
            for t in range(TT):
                ps = see(dve, ("cig", t))
                C(V.tensor_tensor(ci[:, t, :], ps[:, 0:BD], b_ci, ALU.add), "ci")
                C(V.tensor_tensor(cg[:, t, :], ps[:, BD:2 * BD], b_cg, ALU.add), frees=("cig", t))

            def projections(i):
                for nm in hl_pieces.get(i, []):
                    if nm == "rows":
                        for lab in ("cf", "bi", "bf"):
                            see(dve, lab)
                        C(V.memset(xT[:, 0:5, :], 0.0))
                        for lab, dst, k in (("cf", ncS, 0), ("bi", iF, 1), ("bf", nM, 2)):
                            C(V.tensor_scalar(dst[rw, :], see(dve, lab)[rw, 0:S], vT[rw, 0, R_G + 2 + k:R_G + 3 + k], None, ALU.add),
                              frees=lab)
                        C(V.scalar_tensor_tensor(cS[rw, :], ncS[rw, :], -1.0, ncS[rw, :], ALU.mult, ALU.max))
                        C(V.scalar_tensor_tensor(mS[rw, :], nM[rw, :], -1.0, nM[rw, :], ALU.mult, ALU.max), "row_abs")
                        continue
                    if nm[0] == "av":
                        t = nm[1]
                        C(V.tensor_tensor(av[:, t, :], see(dve, nm)[:, :], b_av, ALU.add), frees=nm)
                        lo.upto(pos[("av",), t] + 2)
                        continue
                    lo.upto(pos[nm] + 2)
                    b = nm[1]
                    fm_bias({"aq": aq, "ak": ak, "bqk": bz}[nm[0]][:, 2 * b:2 * b + 2, :], nm, nm[0] + "_b", 2 * b)

            def bvo(t):
                ps = see(dve, ("bvo", t))
                C(V.tensor_tensor(bv[:, t, :, 0:HD], ps[:, 0:BD].rearrange("p (h n) -> p h n", h=BH),
                                  b_bv.rearrange("p (h n) -> p h n", h=BH), ALU.add), "bv")
                C(V.tensor_tensor(bog[:, t, :], ps[:, BD:2 * BD], b_bo, ALU.add), frees=("bvo", t))

            levels("hl", m, 2, projections)
            C(V.tensor_copy(gq[:, 1:2], vT[:, 0, R_G + 1:R_G + 2]))
            C(V.tensor_scalar(gq[:, 0:1], vT[:, 0, R_G:R_G + 1], HD ** -0.5, None, ALU.mult), "aqk")
            bvo(0)
            dve.wait_ge(sg("row_ln"), 1)
            C(V.scalar_tensor_tensor(cS[rw, :], ncS[rw, :], 0.0, cS[rw, :], ALU.min, ALU.subtract))
            C(V.scalar_tensor_tensor(mS[rw, :], nM[rw, :], 0.0, mS[rw, :], ALU.min, ALU.subtract))
            C(V.memset(row1, 1.0))
            C(V.tensor_tensor_scan(ncS[rw, :], row1[rw, :], cS[rw, :], 0.0, ALU.mult, ALU.add))
            C(V.tensor_tensor_scan(nM[rw, :], row1[rw, :], mS[rw, :], 0.0, ALU.mult, ALU.add))
            C(V.tensor_scalar(ncS[rw, :], ncS[rw, :], -1.0, None, ALU.mult), "c_rows")
            C(V.tensor_tensor(iF[rw, :], iF[rw, :], nM[rw, :], ALU.subtract))
            C(V.tensor_tensor_scan(row1[rw, :], iF[rw, :], iF[rw, :], -3.0e38, ALU.max, ALU.max))
            C(V.tensor_tensor(mS[rw, :], nM[rw, :], row1[rw, :], ALU.add))
            C(V.tensor_scalar(nM[rw, :], row1[rw, :], -1.0, None, ALU.mult), "m_rows")
            bvo(1)
            for t in range(TT):
                C(V.tensor_copy(o_all[:, t, AD + BD:AD + 2 * BD], see(dve, ("co", t))[:, 0:BD]), frees=("co", t))
            for dst, i in ((aq, 0), (ak, 1)):
                dve.wait_ge(sg("qk_rstd"), i + 1)
                d2 = dst.rearrange("p b s -> p (b s)")
                C(V.scalar_tensor_tensor(d2, d2, gq[:, i:i + 1], rs[:, i * 4 * S:(i + 1) * 4 * S], ALU.mult, ALU.mult), "qk_n")
            r3 = rowneg3.rearrange("p a s -> p (a s)")

            for hd in range(AH):
                if hd >= 3:
                    see(dve, ("pT", hd - 3))
                row = sS[:, hd % 3, :]
                C(V.tensor_tensor(row, see(dve, ("s", hd))[:, 0:384], r3, ALU.add), frees=("s", hd))
                C(V.tensor_reduce(nmx[:, hd * TT:hd * TT + 1], row[:, 0:P], AX.X, ALU.max, negate=True))
                C(V.tensor_reduce(nmx[:, hd * TT + 1:hd * TT + 2], row[:, P:3 * P], AX.X, ALU.max, negate=True), "s_max")
            dve.wait_ge(sg("s_exp"), AH * TT)
            C(V.reciprocal(arec, asum))
            for t in range(TT):
                C(V.tensor_tensor(o_all[:, t, 0:AD].rearrange("p (h n) -> p h n", h=AH),
                                  see(dve, ("ao", t))[:, :].rearrange("p (h n) -> p h n", h=AH),
                                  bcast(arec.rearrange("p (h t) -> p h t", t=TT)[:, :, t], [P, AH, HD]), ALU.mult), frees=("ao", t))
            tick("o_fox")
            c3 = colneg3.rearrange("p a s -> p (a s)")

            def exponents(hd):
                C(V.tensor_tensor(Dm[:, hd % 2, :], see(dve, ("P2", hd))[:, 0:384], c3, ALU.add), frees=("P2", hd))

            def mean_squares(c0, a, n):
                C(V.tensor_reduce(ssq[:, c0:c0 + TT * n], a.rearrange("p (g n) -> p g n", n=HD), AX.X, ALU.add))

            def scaled(a, c0, n):
                o4 = a.rearrange("p t (g n) -> p t g n", n=HD)
                C(V.tensor_tensor(o4, o4, rstd[:, c0:c0 + TT * n].rearrange("p (t g) -> p t g", t=TT).unsqueeze(3)
                                  .to_broadcast([P, TT, n, HD]), ALU.mult))

            o_b, o_c = o_all[:, :, AD:AD + BD], o_all[:, :, AD + BD:D]
            exponents(0)
            dve.wait_ge(sg("o_sq"), 1)
            mean_squares(0, osq[:, 0:TT * AD], AH)
            mean_squares(16, osq[:, TT * AD:TT * (AD + BD)], CH)
            C(V.tensor_scalar(ms[:, 0:24], ssq[:, 0:24], 1.0 / HD, EPS, ALU.mult, ALU.add), "ms_ready")
            for hd in range(BH):
                if hd + 1 < BH:
                    exponents(hd + 1)
                if hd == BH - 1:
                    root()
                    scaled(o_all[:, :, 0:AD], 0, AH)
                    tick("o_a")
                p1 = see(dve, ("P1", hd))[:, 0:384]
                dve.wait_ge(sg("d_exp"), TT * (hd + 1))
                if hd >= 3:
                    dve.wait_ge(sg("b_pv"), hd - 2)
                C(V.scalar_tensor_tensor(sS[:, hd % 3, :], p1, HD ** -0.5, Dm[:, hd % 2, :], ALU.mult, ALU.mult), frees=("P1", hd))
            evac("yy", [(xT, "out_g_2", 0)], None, order(True)[0:2])
            scaled(o_c, 16, CH)
            C(V.tensor_tensor(o_c, o_c, cg, ALU.mult))
            split_x(quarters("yy", True), first=True)
            gone(dve, "mT")
            for t in range(TT):
                ps = see(dve, ("bo", t))[:, 0:BH * 65].rearrange("p (h n) -> p h n", h=BH)
                dn = den[:, t * BH:(t + 1) * BH]
                C(V.tensor_copy(dn, ps[:, :, HD]))
                C(V.scalar_tensor_tensor(dn, dn, -1.0, dn, ALU.mult, ALU.max))
                C(V.tensor_tensor(dn, dn, em[:, t * BH:(t + 1) * BH], ALU.max))
                C(V.reciprocal(dn, dn))
                C(V.tensor_tensor(o_all[:, t, AD:AD + BD].rearrange("p (h n) -> p h n", h=BH), ps[:, :, 0:HD],
                                  bcast(dn, [P, BH, HD]), ALU.mult), frees=("bo", t))
            tick("o_lstm")
            dve.wait_ge(sg("o_sq"), 2)
            mean_squares(24, osq[:, TT * (AD + BD):TT * D], BH)
            C(V.tensor_scalar(ms[:, 24:32], ssq[:, 24:32], 1.0 / HD, EPS, ALU.mult, ALU.add), "ms_ready")
            root()
            scaled(o_b, 24, BH)
            C(V.tensor_tensor(o_b, o_b, bog, ALU.mult), "o_done")
            evac("yy", [(xT, "out_g_2", 0)], None, order(True)[2:4])
            last = add_h("w2", lambda: lo.upto(pos[("w2", 1), 1] + 2))
            norm("n5", [(xT, "norm_ffn_g_2", 0)], last)
            split_x(quarters("n5"))
            lo.upto(pos[("w2", 1), 1] + NW)
            last = ffn("f2", True)
            for t in range(TT):
                last(t)

        @block.tensor
        def _(pe):
            T = nc.tensor

            def take(label):
                b, n = turns[label]
                if n:
                    pe.wait_ge(freed[b], n)
                return bank[b]

            def done(ins, label):
                ins.then_inc(full[turns[label][0]], 1)

            n_xn = [0]

            def transposes(n, ready, parts=order(False)):
                for t, half in parts:
                    ready(t, half)
                    ps = take((n, t, half))
                    for k in range(4):
                        kk = 4 * half + k
                        ins = T.transpose(ps[:, k * P:(k + 1) * P], xn[:, t, kk * P:(kk + 1) * P], ident[:, :])
                    done(ins, (n, t, half))

            def x_done(n, tiles=range(TT)):
                for t in tiles:
                    for half in range(2):
                        gone(pe, (n, t, half))

            def x_split():
                n_x[0] += 1
                pe.wait_ge(sg("xl_pool"), X_HALF * n_x[0] - 1)
                pe.wait_ge(sg("xl_ready"), X_HALF * n_x[0] - 1)

            def x_first():
                n_x[0] += 1
                pe.wait_ge(sg("xl_ready"), X_HALF * n_x[0])

            def x_rest():
                pe.wait_ge(sg("xl_pool"), X_HALF * n_x[0])
                pe.wait_ge(sg("xl_ready"), X_HALF * n_x[0])

            n_x = [0]

            def norm(n):
                n0 = n_xn[0]
                n_xn[0] += TT
                transposes(n, lambda t, half: pe.wait_ge(sg("xn_ready"), n0 + t + 1))

            def mm3(o, xh, xl, yh, yl, first, last):
                T.matmul(o, xh, yh, start=first, stop=False)
                T.matmul(o, xh, yl, start=False, stop=False)
                return T.matmul(o, xl, yh, start=False, stop=last)

            def fm(label, fresh=False):
                ps, i = take(label), pos[label]
                split_done(pe, i)
                h_, l_ = of(wh, i, KD), of(wl, i, KD)
                for j in range(2):
                    js = slice(j * P, (j + 1) * P)
                    for k in range(KD):
                        if fresh and j == 0 and k == KD // 2:
                            x_rest()
                        ins = mm3(ps[:, j * S:(j + 1) * S], h_[:, k, js], l_[:, k, js], xTh[:, k, :], xTl[:, k, :],
                                  k == 0, k == KD - 1)
                done(ins, label)

            def tm(nm, tiles=range(TT)):
                for t in tiles:
                    ts = slice(t * P, (t + 1) * P)
                    ps = take(nm + (t,))
                    for half in range(2):
                        i = pos[nm, half]
                        split_done(pe, i)
                        h_, l_ = of(wh, i, 4), of(wl, i, 4)
                        for k in range(4):
                            kk = 4 * half + k
                            ins = mm3(ps[:, :], xTh[:, kk, ts], xTl[:, kk, ts], h_[:, k, :], l_[:, k, :],
                                      kk == 0, kk == KD - 1)
                    done(ins, nm + (t,))

            def out_proj(nm, at=None, between=None):
                def part(c, t, half):
                    lab, i = (nm, c, t), pos[(nm, c), half]
                    ps = take(lab) if half == 0 else bank[turns[lab][0]]
                    ts = slice(t * P, (t + 1) * P)
                    split_done(pe, i)
                    h_, l_ = of(wh, i, 4), of(wl, i, 4)
                    for k in range(4):
                        kk = 4 * half + k
                        ins = mm3(ps[:, :], xTh[:, kk, ts], xTl[:, kk, ts], h_[:, k, :], l_[:, k, :], kk == 0, kk == KD - 1)
                    if half:
                        done(ins, lab)
                    return ins

                x_first()
                for c in range(2):
                    for t in range(TT):
                        ins = part(c, t, 0)
                        if t == TT - 1:
                            ins.then_inc(sg("down_done_" + nm), 1)
                        if TT * c + t == at:
                            between()
                x_rest()
                for t in range(TT):
                    for c in range(2):
                        part(c, t, 1)

            def levels(pre, T_, heads, between, first):
                ent = [[(h_, st) for h_ in range(4)] for st in range(2)] if heads else \
                      [[(2 * b + hf, st) for st in range(2) for b in range(2)] for hf in range(2)]

                def operands(hd, lo, hi, level):
                    rws = slice(0, P) if heads else slice(64 * (hd % 2), 64 * (hd % 2) + 64)
                    o = (hd if heads else hd // 2) * S
                    kk, qq = (T_["K"], T_["Q"]) if level == 0 else (T_["kt"], T_["qt"])
                    return kk[rws, o + lo * P:o + (lo + 1) * P], qq[rws, o + hi * P:o + (hi + 1) * P]

                for i, mh in enumerate(LEVELS):
                    between(i)
                    if i == 0:
                        first()
                    else:
                        pe.wait_ge(sg(pre + "_qk"), 2 * i)
                    for gg in range(2):
                        ps = take((pre, mh, gg))
                        for e, (hd, st) in enumerate(ent[gg]):
                            kk, qq = operands(hd, st, st, i)
                            if mh == P // 2:
                                ins = T.matmul(ps[0:mh, e * P + mh:(e + 1) * P], kk[:, 0:mh], qq[:, mh:P], start=True, stop=True)
                            else:
                                ins = T.matmul(ps[:, e * P:(e + 1) * P], kk, qq, start=True, stop=True)
                        done(ins, (pre, mh, gg))
                pe.wait_ge(sg(pre + "_qk"), 2 * len(LEVELS))
                for gg in range(1 if heads else 2):
                    ps = take((pre, P, gg))
                    hds = range(4) if heads else [2 * b + gg for b in range(2)]
                    for e, hd in enumerate(hds):
                        kk, qq = operands(hd, 0, 1, 1)
                        ins = T.matmul(ps[:, e * P:(e + 1) * P], kk, qq, start=True, stop=True)
                    done(ins, (pre, P, gg))
                for gg in range(2):
                    gone(pe, (pre, P // 2, gg))
                for gg in range(1 if heads else 2):
                    gone(pe, (pre, P, gg))

            pe.wait_ge(sg("const"), 1)
            pe.wait_ge(sg("vec_first"), 16 * N_EARLY)
            done(T.transpose(take(("vec", "early"))[:, 0:V_EARLY], vrow[0:V_EARLY, 0, :], ident[0:V_EARLY, 0:V_EARLY]),
                 ("vec", "early"))
            norm("n0")
            x_done("n0")
            pe.wait_ge(sg("glr_in"), 32)
            ps = take("glr")
            for k in range(KD):
                ins = T.matmul(ps[0:GR, 0:S], wglr[:, k, :], xT[:, k, :], start=(k == 0), stop=(k == KD - 1))
            done(ins, "glr")
            gone(pe, "glr")
            for b in range(2):
                ps = take(("gate", b))
                for j in range(2):
                    hd = 2 * b + j
                    ins = T.matmul(ps[:, j * S:(j + 1) * S], wgu[:, hd * P:(hd + 1) * P], glrT, start=True, stop=True)
                done(ins, ("gate", b))
            x_split()
            for nm in ("q", "k"):
                for b in range(2):
                    fm((nm, b), (nm, b) == ("q", 0))

            def project(i):
                if i == 4:
                    pe.wait_ge(sg("vec_in"), 16 * N_VEC)
                    for k in range(3):
                        n = V_ROWS[k]
                        done(T.transpose(take(("vec", k))[:, 0:n], vrow[0:n, k, :], ident[0:n, 0:n]), ("vec", k))
                nm, c, t = gl_tm[i]
                tm((nm, c), [t])

            def q_and_k():
                for lab in (("q", 0), ("q", 1), ("k", 0), ("k", 1)):
                    gone(pe, lab)

            levels("gl", g, True, project, q_and_k)
            for c in range(2):
                for t in range(TT):
                    gone(pe, ("v", c, t))
            for t, hp in order(True):
                    ps = take(("o", t, hp))
                    for i in range(2):
                        hd = 2 * hp + i
                        cs = slice(hd * GDV, (hd + 1) * GDV)
                        o = ps[:, i * GDV:(i + 1) * GDV]
                        if t:
                            T.matmul(o, g["crs"][:, hd * P:(hd + 1) * P], gv[:, 0, cs], start=True, stop=False)
                        ins = T.matmul(o, g["att"][:, t, hd * P:(hd + 1) * P], gv[:, t, cs], start=(t == 0), stop=True)
                    done(ins, ("o", t, hp))

            def y_in(t, hp):
                gone(pe, ("o", t, hp))

            transposes("y", y_in, order(True)[0:2])
            out_proj("wo", 1, lambda: transposes("y", y_in, order(True)[2:4]))
            norm("n1")
            x_split()

            def ffn(f):
                def down(j):
                    pe.wait_ge(sg("actl_" + f), j + 1)
                    i = pos[f, j, "d"]
                    split_done(pe, i)
                    h_, l_ = of(wh, i, 2), of(wl, i, 2)
                    for t in range(TT):
                        for half in range(2):
                            lab = (f, "acc", t, half)
                            ps = take(lab) if j == 0 else bank[turns[lab][0]]
                            hs = slice(half * 512, (half + 1) * 512)
                            for b in range(2):
                                ts = slice(b * S + t * P, b * S + (t + 1) * P)
                                ins = mm3(ps[:, :], acth[:, j % 2, ts], actl[:, j % 2, ts], h_[:, b, hs], l_[:, b, hs],
                                          j == 0 and b == 0, j == NJ1 - 1 and b == 1)
                            if j == NJ1 - 1:
                                done(ins, lab)
                    if j < NJ1 - 1:
                        ins.then_inc(sg("down_done_" + f), 1)

                for j in range(NJ1):
                    fm((f, j, "g"), j == 0)
                    fm((f, j, "u"))
                    if j:
                        down(j - 1)
                down(NJ1 - 1)

            ffn("f1")
            norm("n2")
            x_first()
            tm(("sv", 0), [0])
            x_rest()
            tm(("sv", 0), [1])
            for b in range(4):
                fm(("sk", b))
            tm(("sv", 1))
            x_split()

            def scores(hd):
                gone(pe, ("sk", hd // 2))
                gone(pe, ("sq", hd // 2))
                ps = take(("z", hd))
                T.matmul(ps[:, 0:S], skT[:, hd, 0:P], sqT[:, hd, :], start=True, stop=True)
                done(T.matmul(ps[:, S:384], skT[:, hd, P:S], sqT[:, hd, P:S], start=True, stop=True), ("z", hd))

            def sums(hd):
                pe.wait_ge(sg("sb_keep"), hd + 1)
                ps = take(("stay", hd))
                T.matmul(ps[:, 0:384], ident[:, :], sU[:, hd, :], start=True, stop=False)
                T.matmul(ps[:, 0:P], nafter[:, :], sT[:, hd, 0:P], start=False, stop=False)
                T.matmul(ps[:, P:S], nafter[:, :], sT[:, hd, P:S], start=False, stop=False)
                T.matmul(ps[:, P:S], nones, sT[:, hd, S:384], start=False, stop=False)
                done(T.matmul(ps[:, S:384], nafter[:, :], sT[:, hd, S:384], start=False, stop=True), ("stay", hd))

            for b in range(4):
                fm(("sq", b), b == 0)
                if b:
                    for hd in (2 * b - 2, 2 * b - 1):
                        scores(hd)
            pe.wait_ge(sg("masks2"), 1)
            sums(0)
            for hd in (SH - 2, SH - 1):
                scores(hd)
            for hd in range(1, SH):
                sums(hd)
            for c in range(2):
                for t in range(TT):
                    gone(pe, ("sv", c, t))
            for hp in range(SH // 2):
                ps = take(("so", hp))
                for i in range(2):
                    hd = 2 * hp + i
                    pe.wait_ge(sg("sb_wm"), hd + 1)
                    vs = slice(hd * P, (hd + 1) * P)
                    T.matmul(ps[:, i * S:i * S + P], sv[:, 0, vs], sU[:, hd, 0:P], start=True, stop=True)
                    T.matmul(ps[:, i * S + P:(i + 1) * S], sv[:, 0, vs], sU[:, hd, P:S], start=True, stop=False)
                    ins = T.matmul(ps[:, i * S + P:(i + 1) * S], sv[:, 1, vs], sU[:, hd, S:384], start=False, stop=True)
                done(ins, ("so", hp))
            out_proj("swo")
            norm("n3")
            pe.wait_ge(sg("rt_in"), 16)
            ps = take("lg")
            for t in range(TT):
                x_done("n3", [t])
                for k in range(KD):
                    ins = T.matmul(ps[:, t * NE:(t + 1) * NE], xT[:, k, t * P:(t + 1) * P], wrt[:, k, :],
                                   start=(k == 0), stop=(k == KD - 1))
            done(ins, "lg")
            pe.wait_ge(sg("rt_sel"), 1)
            ps = take("pos")
            T.matmul(ps[:, 0:NE], before3[:, 0, :], selx[:, 0, :], start=True, stop=True)
            T.matmul(ps[:, NE:2 * NE], before3[:, 1, :], selx[:, 0, :], start=True, stop=False)
            done(T.matmul(ps[:, NE:2 * NE], before3[:, 0, :], selx[:, 1, :], start=False, stop=True), "pos")
            ps = take("cnt")
            T.matmul(ps[:, 0:NE], before3[:, 1, :], selx[:, 0, :], start=True, stop=False)
            done(T.matmul(ps[:, 0:NE], before3[:, 1, :], selx[:, 1, :], start=False, stop=True), "cnt")

            for b in range(8):
                pe.wait_ge(freed[b], uses_before_moe[b])

            def gather(half, b):
                for k in range(4):
                    kk = 4 * half + k
                    for t in range(TT):
                        ins = T.matmul(b[:, k * P:(k + 1) * P], xn[:, t, kk * P:(kk + 1) * P], oh[:, t, :],
                                       start=(t == 0), stop=(t == TT - 1))
                ins.then_inc(sg("moe_xgfull"), 1)

            pe.wait_ge(sg("moe_oh"), 1)
            gather(0, bank[7])
            gather(1, bank[0])

            def used(ins):
                ins.then_inc(sg("moe_used"), 1)

            def experts(at, more_follow):
                def here(c, k):
                    moe_split(pe, at, c)
                    return of(wh, M0 + c, k), of(wl, M0 + c, k)

                for i in range(2):
                    def gate_up(b, kind, j):
                        for half in range(2):
                            h_, l_ = here(UC * i + upos[kind, j, half], 4)
                            for k in range(4):
                                kk = 4 * half + k
                                ins = mm3(b[:, :], xgh[:, kk, :], xgl[:, kk, :], h_[:, k, :], l_[:, k, :], kk == 0, kk == KD - 1)
                            used(ins)

                    def transposed(j):
                        n = NEJ * i + j
                        pe.wait_ge(sg("moe_act"), at(2 * NEJ, n + 3))
                        for k in range(4):
                            ins = T.transpose(bank[4][:, k * P:(k + 1) * P], eact[:, n % 2, k * P:(k + 1) * P], ident[:, :])
                        ins.then_inc(sg("moe_Tfull"), 1)

                    def down(j):
                        n = NEJ * i + j
                        pe.wait_ge(sg("moe_actTl"), at(2 * NEJ, n + 1))
                        for part in range(2):
                            h_, l_ = here(UC * i + upos["d", j, part], 2)
                            for k in range(2):
                                kk = 4 * (n % 2) + 2 * part + k
                                for half in range(2):
                                    hs = slice(half * 512, (half + 1) * 512)
                                    ins = mm3(bank[5 + half][:, :], eactTh[:, kk, :], eactTl[:, kk, :], h_[:, k, hs], l_[:, k, hs],
                                              j == 0 and part == 0 and k == 0, j == NEJ - 1 and part == 1 and k == 1)
                            used(ins)

                    pe.wait_ge(sg("moe_xl"), at(4, 2 * i + 2))
                    for j in range(NEJ):
                        n = NEJ * i + j
                        pe.wait_ge(sg("moe_act"), at(2 * NEJ, n + 1))
                        gate_up(bank[n % 2], "g", j)
                        if j == 1:
                            pe.wait_ge(sg("moe_h"), at(8, 4 * i + 1))
                        if j:
                            transposed(j - 1)
                        gate_up(bank[2 + n % 2], "u", j)
                        if j:
                            down(j - 1)
                        if j == 3:
                            pe.wait_ge(sg("moe_oh"), at(4, 2 * i + 2))
                            for t in range(TT):
                                ins = T.transpose(bank[7][:, t * P:(t + 1) * P], ohg[:, t, :], ident[:, :])
                            ins.then_inc(sg("moe_ohfull"), 1)
                    pe.wait_ge(sg("moe_oh"), at(4, 2 * i + 3))
                    pe.wait_ge(sg("moe_ohT"), at(2, i + 1))
                    gather(0, bank[7])
                    transposed(NEJ - 1)
                    gather(1, bank[(NEJ * (i + 1)) % 2])
                    down(NEJ - 1)
                    pe.wait_ge(sg("moe_y0"), at(2, i + 1))
                    pe.wait_ge(sg("moe_y1"), at(2, i + 1))
                    pe.wait_ge(sg("moe_xg"), at(4, 2 * i + 4))
                    for q in range(4):
                        t, half = q // 2, q % 2
                        if q >= 2:
                            pe.wait_ge(sg("moe_h"), at(8, 4 * i + q))
                        T.matmul(bank[7 if q % 2 == 0 else 4][:, :], ohT[:, t * P:(t + 1) * P],
                                 ey[:, half * 512:(half + 1) * 512], start=True, stop=True).then_inc(sg("moe_scfull"), 1)

            pe.wait_ge(sg("more_ready"), 1)
            more = pairs(pe, experts)
            pe.wait_ge(sg("moe_h"), more * 8 + (8 * NPAIR + 1))
            norm("n4")
            x_first()
            tm(("cig",), [0])
            x_rest()
            tm(("cig",), [1])
            for b in range(2):
                fm(("cqf", b))

            def rows():
                pe.wait_ge(sg("ws_in"), 96)
                for i, nm in enumerate(("cf", "bi", "bf")):
                    ps = take(nm)
                    for k in range(KD):
                        ins = T.matmul(ps[0:72, 0:S], ws[:, k, WS0[i]:WS0[i] + 72], xT[:, k, :], start=(k == 0), stop=(k == KD - 1))
                    done(ins, nm)

            def project(i):
                for nm in hl_pieces.get(i, []):
                    if nm == "rows":
                        rows()
                    elif nm[0] == "av":
                        tm(("av",), [nm[1]])
                    else:
                        fm(nm)

            levels("hl", m, False, project, lambda: pe.wait_ge(sg("hl_A"), 1))
            tm(("bvo",), [0])
            pe.wait_ge(sg("qk_sq"), 1)
            for i in range(4):
                done(T.matmul(take(("qkss", i))[:, :], pair64[:, :], rs[:, i * 512:(i + 1) * 512], start=True, stop=True),
                     ("qkss", i))
            tm(("bvo",), [1])
            pe.wait_ge(sg("ci"), TT)
            for t in range(TT):
                ps = take(("co", t))
                for hd in range(CH):
                    b, hf = hd // 2, hd % 2
                    o = ps[:, hd * HD:(hd + 1) * HD]
                    cs = slice(hd * HD, (hd + 1) * HD)
                    if t:
                        T.matmul(o, m["crs"][:, hf * 256 + b * P:hf * 256 + (b + 1) * P], ci[:, 0, cs], start=True, stop=False)
                    ins = T.matmul(o, m["att"][:, hf, (2 * t + b) * P:(2 * t + b + 1) * P], ci[:, t, cs], start=(t == 0), stop=True)
                done(ins, ("co", t))
            pe.wait_ge(sg("qk_n"), 2)
            pe.wait_ge(sg("c_rows"), 1)
            ao = [take(("ao", t)) for t in range(TT)]

            def fox_scores(hd):
                b, r = hd // 2, slice(64 * (hd % 2), 64 * (hd % 2) + 64)
                ps = take(("s", hd))
                for t in range(TT):
                    o, ks = (ps[:, 0:P], slice(0, P)) if t == 0 else (ps[:, P:3 * P], slice(0, S))
                    T.matmul(o, aq[r, b, t * P:(t + 1) * P], ak[r, b, ks], start=True, stop=False)
                    ins = T.matmul(o, sel[r, hd, :], ncS[r, ks], start=False, stop=True)
                done(ins, ("s", hd))

            def fox_values(hd):
                gone(pe, ("pT", hd))
                cs = slice(hd * HD, (hd + 1) * HD)
                i0 = T.matmul(ao[0][:, cs], pTs[:, hd % 2, 0:P], av[:, 0, cs], start=True, stop=True)
                T.matmul(ao[1][:, cs], pTs[:, hd % 2, P:S], av[:, 0, cs], start=True, stop=False)
                i1 = T.matmul(ao[1][:, cs], pTs[:, hd % 2, S:384], av[:, 1, cs], start=False, stop=True)
                if hd == AH - 1:
                    done(i0, ("ao", 0))
                    done(i1, ("ao", 1))

            def fox_transposes(hd):
                ps = take(("pT", hd))
                pe.wait_ge(sg("s_exp"), TT * (hd + 1))
                for i in range(3):
                    ins = T.transpose(ps[:, i * P:(i + 1) * P], sS[:, hd % 3, i * P:(i + 1) * P], ident[:, :])
                done(ins, ("pT", hd))

            fox_scores(0)
            fox_scores(1)
            for hd in range(AH):
                if hd + 2 < AH:
                    fox_scores(hd + 2)
                fox_transposes(hd)
                if hd:
                    fox_values(hd - 1)
            fox_values(AH - 1)
            pe.wait_ge(sg("m_rows"), 1)
            pe.wait_ge(sg("b_act"), 1)
            ps = take("mT")
            for a, row in enumerate((mS, iF)):
                for t in range(TT):
                    ins = T.transpose(ps[:, (TT * a + t) * P:(TT * a + t + 1) * P], row[:, t * P:(t + 1) * P], ident[:, :])
            done(ins, "mT")
            bo = [take(("bo", t)) for t in range(TT)]

            def lstm_scores(hd):
                b, r = hd // 2, slice(64 * (hd % 2), 64 * (hd % 2) + 64)
                ps = take(("P2", hd))
                ss = ((slice(0, S), slice(0, P)), (slice(P, S), slice(P, S)))
                outs = (slice(0, S), slice(S, 384))
                for st in range(TT):
                    ins = T.matmul(ps[:, outs[st]], sel[r, hd, :], nM[r, ss[st][0]], start=True, stop=True)
                done(ins, ("P2", hd))
                ps = take(("P1", hd))
                for st in range(TT):
                    ins = T.matmul(ps[:, outs[st]], bc[r, 2 + b, ss[st][1]], bc[r, b, ss[st][0]], start=True, stop=True)
                done(ins, ("P1", hd))

            def lstm_values(hd):
                gone(pe, ("P1", hd))
                cs = slice(hd * 65, (hd + 1) * 65)
                w = sS[:, hd % 3, :]
                i0 = T.matmul(bo[0][:, cs], w[:, 0:P], bv[:, 0, hd, :], start=True, stop=True)
                T.matmul(bo[1][:, cs], w[:, P:S], bv[:, 0, hd, :], start=True, stop=False)
                i1 = T.matmul(bo[1][:, cs], w[:, S:384], bv[:, 1, hd, :], start=False, stop=True)
                if hd == BH - 1:
                    done(i0, ("bo", 0))
                    done(i1, ("bo", 1))
                else:
                    i1.then_inc(sg("b_pv"), 1)

            lstm_scores(0)
            lstm_scores(1)
            for hd in range(BH):
                if hd + 2 < BH:
                    lstm_scores(hd + 2)
                lstm_values(hd)
                if hd == BH - 2:
                    transposes("yy", lambda t, half: pe.wait_ge(sg("o_a"), 1), order(True)[0:2])
            out_proj("w2", 2, lambda: transposes("yy", lambda t, half: pe.wait_ge(sg("o_done"), 1), order(True)[2:4]))
            norm("n5")
            x_split()
            ffn("f2")


def kernel(**inputs):
    import numpy as np
    import concourse.bacc as bacc
    from concourse import mybir
    from concourse.bass_utils import run_bass_kernel_spmd

    nc = bacc.Bacc("TRN2", target_bir_lowering=False, num_devices=1)
    arrays, aps = {}, {}
    for name, a in inputs.items():
        a = np.ascontiguousarray(a)
        arrays[f"in_{name}"] = a
        aps[name] = nc.dram_tensor(f"in_{name}", a.shape, mybir.dt.from_np(a.dtype), kind="ExternalInput").ap()
    shape = inputs["x"].shape
    out = nc.dram_tensor("out_0", shape, mybir.dt.float32, kind="ExternalOutput").ap()
    build(nc, aps, out)
    r = run_bass_kernel_spmd(nc, [arrays], core_ids=[0])
    return r.results[0]["out_0"]
```
